# Optimizing a Trainium2 kernel written in Bass

```python
import jax, jax.numpy as jnp
from jax import lax
import numpy as np

D_MODEL = 1024
BATCH = 1
SEQ = 128
DEPTH = 1
DEC_BATCH = 1
DEC_SEQ = 512
PAST_LEN = 128

GRID_W = 64
M_HEADS = 8
M_DK = 64
M_DV = 128
M_WIDTH = M_HEADS * M_DV
CHUNK = 64
A_HEADS = 16
KV_HEADS = 4
GROUP = A_HEADS // KV_HEADS
HEAD_DIM = 64
A_WIDTH = A_HEADS * HEAD_DIM
ROPE_THETA = 10000.0
Q_BLOCK = 128
D_FF = 2816
N_MOD = 9
EPS = 1e-6
MIX_SIZES = (M_HEADS * M_DK, M_HEADS * M_DK, M_WIDTH, M_WIDTH, 4 * M_HEADS,
             A_WIDTH, KV_HEADS * HEAD_DIM, KV_HEADS * HEAD_DIM, 2 * D_MODEL)
D_PROJ = sum(MIX_SIZES)

kernel_name = "hybrid_mlstm_gqa_flow_step"

def rms_norm(x, gain):
    xf = x.astype(jnp.float32)
    y = xf * lax.rsqrt(jnp.mean(xf * xf, axis=-1, keepdims=True) + EPS)
    return (y * gain.astype(jnp.float32)).astype(x.dtype)

def swiglu(h, w_in, w_out):
    a, b = jnp.split(h @ w_in, 2, axis=-1)
    return (jax.nn.silu(a) * b) @ w_out

def axial_rope(x):
    B, T, H, hd = x.shape
    rows = T // GRID_W
    r, c = jnp.meshgrid(jnp.arange(rows), jnp.arange(GRID_W), indexing="ij")
    pos = jnp.stack([r.reshape(-1), c.reshape(-1)], axis=-1).astype(jnp.float32)
    half = hd // 2
    pairs = half // 2
    inv_freq = ROPE_THETA ** (-jnp.arange(pairs, dtype=jnp.float32) / pairs)
    ang = pos[:, :, None] * inv_freq
    cos = jnp.cos(ang)[None, :, None]
    sin = jnp.sin(ang)[None, :, None]
    xf = x.astype(jnp.float32).reshape(B, T, H, 2, half)
    x1, x2 = xf[..., :pairs], xf[..., pairs:]
    out = jnp.concatenate([x1 * cos - x2 * sin, x2 * cos + x1 * sin], axis=-1)
    return out.reshape(B, T, H, hd).astype(x.dtype)

def block_attention(q, k, v):
    B, T, H, hd = q.shape
    nb = T // Q_BLOCK
    qb = jnp.moveaxis(q.reshape(B, nb, Q_BLOCK, KV_HEADS, GROUP, hd), 1, 0)
    scale = hd ** -0.5

    def one_block(qi):
        s = jnp.einsum("bqkgd,bskd->bkgqs", qi, k).astype(jnp.float32) * scale
        p = jax.nn.softmax(s, axis=-1).astype(v.dtype)
        return jnp.einsum("bkgqs,bskd->bqkgd", p, v)

    o = lax.map(one_block, qb)
    return jnp.moveaxis(o, 0, 1).reshape(B, T, H, hd)

def mlstm_scan(q, k, v, log_f, log_i, C0, n0, m0):
    B, H, T, DK = q.shape
    DV = v.shape[-1]
    nc = T // CHUNK

    def to_chunks(a):
        return jnp.moveaxis(a.reshape(B, H, nc, CHUNK, *a.shape[3:]), 2, 0)

    xs = tuple(to_chunks(a) for a in (q, k, v, log_f, log_i))
    lower = jnp.tril(jnp.ones((CHUNK, CHUNK), dtype=bool))

    def step(carry, inp):
        C, n, m = carry
        qc, kc, vc, fc, ic = inp
        b = jnp.cumsum(fc, axis=-1)
        dmat = jnp.where(lower, b[..., :, None] - b[..., None, :] + ic[..., None, :], -jnp.inf)
        inter = b + m[..., None]
        m_t = jnp.maximum(inter, jnp.max(dmat, axis=-1))
        w_inter = jnp.exp(inter - m_t)
        s = jnp.einsum("bhtd,bhsd->bhts", qc, kc) * jnp.exp(dmat - m_t[..., None])
        num = (w_inter[..., None] * jnp.einsum("bhtd,bhde->bhte", qc, C)
               + jnp.einsum("bhts,bhse->bhte", s, vc))
        den = w_inter * jnp.einsum("bhtd,bhd->bht", qc, n) + jnp.sum(s, axis=-1)
        h = num / jnp.maximum(jnp.abs(den), jnp.exp(-m_t))[..., None]
        b_last = b[..., -1]
        g = b_last[..., None] - b + ic
        m_new = jnp.maximum(b_last + m, jnp.max(g, axis=-1))
        a_prev = jnp.exp(b_last + m - m_new)
        kw = kc * jnp.exp(g - m_new[..., None])[..., None]
        C_new = a_prev[..., None, None] * C + jnp.einsum("bhsd,bhse->bhde", kw, vc)
        n_new = a_prev[..., None] * n + jnp.sum(kw, axis=2)
        return (C_new, n_new, m_new), h

    (C, n, m), hs = lax.scan(step, (C0, n0, m0), xs)
    h = jnp.moveaxis(hs, 0, 2).reshape(B, H, T, DV)
    return h, C, n, m

def mlstm_bidir(q, k, v, gates, C0, n0, m0):
    hs, Cs, ns, ms = [], [], [], []
    for d in range(2):
        log_i = jnp.moveaxis(gates[:, :, d, 0], 1, 2)
        log_f = jax.nn.log_sigmoid(jnp.moveaxis(gates[:, :, d, 1], 1, 2))
        seq = (q, k, v, log_f, log_i)
        if d == 1:
            seq = tuple(jnp.flip(a, axis=2) for a in seq)
        h, C, n, m = mlstm_scan(*seq, C0[:, d], n0[:, d], m0[:, d])
        if d == 1:
            h = jnp.flip(h, axis=2)
        hs.append(h); Cs.append(C); ns.append(n); ms.append(m)
    return hs[0] + hs[1], jnp.stack(Cs, 1), jnp.stack(ns, 1), jnp.stack(ms, 1)

def token_mixer(h, w_in, gate_bias, m_norm, qk_norm, w_bm, w_ba, w_out, ctx):
    B, T, _ = h.shape
    f32 = jnp.float32
    idx = np.cumsum(MIX_SIZES)[:-1].tolist()
    mq, mk, mv, mo, mg, aq, ak, av, bg = jnp.split(h @ w_in, idx, axis=-1)
    mq = jnp.transpose(mq.reshape(B, T, M_HEADS, M_DK), (0, 2, 1, 3)).astype(f32) * (M_DK ** -0.5)
    mk = jnp.transpose(mk.reshape(B, T, M_HEADS, M_DK), (0, 2, 1, 3)).astype(f32)
    mv = jnp.transpose(mv.reshape(B, T, M_HEADS, M_DV), (0, 2, 1, 3)).astype(f32)
    mg = mg.reshape(B, T, 2, 2, M_HEADS).astype(f32) + gate_bias.astype(f32)
    if ctx is None:
        C0 = jnp.zeros((B, 2, M_HEADS, M_DK, M_DV), f32)
        n0 = jnp.zeros((B, 2, M_HEADS, M_DK), f32)
        m0 = jnp.zeros((B, 2, M_HEADS), f32)
    else:
        C0, n0, m0 = (a.astype(f32) for a in ctx[2:])
    hm, C, n, m = mlstm_bidir(mq, mk, mv, mg, C0, n0, m0)
    hm = rms_norm(jnp.transpose(hm, (0, 2, 1, 3)), m_norm.reshape(M_HEADS, M_DV))
    hm = (hm * jax.nn.sigmoid(mo.reshape(B, T, M_HEADS, M_DV).astype(f32))).reshape(B, T, M_WIDTH)
    aq = rms_norm(aq.reshape(B, T, A_HEADS, HEAD_DIM), qk_norm[0])
    ak = rms_norm(ak.reshape(B, T, KV_HEADS, HEAD_DIM), qk_norm[1])
    av = av.reshape(B, T, KV_HEADS, HEAD_DIM)
    if ctx is None:
        k_all, v_all = ak, av
    else:
        aq = axial_rope(aq)
        k_all = jnp.concatenate([axial_rope(ak), ctx[0].astype(ak.dtype)], axis=1)
        v_all = jnp.concatenate([av, ctx[1].astype(av.dtype)], axis=1)
    ha = block_attention(aq, k_all, v_all).reshape(B, T, A_WIDTH)
    g = jax.nn.sigmoid(bg.reshape(B, T, 2, D_MODEL))
    y = g[:, :, 0] * (hm.astype(h.dtype) @ w_bm) + g[:, :, 1] * (ha @ w_ba)
    return y @ w_out, (ak, av, C, n, m)

def trunk_layer(x, mod, n_pre, n_post, f_in, f_out, mix_w, ctx):
    sh0, sc0, g0, sh1, sc1, g1, sh2, sc2, g2 = jnp.split(mod, N_MOD, axis=-1)
    h = rms_norm(x, n_pre[0]) * (1 + sc0) + sh0
    x = x + 0.5 * g0 * rms_norm(swiglu(h, f_in[0], f_out[0]), n_post[0])
    h = rms_norm(x, n_pre[1]) * (1 + sc1) + sh1
    y, st = token_mixer(h, *mix_w, ctx)
    x = x + g1 * rms_norm(y, n_post[1])
    h = rms_norm(x, n_pre[2]) * (1 + sc2) + sh2
    x = x + 0.5 * g2 * rms_norm(swiglu(h, f_in[1], f_out[1]), n_post[2])
    return x, st

def setup_inputs(seed: int = 0) -> dict:
    key = jax.random.key(seed)
    ks = jax.random.split(key, 24)
    nrm = jax.random.normal
    f_bias_base = jnp.stack([jnp.zeros((M_HEADS,)), jnp.linspace(3.0, 6.0, M_HEADS)])
    return {
        "x_prompt": nrm(ks[0], (BATCH, SEQ, D_MODEL), jnp.float32),
        "x_sample": nrm(ks[1], (DEC_BATCH, DEC_SEQ, D_MODEL), jnp.float32),
        "c": nrm(ks[2], (DEC_BATCH, D_MODEL), jnp.float32),
        "cache_k": nrm(ks[3], (DEC_BATCH, DEPTH, PAST_LEN, KV_HEADS, HEAD_DIM), jnp.float32),
        "cache_v": nrm(ks[4], (DEC_BATCH, DEPTH, PAST_LEN, KV_HEADS, HEAD_DIM), jnp.float32),
        "state_C": 0.5 * nrm(ks[5], (DEC_BATCH, DEPTH, 2, M_HEADS, M_DK, M_DV), jnp.float32),
        "state_n": 0.5 * nrm(ks[6], (DEC_BATCH, DEPTH, 2, M_HEADS, M_DK), jnp.float32),
        "state_m": 0.5 * nrm(ks[7], (DEC_BATCH, DEPTH, 2, M_HEADS), jnp.float32),
        "c_ctx": nrm(ks[8], (D_MODEL,), jnp.float32),
        "w_mod": 0.5 * D_MODEL ** -0.5 * nrm(ks[9], (DEPTH, D_MODEL, N_MOD * D_MODEL), jnp.float32),
        "b_mod": 0.02 * nrm(ks[10], (DEPTH, N_MOD * D_MODEL), jnp.float32),
        "norm_pre": 1.0 + 0.05 * nrm(ks[11], (DEPTH, 3, D_MODEL), jnp.float32),
        "norm_post": 1.0 + 0.05 * nrm(ks[12], (DEPTH, 3, D_MODEL), jnp.float32),
        "ffn_w_in": D_MODEL ** -0.5 * nrm(ks[13], (DEPTH, 2, D_MODEL, 2 * D_FF), jnp.float32),
        "ffn_w_out": D_FF ** -0.5 * nrm(ks[14], (DEPTH, 2, D_FF, D_MODEL), jnp.float32),
        "w_in_mix": D_MODEL ** -0.5 * nrm(ks[15], (DEPTH, D_MODEL, D_PROJ), jnp.float32),
        "mlstm_gate_bias": f_bias_base + 0.1 * nrm(ks[16], (DEPTH, 2, 2, M_HEADS), jnp.float32),
        "mlstm_norm": 1.0 + 0.05 * nrm(ks[17], (DEPTH, M_WIDTH), jnp.float32),
        "qk_norm": 1.0 + 0.05 * nrm(ks[18], (DEPTH, 2, HEAD_DIM), jnp.float32),
        "w_branch_m": M_WIDTH ** -0.5 * nrm(ks[19], (DEPTH, M_WIDTH, D_MODEL), jnp.float32),
        "w_branch_a": A_WIDTH ** -0.5 * nrm(ks[20], (DEPTH, A_WIDTH, D_MODEL), jnp.float32),
        "w_out": D_MODEL ** -0.5 * nrm(ks[21], (DEPTH, D_MODEL, D_MODEL), jnp.float32),
    }

def reference(x_prompt, x_sample, c, cache_k, cache_v, state_C, state_n, state_m, c_ctx,
              w_mod, b_mod, norm_pre, norm_post, ffn_w_in, ffn_w_out, w_in_mix,
              mlstm_gate_bias, mlstm_norm, qk_norm, w_branch_m, w_branch_a, w_out):
    y_prompt = x_prompt
    y_sample = x_sample
    ks_, vs_, Cs_, ns_, ms_ = [], [], [], [], []
    for l in range(DEPTH):
        mix_w = (w_in_mix[l], mlstm_gate_bias[l], mlstm_norm[l], qk_norm[l],
                 w_branch_m[l], w_branch_a[l], w_out[l])
        mod_ctx = (jax.nn.silu(c_ctx) @ w_mod[l] + b_mod[l])[None, None, :]
        mod_lat = (jax.nn.silu(c) @ w_mod[l] + b_mod[l])[:, None, :]
        y_prompt, (k_new, v_new, C_new, n_new, m_new) = trunk_layer(
            y_prompt, mod_ctx, norm_pre[l], norm_post[l], ffn_w_in[l], ffn_w_out[l], mix_w, None)
        ks_.append(k_new); vs_.append(v_new)
        Cs_.append(C_new); ns_.append(n_new); ms_.append(m_new)
        ctx = (cache_k[:, l], cache_v[:, l], state_C[:, l], state_n[:, l], state_m[:, l])
        y_sample, _ = trunk_layer(
            y_sample, mod_lat, norm_pre[l], norm_post[l], ffn_w_in[l], ffn_w_out[l], mix_w, ctx)
    dt = x_prompt.dtype
    new_cache_k = jnp.stack(ks_, axis=1)
    new_cache_v = jnp.stack(vs_, axis=1)
    new_state_C = jnp.stack(Cs_, axis=1).astype(dt)
    new_state_n = jnp.stack(ns_, axis=1).astype(dt)
    new_state_m = jnp.stack(ms_, axis=1).astype(dt)
    return (y_prompt, y_sample, new_cache_k, new_cache_v, new_state_C, new_state_n, new_state_m)


_drawn_inputs = setup_inputs


def setup_inputs(seed=0):
    import zlib

    import numpy as np

    out = dict(_drawn_inputs(seed))
    spreads = {}
    factors = {'cache_k': 4.358,
     'cache_v': 3.71,
     'state_C': 4.986,
     'state_n': 8.0,
     'state_m': 8.0,
     'norm_post': 2.973,
     'mlstm_norm': 4.148}
    for name, (base, spread) in spreads.items():
        noise = np.random.default_rng([zlib.crc32(name.encode()), seed]).standard_normal(out[name].shape)
        drawn = base * np.exp(spread * noise) if base else spread * noise
        out[name] = __import__('jax').numpy.asarray(drawn.astype(out[name].dtype))
    for name, factor in factors.items():
        out[name] = (out[name] * factor).astype(out[name].dtype)
    return out
```

```python
from contextlib import ExitStack

import numpy as np

import concourse.bass as bass
from concourse import mybir

F32 = mybir.dt.float32
F32R = mybir.dt.float32r
ALU = mybir.AluOpType
ACT = mybir.ActivationFunctionType
AX = mybir.AxisListType

P = 128
D = 1024
KC = D // P
TP, TS = 128, 512
N = TP + TS
NT = N // P
HALF = N // 2
DFF = 2816
NJ = DFF // P
PHASES = (8, 8, 6)
PAST = 128
H, DK, DV = 8, 64, 128
AH, KVH, HD = 16, 4, 64
GRID_W = 64
EPS = 1e-6
NMOD = 9
RAWS = 4
GROUPS = ((0, slice(0, TP)), (1, slice(TP, N)))

L_GATE, L_MQ, L_MK, L_MV, L_AQ, L_AK, L_AV, L_MO, L_BM, L_BA, L_OUT, L_END = np.cumsum(
    [0, 1, 4, 4, 8, 8, 4, 2, 8, 16, 16, 8]).tolist()
FFN_TILES = 2 * NJ + KC * len(PHASES)
T_MIX = FFN_TILES
T_FFN1 = T_MIX + L_END
T_END = T_FFN1 + FFN_TILES
ROW_M, ROW_END = 2 + 2 * NT + 4 + 7, 2 + 2 * NT + 4 + 7 + 4 + 3
UNITS = NT * 4
HEADS = NT * AH
STATES = ((0, 0), (1, 0), (0, 1), (1, 4), (0, 2), (1, 3), (0, 3), (1, 2))
C_N = 6 * P + 2 * TS
R_N = H * P + 4 * P + P

V_PRE, V_POST, V_MN, V_CC, V_QG, V_KG, V_N = 72, 96, 120, 128, 144, 145, 146


class Tile:

    def __init__(self, c, i=0):
        self.c, self.i = c, i
        self.raw, self.slot = c % RAWS, c % 2
        self.n = 4 * i + c
        self.quad = i + c // 4
        self.pair = 2 * i + c // 2

    def plus(self, k):
        return Tile(self.c + k, self.i)


def build(nc, a):
    ctx = ExitStack()
    with ctx:
        def sem(name):
            return ctx.enter_context(nc.semaphore(name))

        def at(name, shape, dt, offset):
            return nc.alloc_sbuf_tensor_at(name, shape, dt, offset=offset)

        row = N * 4
        cur = [-(-nc.sbuf_base // 64) * 64]

        def place(name, shape, dt=F32):
            t = at(name, shape, dt, cur[0])
            cur[0] += -(-int(np.prod(shape[1:])) * 4 // 32) * 32
            return t

        cst = place("cst", [P, C_N])
        rowc = place("rowc", [H, R_N])
        vT = place("vT", [P, V_N])
        silc = place("silc", [P, 2, KC])
        mod = place("mod", [P, NMOD * KC, 2])
        pre_s = place("pre_s", [P, 3, KC, 2])
        post_s = place("post_s", [P, 3, KC, 2])
        gbias = place("gbias", [H, 4])
        m0 = place("m0", [H, 2])
        epsc = place("epsc", [P, 2])
        x_at = cur[0]
        x = place("x", [P, KC, N])
        h_at = cur[0]
        h_hi = place("h_hi", [P, KC, N], F32R)
        h_lo = place("h_lo", [P, KC, N], F32R)
        raw = [place(f"raw{s}", [P, KC, P]) for s in range(RAWS)]
        whi = [place(f"whi{s}", [P, KC, P], F32R) for s in range(2)]
        wlo = [place(f"wlo{s}", [P, KC, P], F32R) for s in range(2)]
        sa = [place(f"sa{s}", [P, N]) for s in range(2)]
        sb_at = cur[0]
        sb = [place(f"sb{s}", [P, N]) for s in range(2)]
        sq_at = cur[0]
        sq = [place(f"sq{s}", [P, N]) for s in range(2)]
        rb = place("rb", [P, N])
        r1 = cur[0]
        r2 = r1 + KC * row
        r3 = r2 + KC * row
        y = at("y", [P, KC, N], F32, r1)
        g_hi = at("g_hi", [P, PHASES[0], N], F32R, r2)
        g_lo = at("g_lo", [P, PHASES[0], N], F32R, r2 + KC * row)
        mw_at = r2 + 2 * KC * row
        mw = [at(f"mw{s}", [P, KC, P], F32, mw_at + s * KC * P * 4) for s in range(4)]
        xtok = at("xtok", [P, NT, D], F32, h_at)
        vrow = at("vrow", [P, P], F32, r2)
        vrow2 = at("vrow2", [V_N - P, P], F32, r2 + 512)
        otok = [at(f"otok{s}", [P, D], F32, r2 + s * D * 4) for s in range(2)]
        mkt = at("mkt", [P, NT, H * DK], F32, x_at)
        nm = at("nm", [H, 2, N], F32, x_at + 10240)
        t1 = at("t1", [H, 2, N], F32, x_at + 15360)
        gi = at("gi", [H, 2, N], F32, r1)
        gf = at("gf", [H, 2, N], F32, r1 + 5120)
        gb = at("gb", [H, 2, N], F32, r1 + 10240)
        gm = at("gm", [H, 2, N], F32, r1 + 15360)
        hm = at("hm", [P, H, N], F32, r1)
        mq = at("mq", [P, 4, N], F32, r2)
        mk = at("mk", [P, 4, N], F32, r2 + 4 * row)
        cur[0] = r3
        vt = place("vt", [P, NT, H, DV + 1])
        cs = place("cs", [P, 2, NT - 1, 4, DV + 1])
        tk = place("tk", [P, 3, NT, 2, H])
        ab = place("ab", [P, 4, 2 * NT])
        m_in = place("m_in", [H, 2, NT])
        nml = place("nml", [H, 2, NT])
        ar = place("ar", [H, 2, NT])
        mout = place("mout", [H, 2])
        den = place("den", [P, 2, 2])
        ss = place("ss", [P, 2, 2])
        cp = place("cp", [P, 2, 4, DV + 1])
        end_m = cur[0]
        qw = at("qw", [P, 2, 2, P], F32, sq_at)
        hmt = at("hmt", [P, 2, 2, P], F32, sb_at + 2560)
        ha = at("ha", [P, KC, N], F32, r2)
        cur[0] = r3
        aq = place("aq", [P, KC, N])
        ak = place("ak", [P, KVH, N])
        akc = place("akc", [P, KVH, PAST])
        av = place("av", [P, NT + 1, KVH * HD])
        amax = place("amax", [P, 2])
        asum = place("asum", [P, 2])
        arec = place("arec", [P, 2])
        end_a = cur[0]
        ck2 = at("ck2", [P, KVH, 2, HD], F32, x_at)
        ko = at("ko", [P, KVH * HD], F32, x_at + 2048)
        os_ = at("os", [P, 2, P], F32, sq_at)
        m_hi = at("m_hi", [P, KC, N], F32R, r3)
        m_lo = at("m_lo", [P, KC, N], F32R, r3 + KC * row)
        assert max(end_m, end_a, r3 + 2 * KC * row, mw_at + 4 * KC * P * 4) <= nc.sbuf_usable_end

        ident, ones_d, ones_h, swap = (cst[:, n * P:(n + 1) * P] for n in range(4))
        mask = [cst[:, (4 + d) * P:(5 + d) * P] for d in range(2)]
        cos, sin = cst[:, 6 * P:6 * P + TS], cst[:, 6 * P + TS:6 * P + 2 * TS]
        sel1 = rowc[:, 0:H * P].rearrange("h (g p) -> h g p", g=H)
        sel2 = rowc[:, H * P:H * P + 4 * P].rearrange("h (j p) -> h j p", j=4)
        one_row = rowc[:, H * P + 4 * P:R_N]

        psum = ctx.enter_context(nc.psum_tensor("psum", [P, 8, 512], F32))

        def half_out(slot, h):
            return psum[:, 2 * slot + h, 0:HALF]

        def both(slot):
            return psum[:, 2 * slot:2 * slot + 2, 0:HALF]

        def flat(slot):
            return psum[:, 2 * slot:2 * slot + 2, :].rearrange("p b n -> p (b n)")

        def halves(t):
            return t.rearrange("p (h n) -> p h n", h=2)

        modp = psum[:, 7, 0:2 * NMOD * KC]

        ld_small, ld_row, ld_x = sem("ld_small"), sem("ld_row"), [sem(f"ld_x{c}") for c in range(NT)]
        raw_in = [sem(f"raw_in{s}") for s in range(RAWS)]
        raw_free = sem("raw_free")
        w_hi = sem("w_hi")
        tile_done = sem("tile_done")
        ev = [sem("ev0"), sem("ev1")]
        mod_in = [sem(f"mod_in{s}") for s in range(4)]
        mod_done, mod_ready = sem("mod_done"), sem("mod_ready")
        vec_t, v_ready, silc_ready = sem("vec_t"), sem("v_ready"), sem("silc_ready")
        x_t, x_ev = sem("x_t"), [sem("x_ev0"), sem("x_ev1")]
        sq_in, stat_mm = sem("sq_in"), sem("stat_mm")
        rb_sqrt, rb_ready = sem("rb_sqrt"), sem("rb_ready")
        pre_t, pre_h, pre_hi, h_rdy = sem("pre_t"), sem("pre_h"), sem("pre_hi"), sem("h_rdy")
        post_t, x_upd = sem("post_t"), sem("x_upd")
        g_hi_s, g_lo_s = sem("g_hi_s"), sem("g_lo_s")
        x_spill, x_back = sem("x_spill"), sem("x_back")
        tr_done, tr_ev = sem("tr_done"), sem("tr_ev")
        row_d, row_a, tok_t, tok_ev = sem("row_d"), sem("row_a"), sem("tok_t"), sem("tok_ev")
        st_in, kw_in, kv_done, st_upd = sem("st_in"), sem("kw_in"), sem("kv_done"), sem("st_upd")
        front, e_min, e_exp, qw_in, s_in = (sem(n) for n in ("front", "e_min", "e_exp", "qw_in", "s_in"))
        nums, den_s, hm_in, ss_in, hm_sc, hm_t, hm_ev = (
            sem(n) for n in ("nums", "den_s", "hm_in", "ss_in", "hm_sc", "hm_t", "hm_ev"))
        ones_v, eps_in, dv = sem("ones_v"), sem("eps_in"), sem("dv")
        qk_st, qk_rb, qk_rs = sem("qk_st"), sem("qk_rb"), sem("qk_rs")
        rope, rope_out, rope_c, y_sum = sem("rope"), sem("rope_out"), sem("rope_c"), sem("y_sum")
        ck_in, ck_t, ck_ev = sem("ck_in"), sem("ck_t"), sem("ck_ev")
        sc, nmx, aexp, atr, pta, ptb, pv, oev, pt_o, ha_ev, rcp = (sem(n) for n in (
            "sc", "nmx", "aexp", "atr", "pta", "ptb", "pv", "oev", "pt_o", "ha_ev", "rcp"))
        sig, mg, mg_hi, mg_lo = sem("sig"), sem("mg"), sem("mg_hi"), sem("mg_lo")
        hah, hal, yh, yl = sem("hah"), sem("hal"), sem("yh"), sem("yl")
        ot, oe, out_st, misc_st = sem("ot"), sem("oe"), sem("out_st"), sem("misc_st")

        block = ctx.enter_context(nc.Block())

        @block.sync
        def _(sp):
            def load(t, src, nk=KC):
                sp.wait_ge(raw_free, t.n + 1)
                sp.dma_start(raw[t.raw][:, 0:nk, :].rearrange("p k c -> p (k c)"), src).then_inc(raw_in[t.raw], 16)

            def load_mod(t):
                if t.c >= 4:
                    sp.wait_ge(mod_done, t.n - 3)
                sp.dma_start(mw[t.raw][:, :, :].rearrange("p k c -> p (k c)"), pick(a["w_mod"], t.n)).then_inc(mod_in[t.raw], 16)

            def pick(tiles, n):
                if isinstance(n, int):
                    return tiles[n]
                return tiles[bass.ds(n, 1)].rearrange("o p c -> p (o c)")

            sp.dma_start(vrow[:, :], a["vec_rows"][0:P]).then_inc(ld_small, 16)
            sp.dma_start(vrow2[:, :], a["vec_rows"][P:V_N]).then_inc(ld_small, 16)
            sp.dma_start(cst[:, :], a["cst"]).then_inc(ld_small, 16)
            for t in range(4):
                load_mod(Tile(t))
            for c in range(NT):
                src = a["x_prompt"][0] if c == 0 else a["x_sample"][0, (c - 1) * P:c * P]
                sp.dma_start(xtok[:, c, :], src).then_inc(ld_x[c], 16)
            for t in range(4, 16):
                load_mod(Tile(t))
            for src, dst in ((a["rowc"], rowc[:, :]), (a["gate_bias"], gbias[:, :]), (a["m0"], m0[:, :])):
                sp.dma_start(dst, src).then_inc(ld_row, 16)

            def ffn(f, base):
                it = 0
                j0 = 0
                for p, nj in enumerate(PHASES):
                    with sp.Fori(0, nj // 2) as i:
                        for u in range(4):
                            load(Tile(base + u, i), pick(a["w_ffn_in"], f * 2 * NJ + 2 * j0 + 4 * i + u))
                        if f == 0 and p < 2:
                            for u in range(4):
                                load_mod(Tile(16 + 4 * it + u, i))
                    it += nj // 2
                    base += 2 * nj
                    if f == 0 and p == 2:
                        for u in range(8):
                            load_mod(Tile(16 + 48 + u))
                    with sp.Fori(0, 2) as i:
                        for u in range(4):
                            src = a["w_ffn_out"][:, :, j0 * P:(j0 + nj) * P]
                            load(Tile(base + u, i), pick(src, f * KC + 4 * i + u), nj)
                        if f == 0 and p < 2:
                            for u in range(4):
                                load_mod(Tile(16 + 4 * it + u, i))
                    it += 2
                    base += KC
                    j0 += nj

            ffn(0, 0)

            def mix(lo, hi):
                for l in range(lo, hi):
                    load(Tile(T_MIX + l), a["w_mix"][l])

            mix(L_GATE, RAWS)
            sp.wait_ge(x_upd, KC)
            sp.dma_start(a["x_keep"], x[:, :, :].rearrange("p k n -> p (k n)")).then_inc(x_spill, 16)
            for d in range(2):
                c = (0, NT - 2)[d]
                sp.dma_start(cs[:, d, c, :, 0:DV],
                             a["state_C"][0, 0, d].rearrange("(j g) k v -> (g k) j v", g=2)).then_inc(st_in, 16)
                sp.dma_start(cs[:, d, c, :, DV:DV + 1],
                             a["state_n"][0, 0, d].rearrange("(j g) (k o) -> (g k) j o", g=2, o=1),
                             allow_slow_non_contiguous=True).then_inc(st_in, 16)
            mix(RAWS, L_AQ + 2)
            sp.wait_ge(row_d, ROW_M)
            sp.dma_start(a["o_m"].rearrange("a b d h -> h (a b d)"), mout[:, :],
                         allow_slow_non_contiguous=True).then_inc(misc_st, 16)
            sp.wait_ge(st_upd, 2)
            for d in range(2):
                sp.dma_start(a["o_C"][0, 0, d].rearrange("(j g) k v -> (g k) j v", g=2),
                             cp[:, d, :, 0:DV]).then_inc(misc_st, 16)
                sp.dma_start(a["o_n"][0, 0, d].rearrange("(j g) (k o) -> (g k) j o", g=2, o=1),
                             cp[:, d, :, DV:DV + 1], allow_slow_non_contiguous=True).then_inc(misc_st, 16)
            sp.wait_ge(hm_ev, UNITS)
            sp.wait_ge(misc_st, 16 * 5)
            for r in range(2):
                sp.dma_start(ck2[:, :, r, :], a["cache_k"].rearrange("s (g d) -> s g d", g=KVH)).then_inc(ck_in, 16)
            sp.dma_start(av[:, NT, :], a["cache_v"]).then_inc(ck_in, 16)
            mix(L_AQ + 2, L_MO + 2)
            sp.wait_ge(ck_ev, 2)
            sp.dma_start(a["o_k"], ko[:, :]).then_inc(misc_st, 16)
            sp.wait_ge(tr_ev, 14)
            sp.dma_start(a["o_v"], av[:, 0, :]).then_inc(misc_st, 16)
            sp.wait_ge(misc_st, 16 * 7)
            sp.wait_ge(x_spill, 16)
            sp.dma_start(x[:, :, :].rearrange("p k n -> p (k n)"), a["x_keep"]).then_inc(x_back, 16)
            mix(L_MO + 2, L_END)
            ffn(1, T_FFN1)
            for c in range(NT):
                sp.wait_ge(oe, c + 1)
                dst = a["o_yp"][0] if c == 0 else a["o_ys"][0, (c - 1) * P:c * P]
                sp.dma_start(dst, otok[c % 2][:, :]).then_inc(out_st, 16)
                if c < NT - 1:
                    sp.wait_ge(out_st, 16 * (c + 1))
            sp.wait_ge(out_st, 16 * NT)

        @block.tensor
        def _(pe):
            mm, tp = pe.matmul, pe.transpose

            def project(t, nk, hi, lo, ready=None, first=0):
                pe.wait_ge(raw_free, t.n + 1 + RAWS)
                pe.wait_ge(ev[t.slot], t.pair)
                for k in range(nk):
                    if ready is not None:
                        pe.wait_ge(ready, first + k + 1)
                    for h in range(2):
                        cols = slice(h * HALF, (h + 1) * HALF)
                        out = half_out(t.slot, h)
                        mm(out, whi[t.slot][:, k, :], hi[:, k, cols], start=(k == 0), stop=False)
                        mm(out, whi[t.slot][:, k, :], lo[:, k, cols], start=False, stop=False)
                        last = mm(out, wlo[t.slot][:, k, :], hi[:, k, cols], start=False, stop=(k == nk - 1))
                last.then_inc(tile_done, 1)

            def modulate(t):
                pe.wait_ge(mod_in[t.raw], 16 * (t.quad + 1))
                out = modp[:, 2 * t.c:2 * t.c + 2] if isinstance(t.n, int) else modp[:, bass.ds(2 * t.n, 2)]
                for k in range(KC):
                    last = mm(out, mw[t.raw][:, k, :], silc[:, :, k], start=(k == 0), stop=(k == KC - 1))
                last.then_inc(mod_done, 1)

            def stats(n, group=None):
                for k in range(KC):
                    pe.wait_ge(sq_in, 8 * n + k + 1)
                    for h in range(2):
                        last = mm(half_out(2, h), ones_d, sq[k % 2][:, h * HALF:(h + 1) * HALF],
                                  start=(k == 0), stop=(k == KC - 1))
                    last.then_inc(stat_mm, 1)

            pe.sem_inc(tile_done, 2)
            pe.wait_ge(ld_small, 48)
            tp(psum[:, 6, 0:P], vrow[:, :], ident)
            tp(psum[:, 6, P:V_N], vrow2[:, :], ident[0:V_N - P, 0:V_N - P]).then_inc(vec_t, 1)
            for c in range(NT):
                pe.wait_ge(ld_x[c], 16)
            for k in range(KC):
                if k >= 2:
                    pe.wait_ge(x_ev[k % 2], k // 2)
                for c in range(NT):
                    last = tp(flat(k % 2)[:, c * P:(c + 1) * P], xtok[:, c, k * P:(k + 1) * P], ident)
                last.then_inc(x_t, 1)
            pe.wait_ge(silc_ready, 1)
            for t in range(16):
                modulate(Tile(t))

            def ffn(f, base):
                it, j0 = 0, 0
                for p, nj in enumerate(PHASES):
                    with pe.Fori(0, nj // 2) as i:
                        for u in range(4):
                            project(Tile(base + u, i), KC, h_hi, h_lo, h_rdy if u == 0 else None, 16 * f)
                        if f == 0 and p < 2:
                            for u in range(4):
                                modulate(Tile(16 + 4 * it + u, i))
                    it += nj // 2
                    base += 2 * nj
                    if f == 0 and p == 2:
                        for u in range(8):
                            modulate(Tile(16 + 48 + u))
                    with pe.Fori(0, 2) as i:
                        for u in range(4):
                            project(Tile(base + u, i), nj, g_hi, g_lo, g_lo_s if u == 0 else None, NJ * f + j0)
                        if f == 0 and p < 2:
                            for u in range(4):
                                modulate(Tile(16 + 4 * it + u, i))
                    it += 2
                    base += KC
                    j0 += nj

            stats(0)
            ffn(0, 0)
            stats(1)
            stats(2)

            def gemm(l, hi=h_hi, lo=h_lo, ready=None, first=0):
                project(Tile(T_MIX + l), KC, hi, lo, ready, first)

            def turn(jb):
                l = L_MK + jb if jb < 12 else L_AV + jb - 12
                t = Tile(T_MIX + l)
                pe.wait_ge(ev[t.slot], t.pair + 1)
                if jb >= 2:
                    pe.wait_ge(tr_ev, jb - 1)
                src = mk[:, jb, :] if jb < 4 else sa[jb % 2][:, :]
                for c in range(NT):
                    last = tp(flat(2 + jb % 2)[:, c * P:(c + 1) * P], src[:, c * P:(c + 1) * P], ident)
                last.then_inc(tr_done, 1)

            gemm(0, ready=h_rdy, first=8)
            for l in range(1, L_AQ):
                gemm(l)
                if l > L_MK:
                    turn(l - L_MK - 1)
            turn(11)

            pe.wait_ge(row_a, 6)
            pe.wait_ge(row_d, ROW_END)
            pe.wait_ge(tr_ev, 12)
            for q, src in enumerate((gi, gf, gm)):
                for c in range(NT):
                    for d in range(2):
                        o = ((q * NT + c) * 2 + d) * H
                        last = tp(psum[:, 4, o:o + H], src[:, d, c * P:(c + 1) * P], ident[0:H, 0:H])
            last.then_inc(tok_t, 1)
            for j in range(4):
                last = mm(psum[:, 5, j * 2 * NT:(j + 1) * 2 * NT], sel2[:, j, :],
                          ar[:, :, :].rearrange("h d c -> h (d c)"), start=True, stop=True)
            last.then_inc(tok_t, 1)

            for s, (d, c) in enumerate(STATES):
                pe.wait_ge(kw_in, s + 1)
                pe.wait_ge(ones_v, 1)
                if s >= 2:
                    pe.wait_ge(st_upd, s - 1)
                for g in range(H):
                    j, hh = g // 2, g % 2
                    last = mm(psum[hh * DK:(hh + 1) * DK, 2 * (s % 2) + j // 2, (j % 2) * (DV + 1):(j % 2 + 1) * (DV + 1)],
                              sa[s % 2][:, g * DK:(g + 1) * DK], vt[:, c, g, :], start=True, stop=True)
                last.then_inc(kv_done, 1)

            def front_of(n):
                c, j = n // 4, n % 4
                tok = slice(c * P, (c + 1) * P)
                if n == 0:
                    pe.wait_ge(tok_ev, 2)
                else:
                    pe.wait_ge(s_in, n)
                bc = psum[:, 4, :].rearrange("p (d g t) -> p d g t", d=2, g=2)
                for hh in range(2):
                    mm(bc[:, :, hh, :], sel1[:, 2 * j + hh, :], nm[:, :, tok], start=True, stop=True)
                if c > 0:
                    mm(psum[:, 5, P:3 * P].rearrange("p (d t) -> p d t", d=2), sel2[:, j, :], t1[:, :, tok],
                       start=True, stop=True)
                for hh in range(2):
                    half = slice(hh * DK, (hh + 1) * DK)
                    last = mm(psum[:, 5 + hh, 0:P], mk[half, j, tok], mq[half, j, tok], start=True, stop=True)
                last.then_inc(front, 1)

            def nums_of(n):
                c, j = n // 4, n % 4
                pe.wait_ge(s_in, n + 1)
                if n >= 2:
                    pe.wait_ge(hm_in, n - 1)
                else:
                    pe.wait_ge(st_upd, len(STATES))
                for hh in range(2):
                    half = slice(hh * DK, (hh + 1) * DK)
                    for d in range(2):
                        out = psum[:, 2 * (n % 2) + hh, d * (DV + 1):(d + 1) * (DV + 1)]
                        last = mm(out, sa[n % 2][:, (2 * d + hh) * P:(2 * d + hh + 1) * P], vt[:, c, 2 * j + hh, :],
                                  start=True, stop=(c == 0))
                        if c > 0:
                            last = mm(out, qw[half, n % 2, d, :], cs[half, d, c - 1, j, :], start=False, stop=True)
                last.then_inc(nums, 1)

            def turn_hm(n):
                pe.wait_ge(hm_sc, n + 1)
                if n >= 1:
                    pe.wait_ge(hm_ev, n)
                for hh in range(2):
                    last = tp(psum[:, 7, hh * P:(hh + 1) * P], hmt[:, n % 2, hh, :], ident)
                last.then_inc(hm_t, 1)

            front_of(0)
            for n in range(UNITS):
                if n + 1 < UNITS:
                    front_of(n + 1)
                nums_of(n)
                if n >= 2:
                    turn_hm(n - 2)
            turn_hm(UNITS - 2)
            turn_hm(UNITS - 1)

            def qk_stats(e):
                t = Tile(T_MIX + L_AQ + e)
                dst = aq[:, e, :] if e < KC else ak[:, e - KC, :]
                pe.wait_ge(ev[t.slot], t.pair + 1)
                if e >= 1:
                    pe.wait_ge(qk_rb, e)
                    pe.wait_ge(rope, e)
                for h in range(2):
                    mm(half_out(2, h), ones_h, sq[e % 2][:, h * HALF:(h + 1) * HALF], start=True, stop=True)
                mm(psum[:, 6, :], swap, dst[:, TP:N], start=True, stop=True).then_inc(qk_st, 1)

            for e in range(14):
                gemm(L_AQ + e)
                if 1 <= e <= 12:
                    qk_stats(e - 1)
            pe.wait_ge(rope, 12)
            pe.wait_ge(qk_rb, 12)
            turn(12)
            turn(13)
            pe.wait_ge(ck_in, 48)
            pe.wait_ge(tr_ev, 14)
            for g in range(KVH):
                last = tp(psum[:, 4, g * PAST:(g + 1) * PAST], ck2[:, g, :, :].rearrange("s r d -> s (r d)"), ident)
            last.then_inc(ck_t, 1)
            pe.wait_ge(rope_out, 12)
            for g in range(KVH):
                last = tp(psum[:, 5, g * HD:(g + 1) * HD], ak[0:HD, g, 0:P], ident[0:HD, 0:HD])
            last.then_inc(ck_t, 1)

            def scores(k):
                c, m, s = k // AH, k % AH // 2, k % 2
                half = slice(s * HD, (s + 1) * HD)
                if k >= 2:
                    pe.wait_ge(aexp, k - 1)
                else:
                    pe.wait_ge(ck_ev, 2)
                q = aq[half, m, c * P:(c + 1) * P]
                if c == 0:
                    last = mm(psum[:, 4 * s, 0:P], q, ak[half, m // 2, 0:TP], start=True, stop=True)
                else:
                    mm(psum[:, 4 * s, :], q, ak[half, m // 2, TP:N], start=True, stop=True)
                    last = mm(psum[:, 4 * s + 1, 0:PAST], q, akc[half, m // 2, :], start=True, stop=True)
                last.then_inc(sc, 1)

            def turn_p(k):
                c, s = k // AH, k % 2
                pe.wait_ge(aexp, k + 1)
                if k >= 2:
                    pe.wait_ge(oev, k - 1)
                if k >= 3 and k % 2:
                    pe.wait_ge(ha_ev, (k - 3) // 2 + 1)
                for b in range(1 if c == 0 else NT):
                    last = tp(flat(2 * s + 1)[:, b * P:(b + 1) * P], sa[s][:, b * P:(b + 1) * P], ident)
                last.then_inc(atr, 1)

            def values(k):
                c, m, s = k // AH, k % AH // 2, k % 2
                pe.wait_ge(pta, k + 1)
                if c > 0:
                    pe.wait_ge(ptb, k + 1 - AH)
                tiles = [0] if c == 0 else list(range(1, NT + 1))
                for b, v in enumerate(tiles):
                    last = mm(psum[:, 4 * s + 3, P:P + HD], sb[s][:, b * P:(b + 1) * P],
                              av[:, v, (m // 2) * HD:(m // 2 + 1) * HD], start=(b == 0), stop=(b == len(tiles) - 1))
                last.then_inc(pv, 1)

            def turn_o(q):
                pe.wait_ge(oev, 2 * q + 2)
                tp(psum[:, 7, 2 * P:3 * P], os_[:, q % 2, :], ident).then_inc(pt_o, 1)

            scores(0)
            for k in range(HEADS):
                if k >= 3 and k % 2:
                    turn_o((k - 3) // 2)
                if k + 1 < HEADS:
                    scores(k + 1)
                turn_p(k)
                if k >= 1:
                    values(k - 1)
            values(HEADS - 1)
            turn_o(HEADS // 2 - 1)

            for l in range(L_MO, L_BM):
                if l == L_MO:
                    pe.wait_ge(ha_ev, HEADS // 2)
                gemm(l)
            for m in range(KC):
                gemm(L_BM + 2 * m)
                gemm(L_BM + 2 * m + 1, m_hi, m_lo, mg_lo if m == 0 else None)
            for m in range(KC):
                gemm(L_BA + 2 * m)
                gemm(L_BA + 2 * m + 1, m_hi, m_lo, hal if m == 0 else None)
            for m in range(KC):
                gemm(L_OUT + m, h_hi, h_lo, yl if m == 0 else None)
            stats(3)
            stats(4)
            ffn(1, T_FFN1)
            stats(5)
            for c in range(NT):
                if c >= 2:
                    pe.wait_ge(oe, c - 1)
                else:
                    pe.wait_ge(x_upd, 3 * KC)
                for k in range(KC):
                    last = tp(flat(c % 2)[:, k * P:(k + 1) * P], x[:, k, c * P:(c + 1) * P], ident)
                last.then_inc(ot, 1)

        @block.scalar
        def _(act):
            fn, copy = act.activation, act.copy

            def split(t):
                act.wait_ge(raw_in[t.raw], 16 * (t.quad + 1))
                act.wait_ge(tile_done, t.n + 1)
                copy(whi[t.slot][:, :, :], raw[t.raw][:, :, :]).then_inc(w_hi, 1)

            def done(t):
                act.wait_ge(tile_done, t.n + 3)

            def stats(n, src, ready):
                for k in range(KC):
                    ready(k)
                    if k >= 2:
                        act.wait_ge(stat_mm, 8 * n + k - 1)
                    fn(sq[k % 2][:, :], src[:, k, :], ACT.Square).then_inc(sq_in, 1)
                act.wait_ge(stat_mm, 8 * n + KC)
                fn(halves(rb[:, :]), both(2), ACT.Sqrt, bias=epsc[:, 0:1]).then_inc(rb_sqrt, 1)

            def normed(l):
                for k in range(KC):
                    act.wait_ge(pre_t, 8 * l + k + 1)
                    if k >= 2:
                        act.wait_ge(h_rdy, 8 * l + k - 1)
                    for g, cols in GROUPS:
                        last = fn(sb[k % 2][:, cols], sa[k % 2][:, cols], ACT.Identity,
                                  bias=mod[:, 3 * l * KC + k, g:g + 1], scale=pre_s[:, l, k, g:g + 1])
                    last.then_inc(pre_h, 1)
                    act.wait_ge(pre_h, 8 * l + k + 1)
                    copy(h_hi[:, k, :], sb[k % 2][:, :]).then_inc(pre_hi, 1)

            def wait_upd(count):
                return lambda k: act.wait_ge(x_upd, count + k + 1)

            def wait_out(base):
                def ready(k):
                    t = Tile(base + k)
                    act.wait_ge(ev[t.slot], t.pair + 1)
                return ready

            act.wait_ge(v_ready, 1)
            fn(silc[:, :, :], vT[:, V_CC:V_QG].rearrange("p (g k) -> p g k", g=2), ACT.Silu).then_inc(silc_ready, 1)
            for k in range(0, KC, 2):
                act.wait_ge(x_t, k + 1)
                copy(x[:, k, :], flat(0)[:, 0:N]).then_inc(x_ev[0], 1)
            split(Tile(0))
            split(Tile(1))
            act.wait_ge(eps_in, 2)
            stats(0, x, lambda k: act.wait_ge(x_ev[k % 2], k // 2 + 1))
            act.wait_ge(mod_ready, 1)
            normed(0)

            def ffn(f, base):
                j0 = 0
                for p, nj in enumerate(PHASES):
                    with act.Fori(0, nj // 2) as i:
                        for u in range(4):
                            t = Tile(base + u, i)
                            s = t.c // 2 % 2
                            if u % 2 == 0:
                                done(t)
                                fn(halves(sa[s][:, :]), both(t.slot), ACT.Silu).then_inc(ev[t.slot], 1)
                                split(t.plus(2))
                            else:
                                split(t.plus(2))
                                act.wait_ge(ev[t.slot], t.pair + 1)
                                out = g_hi[:, bass.ds(2 * i + u // 2, 1), :].rearrange("p o n -> p (o n)")
                                copy(out, sb[s][:, :]).then_inc(g_hi_s, 1)
                    base += 2 * nj
                    tail = f == 1 and p == len(PHASES) - 1

                    def outs(t, m):
                        done(t)
                        if p == 0:
                            dst = y[:, bass.ds(m, 1), :].rearrange("p o (h n) -> p (o h) n", h=2)
                            copy(dst, both(t.slot)).then_inc(ev[t.slot], 1)
                    if tail:
                        for u in range(KC - 2):
                            split(Tile(base + u + 2))
                    else:
                        with act.Fori(0, 2) as i:
                            for u in range(4):
                                t = Tile(base + u, i)
                                outs(t, 4 * i + u)
                                split(t.plus(2))
                    base += KC
                    j0 += nj

            ffn(0, 0)
            stats(1, y, wait_out(FFN_TILES - KC))
            stats(2, x, wait_upd(0))
            act.wait_ge(mod_ready, 2)
            normed(1)

            for l in range(L_AQ):
                t = Tile(T_MIX + l)
                done(t)
                if l == L_GATE:
                    act.wait_ge(ld_row, 48)
                    for q, dst in enumerate((gi, gf, gi, gf)):
                        last = fn(halves(dst[:, q // 2, :]), psum[32 * q:32 * q + H, 2 * t.slot:2 * t.slot + 2, 0:HALF],
                                  ACT.Identity, bias=gbias[:, q:q + 1])
                elif l < L_MK:
                    last = fn(halves(mq[:, l - L_MQ, :]), both(t.slot), ACT.Copy, scale=DK ** -0.5)
                elif l < L_MV:
                    last = copy(halves(mk[:, l - L_MK, :]), both(t.slot))
                else:
                    jb = 4 + l - L_MV
                    if jb >= 6:
                        act.wait_ge(tr_done, jb - 1)
                    last = copy(halves(sa[jb % 2][:, :]), both(t.slot))
                last.then_inc(ev[t.slot], 1)
                split(t.plus(2))

            act.wait_ge(row_d, 1)
            fn(t1[:, :, :], t1[:, :, :], ACT.Exp, scale=-1.0).then_inc(row_a, 1)
            act.wait_ge(row_a, 1)
            fn(t1[:, :, :], t1[:, :, :], ACT.Ln, bias=epsc[0:H, 1:2]).then_inc(row_a, 1)
            act.wait_ge(row_d, ROW_END)
            fn(ar[:, :, :], ar[:, :, :], ACT.Exp).then_inc(row_a, 1)
            fn(t1[:, :, :], t1[:, :, :], ACT.Exp).then_inc(row_a, 1)
            fn(gf[:, :, :], gf[:, :, :], ACT.Exp).then_inc(row_a, 1)
            fn(gm[:, :, :], gm[:, :, :], ACT.Exp, scale=-1.0).then_inc(row_a, 1)

            def squares(n):
                act.wait_ge(hm_in, n + 1)
                for hh in range(2):
                    last = fn(sq[1][:, (2 * (n % 2) + hh) * P:(2 * (n % 2) + hh + 1) * P], hmt[:, n % 2, hh, :], ACT.Square, accum_out=ss[:, n % 2, hh:hh + 1])
                last.then_inc(ss_in, 1)
                act.wait_ge(ss_in, 3 * n + 1)
                fn(ss[:, n % 2, :], ss[:, n % 2, :], ACT.Ln, bias=epsc[:, 0:1], scale=1.0 / DV).then_inc(ss_in, 1)
                act.wait_ge(ss_in, 3 * n + 2)
                fn(ss[:, n % 2, :], ss[:, n % 2, :], ACT.Exp, scale=-0.5).then_inc(ss_in, 1)

            def store_hm(n):
                c, j = n // 4, n % 4
                act.wait_ge(hm_t, n + 1)
                for hh in range(2):
                    g = 2 * j + hh
                    last = fn(hm[:, g, c * P:(c + 1) * P], psum[:, 7, hh * P:(hh + 1) * P], ACT.Copy,
                              scale=vT[:, V_MN + g:V_MN + g + 1])
                last.then_inc(hm_ev, 1)

            for n in range(UNITS):
                act.wait_ge(e_min, n + 1)
                fn(sa[n % 2][:, 0:4 * P], sa[n % 2][:, 0:4 * P], ACT.Exp).then_inc(e_exp, 1)
                if n >= 3:
                    store_hm(n - 3)
                if n >= 1:
                    squares(n - 1)
            squares(UNITS - 1)
            for n in range(UNITS - 3, UNITS):
                store_hm(n)

            def inv_rms(e):
                act.wait_ge(qk_st, e + 1)
                if e >= 1:
                    act.wait_ge(rope_out, e)
                fn(halves(rb[:, :]), both(2), ACT.Ln, bias=epsc[:, 0:1]).then_inc(qk_rb, 1)
                act.wait_ge(qk_rb, e + 1)
                fn(rb[:, :], rb[:, :], ACT.Exp, scale=-0.5).then_inc(qk_rs, 1)

            for e in range(14):
                t = Tile(T_MIX + L_AQ + e)
                done(t)
                if e < 12:
                    dst, gain = (aq[:, e, :], V_QG) if e < KC else (ak[:, e - KC, :], V_KG)
                    fn(halves(dst), both(t.slot), ACT.Copy, scale=vT[:, gain:gain + 1])
                    if e >= 2:
                        act.wait_ge(qk_st, e - 1)
                    last = fn(halves(sq[e % 2][:, :]), both(t.slot), ACT.Square)
                else:
                    last = copy(halves(sa[e % 2][:, :]), both(t.slot))
                last.then_inc(ev[t.slot], 1)
                split(t.plus(2))
                if 1 <= e <= 12:
                    inv_rms(e - 1)

            def store_ha(q):
                c, m = q // KC, q % KC
                act.wait_ge(pt_o, q + 1)
                copy(ha[:, m, c * P:(c + 1) * P], psum[:, 7, 2 * P:3 * P]).then_inc(ha_ev, 1)

            def take_p(k):
                c, s = k // AH, k % 2
                act.wait_ge(atr, k + 1)
                if k >= 2:
                    act.wait_ge(pv, k - 1)
                w = P if c == 0 else 4 * P
                copy(sb[s][:, 0:w], flat(2 * s + 1)[:, 0:w]).then_inc(pta, 1)

            for k in range(HEADS):
                c, s = k // AH, k % 2
                act.wait_ge(nmx, 2 * k + 2)
                if k >= 2:
                    act.wait_ge(atr, k - 1)
                w = P if c == 0 else N
                fn(sa[s][:, 0:w], flat(2 * s)[:, 0:w], ACT.Exp, bias=amax[:, s:s + 1], scale=HD ** -0.5,
                   accum_out=asum[:, s:s + 1]).then_inc(aexp, 1)
                if k >= 3 and k % 2:
                    store_ha((k - 3) // 2)
                if k >= 1:
                    take_p(k - 1)
            take_p(HEADS - 1)
            store_ha(HEADS // 2 - 1)

            def high(k, dst, src, ready, count, out):
                act.wait_ge(ready, count)
                copy(dst[:, k, :], src).then_inc(out, 1)

            for l in range(L_MO, L_END):
                t = Tile(T_MIX + l)
                done(t)
                if l < L_BM:
                    m = l - L_MO
                    if m >= 2:
                        act.wait_ge(mg, m - 1)
                    fn(halves(sa[m % 2][:, :]), both(t.slot), ACT.Exp, scale=-1.0).then_inc(ev[t.slot], 1)
                elif l < L_OUT:
                    m, gate = (l - L_BM) % 16 // 2, (l - L_BM) % 2 == 0
                    if gate:
                        if m >= 2:
                            v = t.plus(-3)
                            act.wait_ge(ev[v.slot], v.pair + 1)
                        fn(halves(sa[m % 2][:, :]), both(t.slot), ACT.Exp, scale=-1.0).then_inc(ev[t.slot], 1)
                else:
                    m = l - L_OUT
                    act.wait_ge(yl, m + 1)
                    copy(halves(y[:, m, :]), both(t.slot)).then_inc(ev[t.slot], 1)
                split(t.plus(2))
                if L_MO < l <= L_BM:
                    m = l - 1 - L_MO
                    high(m, m_hi, sb[m % 2][:, :], mg, m + 1, mg_hi)
                if l == L_BA - 1:
                    for k in range(KC):
                        high(k, m_hi, ha[:, k, :], ha_ev, HEADS // 2, hah)
                if l == L_OUT - 2:
                    for k in range(KC - 1):
                        high(k, h_hi, y[:, k, :], y_sum, k + 1, yh)
                if l == L_OUT - 1:
                    high(KC - 1, h_hi, y[:, KC - 1, :], y_sum, KC, yh)

            stats(3, y, wait_out(T_MIX + L_OUT))
            stats(4, x, wait_upd(KC))
            normed(2)
            ffn(1, T_FFN1)
            stats(5, y, wait_out(T_END - KC))
            for c in range(NT):
                act.wait_ge(ot, c + 1)
                if c >= 2:
                    act.wait_ge(out_st, 16 * (c - 1))
                copy(otok[c % 2][:, :], flat(c % 2)).then_inc(oe, 1)

        @block.vector
        def _(dve):
            tt, ts, stt, copy = dve.tensor_tensor, dve.tensor_scalar, dve.scalar_tensor_tensor, dve.tensor_copy
            steps = [0]

            def step(ins):
                steps[0] += 1
                ins.then_inc(dv, 1)
                dve.wait_ge(dv, steps[0])

            def split(t):
                dve.wait_ge(w_hi, t.n + 1)
                tt(wlo[t.slot][:, :, :], raw[t.raw][:, :, :], whi[t.slot][:, :, :].bitcast(F32),
                   ALU.subtract).then_inc(raw_free, 1)

            def done(t):
                dve.wait_ge(tile_done, t.n + 3)

            def inverse(n):
                dve.wait_ge(rb_sqrt, n + 1)
                dve.reciprocal(rb[:, :], rb[:, :]).then_inc(rb_ready, 1)
                dve.wait_ge(rb_ready, n + 1)

            def normed(l):
                def low(k):
                    dve.wait_ge(pre_hi, 8 * l + k + 1)
                    tt(h_lo[:, k, :], sb[k % 2][:, :], h_hi[:, k, :].bitcast(F32), ALU.subtract).then_inc(h_rdy, 1)
                for k in range(KC):
                    if k >= 2:
                        dve.wait_ge(pre_h, 8 * l + k - 1)
                    tt(sa[k % 2][:, :], x[:, k, :], rb[:, :], ALU.mult).then_inc(pre_t, 1)
                    if k >= 1:
                        low(k - 1)
                low(KC - 1)

            def residual(l):
                def add(k):
                    dve.wait_ge(post_t, 8 * l + k + 1)
                    for g, cols in GROUPS:
                        last = stt(x[:, k, cols], sa[k % 2][:, cols], post_s[:, l, k, g:g + 1], x[:, k, cols],
                                   ALU.mult, ALU.add)
                    last.then_inc(x_upd, 1)
                for k in range(KC):
                    if k >= 2:
                        dve.wait_ge(x_upd, 8 * l + k - 1)
                    tt(sa[k % 2][:, :], y[:, k, :], rb[:, :], ALU.mult).then_inc(post_t, 1)
                    if k >= 1:
                        add(k - 1)
                add(KC - 1)

            def per_group(col):
                return vT[:, col:col + KC].rearrange("p (k o) -> p k o", o=1).broadcast_to([P, KC, 2])

            def scales(l, which):
                if which == "pre":
                    step(stt(pre_s[:, l, :, :], mod[:, (3 * l + 1) * KC:(3 * l + 2) * KC, :], 1.0,
                             per_group(V_PRE + l * KC), ALU.add, ALU.mult))
                else:
                    step(stt(post_s[:, l, :, :], mod[:, (3 * l + 2) * KC:(3 * l + 3) * KC, :], 0.5 if l != 1 else 1.0,
                             per_group(V_POST + l * KC), ALU.mult, ALU.mult))

            def take_mod(lo, hi):
                dve.wait_ge(mod_done, hi)
                step(tt(mod[:, lo:hi, :], modp[:, 2 * lo:2 * hi].rearrange("p (t g) -> p t g", g=2),
                        vT[:, lo:hi].rearrange("p (t o) -> p t o", o=1).broadcast_to([P, hi - lo, 2]), ALU.add))

            dve.sem_inc(raw_free, RAWS)
            dve.memset(epsc[:, 0:1], EPS).then_inc(eps_in, 1)
            dve.memset(epsc[:, 1:2], 1.0).then_inc(eps_in, 1)
            dve.wait_ge(vec_t, 1)
            copy(vT[:, :], psum[:, 6, 0:V_N]).then_inc(v_ready, 1)
            for k in range(1, KC, 2):
                dve.wait_ge(x_t, k + 1)
                copy(x[:, k, :], flat(1)[:, 0:N]).then_inc(x_ev[1], 1)
            split(Tile(0))
            split(Tile(1))
            dve.wait_ge(v_ready, 1)
            take_mod(0, 2 * KC)
            stt(pre_s[:, 0, :, :], mod[:, KC:2 * KC, :], 1.0, per_group(V_PRE), ALU.add, ALU.mult).then_inc(mod_ready, 1)
            inverse(0)
            dve.wait_ge(x_ev[0], 4)
            dve.wait_ge(x_ev[1], 4)
            normed(0)

            def ffn(f, base):
                j0 = 0
                for p, nj in enumerate(PHASES):
                    with dve.Fori(0, nj // 2) as i:
                        for u in range(4):
                            t = Tile(base + u, i)
                            s = t.c // 2 % 2 if u % 2 == 0 else t.plus(-1).c // 2 % 2
                            split(t.plus(2))
                            if u % 2:
                                g = t.plus(-1)
                                done(t)
                                dve.wait_ge(ev[g.slot], g.pair + 1)
                                tt(halves(sb[s][:, :]), halves(sa[s][:, :]), both(t.slot), ALU.mult).then_inc(ev[t.slot], 1)
                                dve.wait_ge(g_hi_s, NJ * f + j0 + 2 * i + u // 2 + 1)
                                jj = bass.ds(2 * i + u // 2, 1)
                                tt(g_lo[:, jj, :].rearrange("p o n -> p (o n)"), sb[s][:, :],
                                   g_hi[:, jj, :].rearrange("p o n -> p (o n)").bitcast(F32),
                                   ALU.subtract).then_inc(g_lo_s, 1)
                    base += 2 * nj
                    if p > 0:
                        for q in (base - 2 * nj - 1, base - 2 * nj - 2):
                            dve.wait_ge(ev[q % 2], q // 2 + 1)

                    def outs(t, m):
                        if p > 0:
                            done(t)
                            yv = y[:, bass.ds(m, 1), :].rearrange("p o (h n) -> p (o h) n", h=2)
                            tt(yv, yv, both(t.slot), ALU.add).then_inc(ev[t.slot], 1)
                    if f == 1 and p == len(PHASES) - 1:
                        for u in range(KC):
                            if u < KC - 2:
                                split(Tile(base + u + 2))
                            outs(Tile(base + u), u)
                    else:
                        with dve.Fori(0, 2) as i:
                            for u in range(4):
                                t = Tile(base + u, i)
                                split(t.plus(2))
                                outs(t, 4 * i + u)
                    base += KC
                    j0 += nj

            ffn(0, 0)
            take_mod(2 * KC, NMOD * KC)
            for l in range(3):
                scales(l, "post")
            scales(1, "pre")
            stt(pre_s[:, 2, :, :], mod[:, 7 * KC:8 * KC, :], 1.0, per_group(V_PRE + 2 * KC),
                ALU.add, ALU.mult).then_inc(mod_ready, 1)
            inverse(1)
            residual(0)
            inverse(2)
            dve.wait_ge(x_upd, KC)
            normed(1)

            def take_turned(jb):
                dve.wait_ge(tr_done, jb + 1)
                if jb < 4:
                    dst = mkt[:, :, jb * P:(jb + 1) * P]
                elif jb < 12:
                    dst = vt[:, :, jb - 4, 0:DV]
                else:
                    dst = av[:, 0:NT, (jb - 12) * P:(jb - 11) * P]
                copy(dst, flat(2 + jb % 2)[:, 0:N].rearrange("p (c t) -> p c t", c=NT)).then_inc(tr_ev, 1)

            dve.wait_ge(x_spill, 16)
            for l in range(L_AQ):
                split(Tile(T_MIX + l + 2))
                if l == 0:
                    dve.wait_ge(tile_done, 2 + T_MIX)
                    dve.memset(vt[:, :, :, DV:DV + 1], 1.0).then_inc(ones_v, 1)
                if l > L_MK:
                    take_turned(l - L_MK - 1)
            take_turned(11)

            rows = [0]

            def row_step(ins, wait=True):
                rows[0] += 1
                ins.then_inc(row_d, 1)
                if wait:
                    dve.wait_ge(row_d, rows[0])

            t = Tile(T_MIX)
            dve.wait_ge(ev[t.slot], t.pair + 1)
            row_step(stt(t1[:, :, :], gf[:, :, :], -1.0, gf[:, :, :], ALU.mult, ALU.max))
            dve.wait_ge(row_a, 2)
            row_step(stt(gf[:, :, :], gf[:, :, :], 0.0, t1[:, :, :], ALU.min, ALU.subtract))
            for c in range(NT):
                for d in range(2):
                    seg = slice(c * P, (c + 1) * P) if d == 0 else slice((c + 1) * P - 1, c * P - 1 if c else None, -1)
                    row_step(dve.tensor_tensor_scan(gb[:, d, seg], one_row, gf[:, d, seg], 0.0, ALU.mult, ALU.add), False)
            for d in range(2):
                for g, cols in GROUPS:
                    if d:
                        cols = slice(cols.stop - 1, cols.start - 1 if cols.start else None, -1)
                    row_step(dve.tensor_tensor_scan(gm[:, d, cols], gf[:, d, cols], gi[:, d, cols],
                                                    m0[:, d:d + 1] if g else 0.0, ALU.add, ALU.max), False)
            dve.wait_ge(row_d, rows[0])
            row_step(dve.memset(m_in[:, :, 0:1], 0.0), False)
            row_step(copy(m_in[:, 0, 1:2], m0[:, 0:1]), False)
            row_step(copy(m_in[:, 1, NT - 1:NT], m0[:, 1:2]), False)
            row_step(copy(m_in[:, 0, 2:NT], gm[:, 0, 2 * P - 1:(NT - 1) * P:P]), False)
            row_step(copy(m_in[:, 1, 1:NT - 1], gm[:, 1, 2 * P:(NT - 1) * P + 1:P]), False)
            row_step(copy(mout[:, 0:1], gm[:, 0, TP - 1:TP]), False)
            row_step(copy(mout[:, 1:2], gm[:, 1, 0:1]), False)
            assert rows[0] == ROW_M
            row_step(tt(gi[:, :, :], gi[:, :, :], gb[:, :, :], ALU.subtract), False)
            row_step(tt(nm[:, :, :], gb[:, :, :], gm[:, :, :], ALU.subtract))
            row_step(copy(nml[:, 0, :], nm[:, 0, P - 1:N:P]), False)
            row_step(copy(nml[:, 1, :], nm[:, 1, 0:N:P]))

            def tiles(v):
                return v[:, :, :].rearrange("h d (c t) -> h (d c) t", t=P)

            def spread(v):
                return v[:, :, :].rearrange("h d (c o) -> h (d c) o", o=1).broadcast_to([H, 2 * NT, P])

            row_step(tt(ar[:, :, :], m_in[:, :, :], nml[:, :, :], ALU.add), False)
            row_step(tt(tiles(t1), tiles(nm), spread(m_in), ALU.add), False)
            row_step(tt(tiles(gf), tiles(gi), spread(nml), ALU.add), False)
            assert rows[0] == ROW_END
            dve.wait_ge(tok_t, 2)
            copy(tk[:, :, :, :, :].rearrange("p q c d h -> p (q c d h)"), psum[:, 4, 0:3 * NT * 2 * H]).then_inc(tok_ev, 1)
            copy(ab[:, :, :].rearrange("p j c -> p (j c)"), psum[:, 5, 0:8 * NT]).then_inc(tok_ev, 1)
            dve.wait_ge(tok_ev, 2)

            dve.wait_ge(st_in, 64)
            for s in range(len(STATES) + 1):
                if s < len(STATES):
                    d, c = STATES[s]
                    if s >= 2:
                        dve.wait_ge(kv_done, s - 1)
                    w = tk[:, 1, c, d, :].rearrange("p (h o) -> p h o", o=1).broadcast_to([P, H, DK])
                    tt(sa[s % 2][:, 0:H * DK].rearrange("p (h k) -> p h k", h=H),
                       mkt[:, c, :].rearrange("p (h k) -> p h k", h=H), w, ALU.mult).then_inc(kw_in, 1)
                if s >= 1:
                    d, c = STATES[s - 1]
                    s1 = (s - 1) % 2
                    dve.wait_ge(kv_done, s)
                    if c == 0:
                        for b in range(2):
                            last = copy(cp[:, d, 2 * b:2 * b + 2, :].rearrange("p j v -> p (j v)"),
                                        psum[:, 2 * s1 + b, 0:2 * (DV + 1)])
                    else:
                        if s >= 3:
                            dve.wait_ge(st_upd, s - 2)
                        for j in range(4):
                            to = c - 1 + (1 if d == 0 else -1)
                            last = stt(cs[:, d, to, j, :], cs[:, d, c - 1, j, :], ab[:, j, d * NT + c:d * NT + c + 1],
                                       psum[:, 2 * s1 + j // 2, (j % 2) * (DV + 1):(j % 2 + 1) * (DV + 1)],
                                       ALU.mult, ALU.add)
                    last.then_inc(st_upd, 1)

            def decays(n):
                c, j = n // 4, n % 4
                dve.wait_ge(front, n + 1)
                if n >= 2:
                    dve.wait_ge(nums, n - 1)
                e = sa[n % 2][:, 0:4 * P].rearrange("p (d g t) -> p d g t", d=2, g=2)
                for d in range(2):
                    for hh in range(2):
                        o = (2 * d + hh) * P
                        last = stt(e[:, d, hh, :], psum[:, 4, o:o + P], tk[:, 0, c, d, 2 * j + hh:2 * j + hh + 1],
                                   mask[d], ALU.add, ALU.min)
                last.then_inc(e_min, 1)
                if c > 0:
                    q = mq[:, j, c * P:(c + 1) * P].rearrange("p (o t) -> p o t", o=1).broadcast_to([P, 2, P])
                    tt(qw[:, n % 2, :, :], q, psum[:, 5, P:3 * P].rearrange("p (d t) -> p d t", d=2), ALU.mult)
                dve.wait_ge(e_exp, n + 1)
                for hh in range(2):
                    s = psum[:, 5 + hh, 0:P].rearrange("p (o t) -> p o t", o=1).broadcast_to([P, 2, P])
                    last = tt(e[:, :, hh, :], e[:, :, hh, :], s, ALU.mult)
                last.then_inc(s_in, 1)

            def outputs(n):
                c, j, s = n // 4, n % 4, n % 2
                dve.wait_ge(nums, n + 1)
                v = psum[:, 2 * s:2 * s + 2, 0:2 * (DV + 1)].rearrange("p g (d v) -> p g d v", d=2)
                dv_, num = v[:, :, :, DV:DV + 1].rearrange("p g d o -> p g (d o)"), v[:, :, :, 0:DV]
                floor = tk[:, 2, c, :, 2 * j:2 * j + 2].rearrange("p d g -> p g d")
                stt(den[:, :, :], dv_, -1.0, floor, ALU.mult, ALU.max).then_inc(den_s, 1)
                dve.wait_ge(den_s, 4 * n + 1)
                tt(den[:, :, :], den[:, :, :], dv_, ALU.max).then_inc(den_s, 1)
                dve.wait_ge(den_s, 4 * n + 2)
                dve.reciprocal(den[:, :, :], den[:, :, :]).then_inc(den_s, 1)
                dve.wait_ge(den_s, 4 * n + 3)
                tmp = sb[0][:, 0:4 * P].rearrange("p (g d v) -> p g d v", g=2, d=2)
                for hh in range(2):
                    r = den[:, hh, :].rearrange("p (d o) -> p d o", o=1).broadcast_to([P, 2, DV])
                    last = tt(tmp[:, hh, :, :], num[:, hh, :, :], r, ALU.mult)
                last.then_inc(den_s, 1)
                dve.wait_ge(den_s, 4 * n + 4)
                if n >= 2:
                    dve.wait_ge(hm_t, n - 1)
                tt(hmt[:, s, :, :], tmp[:, :, 0, :], tmp[:, :, 1, :], ALU.add).then_inc(hm_in, 1)

            def scale_hm(n):
                dve.wait_ge(ss_in, 3 * n + 3)
                r = ss[:, n % 2, :].rearrange("p (g o) -> p g o", o=1).broadcast_to([P, 2, DV])
                tt(hmt[:, n % 2, :, :], hmt[:, n % 2, :, :], r, ALU.mult).then_inc(hm_sc, 1)

            dve.wait_ge(kv_done, len(STATES))
            dve.wait_ge(st_upd, len(STATES))
            for n in range(UNITS):
                decays(n)
                if n >= 1:
                    outputs(n - 1)
                if n >= 2:
                    scale_hm(n - 2)
            outputs(UNITS - 1)
            scale_hm(UNITS - 2)
            scale_hm(UNITS - 1)

            def turn_halves(e):
                dst = aq[:, e, :] if e < KC else ak[:, e - KC, :]
                lat = dst[:, TP:N]
                dve.wait_ge(qk_st, e + 1)
                tt(sb[0][:, 0:TS], psum[:, 6, :], sin, ALU.mult).then_inc(rope, 1)
                tt(lat, lat, cos, ALU.mult).then_inc(rope_c, 1)
                dve.wait_ge(rope_c, 2 * e + 1)
                tt(lat, lat, sb[0][:, 0:TS], ALU.add).then_inc(rope_c, 1)
                dve.wait_ge(rope_c, 2 * e + 2)
                dve.wait_ge(qk_rs, e + 1)
                tt(dst, dst, rb[:, :], ALU.mult).then_inc(rope_out, 1)

            for e in range(14):
                split(Tile(T_MIX + L_AQ + e + 2))
                if 1 <= e <= 12:
                    turn_halves(e - 1)
            take_turned(12)
            take_turned(13)
            dve.wait_ge(ck_t, 1)
            copy(akc[:, :, :].rearrange("p g s -> p (g s)"), psum[:, 4, :]).then_inc(ck_ev, 1)
            dve.wait_ge(ck_t, 2)
            copy(ko[:, :], psum[:, 5, 0:KVH * HD]).then_inc(ck_ev, 1)

            def top(k):
                c, s = k // AH, k % 2
                w = P if c == 0 else N
                dve.wait_ge(sc, k + 1)
                dve.reduce_max(amax[:, s:s + 1], flat(2 * s)[:, 0:w], AX.X).then_inc(nmx, 1)
                dve.wait_ge(nmx, 2 * k + 1)
                ts(amax[:, s:s + 1], amax[:, s:s + 1], -HD ** -0.5, None, ALU.mult).then_inc(nmx, 1)

            def middle(k):
                c, s = k // AH, k % 2
                dve.wait_ge(aexp, k + 1)
                if k >= 2:
                    dve.wait_ge(oev, k - 1)
                dve.reciprocal(arec[:, s:s + 1], asum[:, s:s + 1]).then_inc(rcp, 1)
                if c > 0:
                    dve.wait_ge(atr, k + 1)
                    dve.wait_ge(pv, k - 1)
                    copy(sb[s][:, 4 * P:N], flat(2 * s + 1)[:, 4 * P:N]).then_inc(ptb, 1)

            def final(k):
                q, s = k // 2, k % 2
                dve.wait_ge(pv, k + 1)
                dve.wait_ge(rcp, k + 1)
                if q >= 2:
                    dve.wait_ge(pt_o, q - 1)
                ts(os_[:, q % 2, s * HD:(s + 1) * HD], psum[:, 4 * s + 3, P:P + HD], arec[:, s:s + 1], None,
                   ALU.mult).then_inc(oev, 1)

            for k in range(HEADS):
                top(k)
                if k >= 1:
                    middle(k - 1)
                if k >= 2:
                    final(k - 2)
            middle(HEADS - 1)
            final(HEADS - 2)
            final(HEADS - 1)

            def sigmoid(t, m):
                dve.wait_ge(ev[t.slot], t.pair + 1)
                v = sa[m % 2][:, :]
                ts(v, v, 1.0, None, ALU.add).then_inc(sig, 1)
                sigs[0] += 1
                dve.wait_ge(sig, sigs[0])
                dve.reciprocal(v, v).then_inc(sig, 1)
                sigs[0] += 1
                dve.wait_ge(sig, sigs[0])

            sigs = [0]

            def low_m(m):
                dve.wait_ge(mg_hi, m + 1)
                tt(m_lo[:, m, :], sb[m % 2][:, :], m_hi[:, m, :].bitcast(F32), ALU.subtract).then_inc(mg_lo, 1)

            for l in range(L_MO, L_END):
                t = Tile(T_MIX + l)
                split(t.plus(2))
                if l < L_BM:
                    m = l - L_MO
                    sigmoid(t, m)
                    tt(sb[m % 2][:, :], hm[:, m, :], sa[m % 2][:, :], ALU.mult).then_inc(mg, 1)
                    if m >= 1:
                        low_m(m - 1)
                elif l < L_OUT:
                    m, gate = (l - L_BM) % 16 // 2, (l - L_BM) % 2 == 0
                    if l == L_BM:
                        low_m(KC - 1)
                    if gate:
                        sigmoid(t, m)
                    elif l < L_BA:
                        done(t)
                        tt(halves(y[:, m, :]), halves(sa[m % 2][:, :]), both(t.slot), ALU.mult).then_inc(ev[t.slot], 1)
                    else:
                        done(t)
                        tt(halves(sb[m % 2][:, :]), halves(sa[m % 2][:, :]), both(t.slot), ALU.mult).then_inc(ev[t.slot], 1)
                        dve.wait_ge(ev[t.slot], t.pair + 1)
                        tt(y[:, m, :], y[:, m, :], sb[m % 2][:, :], ALU.add).then_inc(y_sum, 1)
                if l == L_BA - 1:
                    for k in range(KC):
                        dve.wait_ge(hah, k + 1)
                        tt(m_lo[:, k, :], ha[:, k, :], m_hi[:, k, :].bitcast(F32), ALU.subtract).then_inc(hal, 1)
                if l in (L_OUT - 2, L_OUT - 1):
                    for k in range(KC - 1) if l == L_OUT - 2 else (KC - 1,):
                        dve.wait_ge(yh, k + 1)
                        tt(h_lo[:, k, :], y[:, k, :], h_hi[:, k, :].bitcast(F32), ALU.subtract).then_inc(yl, 1)

            inverse(3)
            dve.wait_ge(x_back, 16)
            residual(1)
            inverse(4)
            dve.wait_ge(x_upd, 2 * KC)
            normed(2)
            ffn(1, T_FFN1)
            inverse(5)
            residual(2)


def constants():
    c = np.zeros((P, C_N), np.float32)
    r = np.arange(P)
    c[:, 0:P] = np.eye(P)
    c[:, P:2 * P] = 1.0 / D
    c[:, 2 * P:3 * P] = (r[:, None] // HD == r[None, :] // HD) / HD
    for p in range(P):
        if p % 32 < 16:
            c[p + 16, 3 * P + p] = -1.0
        else:
            c[p - 16, 3 * P + p] = 1.0
    c[:, 4 * P:5 * P] = np.where(r[:, None] <= r[None, :], 0.0, -1e4)
    c[:, 5 * P:6 * P] = np.where(r[:, None] >= r[None, :], 0.0, -1e4)
    tok = np.arange(TS)
    pos = np.stack([tok // GRID_W, tok % GRID_W]).astype(np.float32)
    freq = np.float32(10000.0) ** (-np.arange(16, dtype=np.float32) / np.float32(16))
    ang = pos[(r % HD) // 32] * freq[r % 16][:, None]
    c[:, 6 * P:6 * P + TS] = np.cos(ang)
    c[:, 6 * P + TS:] = np.sin(ang)
    rc = np.zeros((H, R_N), np.float32)
    for h in range(H):
        rc[h, h * P:(h + 1) * P] = 1.0
        o = H * P + (h // 2) * P + (h % 2) * DK
        rc[h, o:o + DK] = 1.0
    rc[:, H * P + 4 * P:] = 1.0
    return c, rc


def lay_out(i):
    f = lambda n: np.asarray(i[n])

    def tiles(w, order=None):
        k, n = w.shape
        w = w.reshape(k // P, P, n // P, P).transpose(2, 1, 0, 3)
        return w.reshape(n // P, P, k)

    wi = f("ffn_w_in")[0].reshape(2, D, 2, NJ, P).transpose(0, 1, 3, 2, 4).reshape(2, D, 2 * DFF)
    mix = f("w_in_mix")[0]
    sizes = (H * DK, H * DK, H * DV, H * DV, 4 * H, AH * HD, KVH * HD, KVH * HD, 2 * D)
    mq, mk, mv, mo, mg, aq, ak, av, bg = np.split(mix, np.cumsum(sizes)[:-1], axis=1)
    gates = np.tile(mg.reshape(D, 4, 1, H), (1, 1, 4, 1)).reshape(D, P)
    keys = np.tile(ak.reshape(D, KVH, 1, HD), (1, 1, 2, 1)).reshape(D, KVH * P)

    def paired(g, w):
        return np.stack([tiles(g), tiles(w)], 1).reshape(2 * KC, P, D)

    w_mix = np.concatenate([
        tiles(gates), tiles(mq), tiles(mk), tiles(mv), tiles(aq), tiles(keys), tiles(av), tiles(mo),
        paired(bg[:, :D], f("w_branch_m")[0]), paired(bg[:, D:], f("w_branch_a")[0]), tiles(f("w_out")[0])])
    qk = f("qk_norm")[0]
    vecs = np.concatenate([
        f("b_mod")[0].reshape(-1, P), f("norm_pre")[0].reshape(-1, P), f("norm_post")[0].reshape(-1, P),
        f("mlstm_norm")[0].reshape(-1, P), f("c_ctx").reshape(-1, P), f("c")[0].reshape(-1, P),
        np.concatenate([qk, qk], axis=1)])
    cst, rowc = constants()
    return {
        "x_prompt": f("x_prompt"), "x_sample": f("x_sample"),
        "w_mod": tiles(f("w_mod")[0]),
        "w_ffn_in": np.concatenate([tiles(wi[0]), tiles(wi[1])]),
        "w_ffn_out": np.concatenate([tiles(f("ffn_w_out")[0, n]) for n in range(2)]),
        "w_mix": w_mix, "vec_rows": vecs, "cst": cst, "rowc": rowc,
        "gate_bias": f("mlstm_gate_bias")[0].reshape(4, H).T,
        "m0": f("state_m")[0, 0].T, "state_C": f("state_C"), "state_n": f("state_n"),
        "cache_k": f("cache_k").reshape(PAST, KVH * HD), "cache_v": f("cache_v").reshape(PAST, KVH * HD),
    }


OUTS = (("o_yp", (1, TP, D)), ("o_ys", (1, TS, D)), ("o_k", (PAST, KVH * HD)), ("o_v", (PAST, KVH * HD)),
        ("o_C", (1, 1, 2, H, DK, DV)), ("o_n", (1, 1, 2, H, DK)), ("o_m", (1, 1, 2, H)))


def kernel(**inputs):
    import concourse.bacc as bacc
    from concourse.bass_utils import run_bass_kernel_spmd

    nc = bacc.Bacc("TRN2", target_bir_lowering=False, num_devices=1)
    arrays, a = {}, {}
    for name, v in lay_out(inputs).items():
        v = np.ascontiguousarray(v)
        arrays[f"in_{name}"] = v
        a[name] = nc.dram_tensor(f"in_{name}", v.shape, mybir.dt.from_np(v.dtype), kind="ExternalInput").ap()
    for name, shape in OUTS:
        a[name] = nc.dram_tensor(name, shape, F32, kind="ExternalOutput").ap()
    a["x_keep"] = nc.dram_tensor("x_keep", (P, KC * N), F32, kind="Internal").ap()
    build(nc, a)
    r = run_bass_kernel_spmd(nc, [arrays], core_ids=[0]).results[0]
    out = [np.asarray(r[name]) for name, _ in OUTS]
    out[2] = out[2].reshape(1, 1, TP, KVH, HD)
    out[3] = out[3].reshape(1, 1, TP, KVH, HD)
    return tuple(out)
```

```python
from contextlib import ExitStack

import numpy as np

import concourse.bass as bass
from concourse import mybir

F32 = mybir.dt.float32
F32R = mybir.dt.float32r
ALU = mybir.AluOpType
ACT = mybir.ActivationFunctionType
AX = mybir.AxisListType

P = 128
D = 1024
KC = D // P
TP, TS = 128, 512
N = TP + TS
LAG = 3
LN_EXP = "natural_log_exp_and_others"
NT = N // P
HALF = N // 2
DFF = 2816
NJ = DFF // P
PHASES = (8, 8, 6)
PAST = 128
H, DK, DV = 8, 64, 128
AH, KVH, HD = 16, 4, 64
GRID_W = 64
EPS = 1e-6
NMOD = 9
MOD_T = 4
MOD_W = MOD_T * P
MOD_FIRST = 2 * KC // MOD_T
MOD_LATER = NMOD * KC // MOD_T - MOD_FIRST
MOD_DVE = 2
MOD_K = ((0, 3), (3, 6), (6, 8))
RAWS = 4
GROUPS = ((0, slice(0, TP)), (1, slice(TP, N)))

L_GATE, L_MQ, L_MK, L_MV, L_AQ, L_AK, L_AV, L_MO, L_BM, L_BA, L_OUT, L_END = np.cumsum(
    [0, 1, 4, 4, 8, 8, 4, 2, 8, 16, 16, 8]).tolist()
FFN_TILES = 2 * NJ + KC * len(PHASES)
T_MIX = FFN_TILES
T_FFN1 = T_MIX + L_END
T_END = T_FFN1 + FFN_TILES
ROW_M, ROW_END = 2 + 2 * NT + 4 + 7, 2 + 2 * NT + 4 + 7 + 4 + 3
UNITS = NT * 4
HEADS = NT * AH
STATES = ((0, 0), (1, 0), (0, 1), (1, 4), (0, 2), (1, 3), (0, 3), (1, 2))
C_N = 6 * P + 2 * TS
R_N = H * P + 4 * P + P

V_PRE, V_POST, V_MN, V_CC, V_QG, V_KG, V_N = 72, 96, 120, 128, 144, 145, 146


class Tile:

    def __init__(self, c, i=0):
        self.c, self.i = c, i
        self.raw, self.slot = c % RAWS, c % 2
        self.n = 4 * i + c
        self.quad = i + c // 4
        self.pair = 2 * i + c // 2

    def plus(self, k):
        return Tile(self.c + k, self.i)


def build(nc, a):
    ctx = ExitStack()
    with ctx:
        def sem(name):
            return ctx.enter_context(nc.semaphore(name))

        def at(name, shape, dt, offset):
            return nc.alloc_sbuf_tensor_at(name, shape, dt, offset=offset)

        row = N * 4
        cur = [-(-nc.sbuf_base // 64) * 64]

        def place(name, shape, dt=F32):
            t = at(name, shape, dt, cur[0])
            cur[0] += -(-int(np.prod(shape[1:])) * 4 // 32) * 32
            return t

        cst = place("cst", [P, C_N])
        rowc = place("rowc", [H, R_N])
        vT = place("vT", [P, V_N])
        silc = place("silc", [P, 2, KC])
        mod = place("mod", [P, NMOD * KC, 2])
        pre_s = place("pre_s", [P, 3, KC, 2])
        post_s = place("post_s", [P, 3, KC, 2])
        gbias = place("gbias", [H, 4])
        m0 = place("m0", [H, 2])
        epsc = place("epsc", [P, 2])
        x_at = cur[0]
        x = place("x", [P, KC, N])
        h_at = cur[0]
        h_hi = place("h_hi", [P, KC, N], F32R)
        h_lo = place("h_lo", [P, KC, N], F32R)
        raw = [place(f"raw{s}", [P, KC, P]) for s in range(RAWS)]
        whi = [place(f"whi{s}", [P, KC, P], F32R) for s in range(2)]
        wlo = [place(f"wlo{s}", [P, KC, P], F32R) for s in range(2)]
        sa = [place(f"sa{s}", [P, N]) for s in range(2)]
        sb_at = cur[0]
        sb = [place(f"sb{s}", [P, N]) for s in range(2)]
        sq_at = cur[0]
        sq = [place(f"sq{s}", [P, N]) for s in range(2)]
        rb = place("rb", [P, N])
        r1 = cur[0]
        r2 = r1 + KC * row
        r3 = r2 + KC * row
        y = at("y", [P, KC, N], F32, r1)
        g_hi = at("g_hi", [P, PHASES[0], N], F32R, r2)
        g_lo = at("g_lo", [P, PHASES[0], N], F32R, r2 + KC * row)
        mw_at = r2 + 2 * KC * row
        mw = at("mw", [P, KC, MOD_W], F32, mw_at)
        macc = at("macc", [P, 2, MOD_W], F32, mw_at + KC * MOD_W * 4)
        mw0 = [at(f"mw0_{s}", [P, KC, MOD_W], F32, r1 + s * KC * MOD_W * 4) for s in range(MOD_FIRST)]
        xtok = at("xtok", [P, NT, D], F32, h_at)
        vrow = at("vrow", [P, P], F32, r1 + MOD_FIRST * KC * MOD_W * 4)
        vrow2 = at("vrow2", [V_N - P, P], F32, r1 + MOD_FIRST * KC * MOD_W * 4 + 512)
        otok = [at(f"otok{s}", [P, D], F32, r2 + s * D * 4) for s in range(2)]
        mkt = at("mkt", [P, NT, H * DK], F32, x_at)
        nm = at("nm", [H, 2, N], F32, x_at + 10240)
        t1 = at("t1", [H, 2, N], F32, x_at + 15360)
        gi = at("gi", [H, 2, N], F32, r1)
        gf = at("gf", [H, 2, N], F32, r1 + 5120)
        gb = at("gb", [H, 2, N], F32, r1 + 10240)
        gm = at("gm", [H, 2, N], F32, r1 + 15360)
        hm = at("hm", [P, H, N], F32, r1)
        mq = at("mq", [P, 4, N], F32, r2)
        mk = at("mk", [P, 4, N], F32, r2 + 4 * row)
        cur[0] = r3
        vt = place("vt", [P, NT, H, DV + 1])
        cs = place("cs", [P, 2, NT - 1, 4, DV + 1])
        tk = place("tk", [P, 3, NT, 2, H])
        ab = place("ab", [P, 4, 2 * NT])
        m_in = place("m_in", [H, 2, NT])
        nml = place("nml", [H, 2, NT])
        ar = place("ar", [H, 2, NT])
        mout = place("mout", [H, 2])
        den = place("den", [P, 2, 2])
        ss = place("ss", [P, 2, 2])
        cp = place("cp", [P, 2, 4, DV + 1])
        end_m = cur[0]
        qw = at("qw", [P, 2, 2, P], F32, sq_at)
        hmt = at("hmt", [P, 2, 2, P], F32, sb_at + 2560)
        ha = at("ha", [P, KC, N], F32, r2)
        cur[0] = r3
        aq = place("aq", [P, KC, N])
        ak = place("ak", [P, KVH, N])
        akc = place("akc", [P, KVH, PAST])
        av = place("av", [P, NT + 1, KVH * HD])
        amax = place("amax", [P, 2])
        asum = place("asum", [P, 2])
        arec = place("arec", [P, 2])
        end_a = cur[0]
        ck2 = at("ck2", [P, KVH, 2, HD], F32, x_at)
        ko = at("ko", [P, KVH * HD], F32, x_at + 2048)
        m_hi = at("m_hi", [P, KC, N], F32R, r3)
        m_lo = at("m_lo", [P, KC, N], F32R, r3 + KC * row)
        assert max(end_m, end_a, r3 + 2 * KC * row, mw_at + (KC + 2) * MOD_W * 4) <= nc.sbuf_usable_end

        ident, ones_d, ones_h, swap = (cst[:, n * P:(n + 1) * P] for n in range(4))
        mask = [cst[:, (4 + d) * P:(5 + d) * P] for d in range(2)]
        cos, sin = cst[:, 6 * P:6 * P + TS], cst[:, 6 * P + TS:6 * P + 2 * TS]
        sel1 = rowc[:, 0:H * P].rearrange("h (g p) -> h g p", g=H)
        sel2 = rowc[:, H * P:H * P + 4 * P].rearrange("h (j p) -> h j p", j=4)
        one_row = rowc[:, H * P + 4 * P:R_N]

        psum = ctx.enter_context(nc.psum_tensor("psum", [P, 8, 512], F32))

        def half_out(slot, h):
            return psum[:, 2 * slot + h, 0:HALF]

        def both(slot):
            return psum[:, 2 * slot:2 * slot + 2, 0:HALF]

        def flat(slot):
            return psum[:, 2 * slot:2 * slot + 2, :].rearrange("p b n -> p (b n)")

        def halves(t):
            return t.rearrange("p (h n) -> p h n", h=2)

        def mod_out(n, bank=7):
            return psum[:, bank, n:n + P]

        ld_small, ld_row, ld_x = sem("ld_small"), sem("ld_row"), [sem(f"ld_x{c}") for c in range(NT)]
        raw_in = [sem(f"raw_in{s}") for s in range(RAWS)]
        raw_free = sem("raw_free")
        w_hi = sem("w_hi")
        tile_done = sem("tile_done")
        ev = [sem("ev0"), sem("ev1")]
        mod0_in = [sem(f"mod0_in{s}") for s in range(MOD_FIRST)]
        mod_in = [sem(f"mod_in{s}") for s in range(3)]
        mod0_mul, mod0_ev = sem("mod0_mul"), sem("mod0_ev")
        mod_mul, mod_done, mod_ev = sem("mod_mul"), sem("mod_done"), sem("mod_ev")
        mod_ready = sem("mod_ready")
        vec_t, v_ready, silc_ready = sem("vec_t"), sem("v_ready"), sem("silc_ready")
        post_ready, y_in = sem("post_ready"), sem("y_in")
        ysq_in, sq_sum, ystat_mm = sem("ysq_in"), sem("sq_sum"), sem("ystat_mm")
        x_t, x_ev = sem("x_t"), [sem("x_ev0"), sem("x_ev1")]
        sq_in, stat_mm = sem("sq_in"), sem("stat_mm")
        rb_ln, rb_ready = sem("rb_ln"), sem("rb_ready")
        pre_t, pre_h, pre_hi, h_rdy = sem("pre_t"), sem("pre_h"), sem("pre_hi"), sem("h_rdy")
        post_t, x_upd = sem("post_t"), sem("x_upd")
        g_hi_s, g_lo_s = sem("g_hi_s"), sem("g_lo_s")
        x_spill, x_back = sem("x_spill"), sem("x_back")
        tr_done, tr_ev = sem("tr_done"), sem("tr_ev")
        row_d, row_a, tok_t, tok_ev = sem("row_d"), sem("row_a"), sem("tok_t"), sem("tok_ev")
        st_in, kw_in, kv_done, st_upd = sem("st_in"), sem("kw_in"), sem("kv_done"), sem("st_upd")
        front, e_min, e_exp, qw_in, s_in = (sem(n) for n in ("front", "e_min", "e_exp", "qw_in", "s_in"))
        nums, den_s, hm_in, ss_in, hm_sc, hm_t, hm_ev = (
            sem(n) for n in ("nums", "den_s", "hm_in", "ss_in", "hm_sc", "hm_t", "hm_ev"))
        ones_v, eps_in, dv = sem("ones_v"), sem("eps_in"), sem("dv")
        qk_st, qk_rb, qk_rs = sem("qk_st"), sem("qk_rb"), sem("qk_rs")
        rope, rope_out, rope_c, y_sum = sem("rope"), sem("rope_out"), sem("rope_c"), sem("y_sum")
        ck_in, ck_t, ck_ev = sem("ck_in"), sem("ck_t"), sem("ck_ev")
        sc, nmx, aexp, rcp, p_nrm, atr, pta, ptb, pv, ha_ev = (sem(n) for n in (
            "sc", "nmx", "aexp", "rcp", "p_nrm", "atr", "pta", "ptb", "pv", "ha_ev"))
        mg, mg_hi, mg_lo = sem("mg"), sem("mg_hi"), sem("mg_lo")
        hah, hal, yh, yl = sem("hah"), sem("hal"), sem("yh"), sem("yl")
        ot, oe, out_st, misc_st = sem("ot"), sem("oe"), sem("out_st"), sem("misc_st")

        block = ctx.enter_context(nc.Block())

        @block.sync
        def _(sp):
            def load(t, src, nk=KC):
                sp.wait_ge(raw_free, t.n + 1)
                sp.dma_start(raw[t.raw][:, 0:nk, :].rearrange("p k c -> p (k c)"), src).then_inc(raw_in[t.raw], 16)

            def load_mod(n, part):
                lo, hi = MOD_K[part]
                if not (isinstance(n, int) and n == 0):
                    sp.wait_ge(mod_mul, 2 * (KC * (n - 1) + hi))
                src = pick(a["w_mod"][:, :, lo * MOD_W:hi * MOD_W], MOD_FIRST + n)
                sp.dma_start(mw[:, lo:hi, :].rearrange("p k c -> p (k c)"), src).then_inc(mod_in[part], 16)

            def pick(tiles, n):
                if isinstance(n, int):
                    return tiles[n]
                return tiles[bass.ds(n, 1)].rearrange("o p c -> p (o c)")

            sp.dma_start(vrow[:, :], a["vec_rows"][0:P]).then_inc(ld_small, 16)
            sp.dma_start(vrow2[:, :], a["vec_rows"][P:V_N]).then_inc(ld_small, 16)
            sp.dma_start(cst[:, :], a["cst"]).then_inc(ld_small, 16)
            for c in range(NT):
                src = a["x_prompt"][0] if c == 0 else a["x_sample"][0, (c - 1) * P:c * P]
                sp.dma_start(xtok[:, c, :], src).then_inc(ld_x[c], 16)
            for s in range(MOD_FIRST):
                sp.dma_start(mw0[s][:, :, :].rearrange("p k c -> p (k c)"), a["w_mod"][s]).then_inc(mod0_in[s], 16)
            for t in range(RAWS):
                load(Tile(t), a["w_ffn_in"][t])
            for src, dst in ((a["rowc"], rowc[:, :]), (a["gate_bias"], gbias[:, :]), (a["m0"], m0[:, :])):
                sp.dma_start(dst, src).then_inc(ld_row, 16)
            sp.wait_ge(mod_done, 1)

            def ffn(f, base):
                it = 0
                j0 = 0
                for p, nj in enumerate(PHASES):

                    def ahead(n, u):
                        if u == 0 and not (isinstance(n, int) and n in (0, MOD_LATER - 2)):
                            load_mod(n - 1, 2)
                        elif u >= 2:
                            load_mod(n, u - 2)

                    def load_in(i):
                        for u in range(4):
                            if not (isinstance(i, int) and f == 0 and p == 0 and i == 0):
                                load(Tile(base + u, i), pick(a["w_ffn_in"], f * 2 * NJ + 2 * j0 + 4 * i + u))
                            if f == 0 and p < 2:
                                ahead(it + i, u)

                    def load_out(i):
                        for u in range(4):
                            src = a["w_ffn_out"][:, :, j0 * P:(j0 + nj) * P]
                            load(Tile(base + u, i), pick(src, f * KC + 4 * i + u), nj)
                            if f == 0:
                                ahead(it + i, u)

                    if f == 0 and p == 0:
                        load_in(0)
                        with sp.Fori(0, nj // 2 - 1) as i:
                            load_in(i + 1)
                    else:
                        with sp.Fori(0, nj // 2) as i:
                            load_in(i)
                    if p < 2:
                        it += nj // 2
                    base += 2 * nj
                    if f == 0 and p == 2:
                        load_out(0)
                        load_out(1)
                    else:
                        with sp.Fori(0, 2) as i:
                            load_out(i)
                    it += 2
                    base += KC
                    j0 += nj
                    if f == 0 and p > 0:
                        load_mod(it - 1, 2)

            ffn(0, 0)

            def mix(lo, hi):
                for l in range(lo, hi):
                    load(Tile(T_MIX + l), a["w_mix"][l])

            mix(L_GATE, RAWS)
            sp.wait_ge(x_upd, KC)
            sp.dma_start(a["x_keep"], x[:, :, :].rearrange("p k n -> p (k n)")).then_inc(x_spill, 16)
            for d in range(2):
                c = (0, NT - 2)[d]
                sp.dma_start(cs[:, d, c, :, 0:DV],
                             a["state_C"][0, 0, d].rearrange("(j g) k v -> (g k) j v", g=2)).then_inc(st_in, 16)
                sp.dma_start(cs[:, d, c, :, DV:DV + 1],
                             a["state_n"][0, 0, d].rearrange("(j g) (k o) -> (g k) j o", g=2, o=1),
                             allow_slow_non_contiguous=True).then_inc(st_in, 16)
            mix(RAWS, L_AQ + 2)
            sp.wait_ge(row_d, ROW_M)
            sp.dma_start(a["o_m"].rearrange("a b d h -> h (a b d)"), mout[:, :],
                         allow_slow_non_contiguous=True).then_inc(misc_st, 16)
            sp.wait_ge(st_upd, 2)
            for d in range(2):
                sp.dma_start(a["o_C"][0, 0, d].rearrange("(j g) k v -> (g k) j v", g=2),
                             cp[:, d, :, 0:DV]).then_inc(misc_st, 16)
                sp.dma_start(a["o_n"][0, 0, d].rearrange("(j g) (k o) -> (g k) j o", g=2, o=1),
                             cp[:, d, :, DV:DV + 1], allow_slow_non_contiguous=True).then_inc(misc_st, 16)
            sp.wait_ge(hm_ev, UNITS)
            sp.wait_ge(misc_st, 16 * 5)
            for r in range(2):
                sp.dma_start(ck2[:, :, r, :], a["cache_k"].rearrange("s (g d) -> s g d", g=KVH)).then_inc(ck_in, 16)
            sp.dma_start(av[:, NT, :], a["cache_v"]).then_inc(ck_in, 16)
            mix(L_AQ + 2, L_MO + 2)
            sp.wait_ge(ck_ev, 2)
            sp.dma_start(a["o_k"], ko[:, :]).then_inc(misc_st, 16)
            sp.wait_ge(tr_ev, 14)
            sp.dma_start(a["o_v"], av[:, 0, :]).then_inc(misc_st, 16)
            sp.wait_ge(misc_st, 16 * 7)
            sp.wait_ge(x_spill, 16)
            sp.dma_start(x[:, :, :].rearrange("p k n -> p (k n)"), a["x_keep"]).then_inc(x_back, 16)
            mix(L_MO + 2, L_END)
            ffn(1, T_FFN1)
            for c in range(NT):
                sp.wait_ge(oe, c + 1)
                dst = a["o_yp"][0] if c == 0 else a["o_ys"][0, (c - 1) * P:c * P]
                sp.dma_start(dst, otok[c % 2][:, :]).then_inc(out_st, 16)
                if c < NT - 1:
                    sp.wait_ge(out_st, 16 * (c + 1))
            sp.wait_ge(out_st, 16 * NT)

        @block.tensor
        def _(pe):
            mm, tp = pe.matmul, pe.transpose

            def project(t, nk, hi, lo, ready=None, first=0):
                pe.wait_ge(raw_free, t.n + 1 + RAWS)
                pe.wait_ge(ev[t.slot], t.pair)
                for k in range(nk):
                    if ready is not None:
                        pe.wait_ge(ready, first + k + 1)
                    for h in range(2):
                        cols = slice(h * HALF, (h + 1) * HALF)
                        out = half_out(t.slot, h)
                        mm(out, whi[t.slot][:, k, :], hi[:, k, cols], start=(k == 0), stop=False)
                        mm(out, whi[t.slot][:, k, :], lo[:, k, cols], start=False, stop=False)
                        last = mm(out, wlo[t.slot][:, k, :], hi[:, k, cols], start=False, stop=(k == nk - 1))
                last.then_inc(tile_done, 1)

            def project_two(t0, t1, ready, first):
                for t in (t0, t1):
                    pe.wait_ge(raw_free, t.n + 1 + RAWS)
                    pe.wait_ge(ev[t.slot], t.pair)
                for step in range(KC + LAG):
                    if step < KC:
                        pe.wait_ge(ready, first + step + 1)
                    for t, k in ((t0, step), (t1, step - LAG)):
                        if not 0 <= k < KC:
                            continue
                        for h in range(2):
                            cols = slice(h * HALF, (h + 1) * HALF)
                            out = half_out(t.slot, h)
                            mm(out, whi[t.slot][:, k, :], h_hi[:, k, cols], start=(k == 0), stop=False)
                            mm(out, whi[t.slot][:, k, :], h_lo[:, k, cols], start=False, stop=False)
                            last = mm(out, wlo[t.slot][:, k, :], h_hi[:, k, cols], start=False, stop=(k == KC - 1))
                        if k == KC - 1:
                            last.then_inc(tile_done, 1)

            def modulate(s):
                pe.wait_ge(mod0_in[s], 16)
                for t in range(MOD_T):
                    out = mod_out(2 * (MOD_T * s + t)).rearrange("p (o g) -> p o g", g=2)
                    for k in range(KC):
                        both_c = silc[:, :, k].rearrange("p (o g) -> p o g", o=1).broadcast_to([P, P // 2, 2])
                        last = mm(out, mw0[s][:, k, t * P:(t + 1) * P], both_c, start=(k == 0), stop=(k == KC - 1))
                return last

            def sum_mod(n):
                pe.wait_ge(mod_mul, 2 * KC * (n + 1))
                pe.wait_ge(mod_ev, n + 1)
                sum_products(7).then_inc(mod_done, 1)

            def sum_products(bank):
                for t in range(MOD_T):
                    for g in range(2):
                        last = mm(mod_out(2 * t + g, bank), macc[:, g, t * P:(t + 1) * P], ones_d, start=True, stop=True)
                return last

            def stats_y(n):
                for part, src in enumerate((rb, sq[(KC - 1) % 2])):
                    if part == 0:
                        pe.wait_ge(sq_sum, (KC - 2) * (n + 1))
                    else:
                        pe.wait_ge(ysq_in, KC * (n + 1))
                    for h in range(2):
                        last = mm(half_out(2, h), ones_d, src[:, h * HALF:(h + 1) * HALF],
                                  start=(part == 0), stop=(part == 1))
                last.then_inc(ystat_mm, 1)

            def stats(n):
                for k in range(KC):
                    pe.wait_ge(sq_in, 8 * n + k + 1)
                    for h in range(2):
                        last = mm(half_out(2, h), ones_d, sq[k % 2][:, h * HALF:(h + 1) * HALF],
                                  start=(k == 0), stop=(k == KC - 1))
                    last.then_inc(stat_mm, 1)

            pe.sem_inc(tile_done, 2)
            pe.wait_ge(ld_small, 48)
            tp(psum[:, 6, 0:P], vrow[:, :], ident)
            tp(psum[:, 6, P:V_N], vrow2[:, :], ident[0:V_N - P, 0:V_N - P]).then_inc(vec_t, 1)
            for c in range(NT):
                pe.wait_ge(ld_x[c], 16)
            for k in range(KC):
                if k >= 2:
                    pe.wait_ge(x_ev[k % 2], k // 2)
                for c in range(NT):
                    last = tp(flat(k % 2)[:, c * P:(c + 1) * P], xtok[:, c, k * P:(k + 1) * P], ident)
                last.then_inc(x_t, 1)

            def ffn(f, base):
                it, j0 = 0, 0
                for p, nj in enumerate(PHASES):
                    def tiles_in(i, lo=0):
                        for u in range(lo, 4):
                            project(Tile(base + u, i), KC, h_hi, h_lo)
                        if f == 0 and p < 2:
                            sum_mod(it + i)

                    if p == 0:
                        project_two(Tile(base), Tile(base + 1), h_rdy, 16 * f)
                        tiles_in(0, 2)
                        with pe.Fori(0, nj // 2 - 1) as i:
                            tiles_in(i + 1)
                    else:
                        with pe.Fori(0, nj // 2) as i:
                            tiles_in(i)
                    if p < 2:
                        it += nj // 2
                    base += 2 * nj
                    with pe.Fori(0, 2) as i:
                        for u in range(4):
                            project(Tile(base + u, i), nj, g_hi, g_lo, g_lo_s if u == 0 else None, NJ * f + j0)
                        if f == 0:
                            sum_mod(it + i)
                    it += 2
                    base += KC
                    j0 += nj

            stats(0)
            pe.wait_ge(silc_ready, 1)
            for s in range(MOD_FIRST):
                if s != MOD_DVE:
                    modulate(s)
            pe.wait_ge(mod0_mul, 2 * KC)
            sum_products(6).then_inc(mod_done, 1)
            ffn(0, 0)
            stats_y(0)
            stats(1)

            def gemm(l, hi=h_hi, lo=h_lo, ready=None, first=0):
                project(Tile(T_MIX + l), KC, hi, lo, ready, first)

            def turn(jb):
                l = L_MK + jb if jb < 12 else L_AV + jb - 12
                t = Tile(T_MIX + l)
                pe.wait_ge(ev[t.slot], t.pair + 1)
                if jb >= 2:
                    pe.wait_ge(tr_ev, jb - 1)
                src = mk[:, jb, :] if jb < 4 else sa[jb % 2][:, :]
                for c in range(NT):
                    last = tp(flat(2 + jb % 2)[:, c * P:(c + 1) * P], src[:, c * P:(c + 1) * P], ident)
                last.then_inc(tr_done, 1)

            project_two(Tile(T_MIX), Tile(T_MIX + 1), h_rdy, KC)
            for l in range(2, L_AQ):
                gemm(l)
                if l > L_MK:
                    turn(l - L_MK - 1)
            turn(11)

            pe.wait_ge(row_a, 6)
            pe.wait_ge(row_d, ROW_END)
            pe.wait_ge(tr_ev, 12)
            for q, src in enumerate((gi, gf, gm)):
                for c in range(NT):
                    for d in range(2):
                        o = ((q * NT + c) * 2 + d) * H
                        last = tp(psum[:, 4, o:o + H], src[:, d, c * P:(c + 1) * P], ident[0:H, 0:H])
            last.then_inc(tok_t, 1)
            for j in range(4):
                last = mm(psum[:, 5, j * 2 * NT:(j + 1) * 2 * NT], sel2[:, j, :],
                          ar[:, :, :].rearrange("h d c -> h (d c)"), start=True, stop=True)
            last.then_inc(tok_t, 1)

            for s, (d, c) in enumerate(STATES):
                pe.wait_ge(kw_in, s + 1)
                pe.wait_ge(ones_v, 1)
                if s >= 2:
                    pe.wait_ge(st_upd, s - 1)
                for g in range(H):
                    j, hh = g // 2, g % 2
                    last = mm(psum[hh * DK:(hh + 1) * DK, 2 * (s % 2) + j // 2, (j % 2) * (DV + 1):(j % 2 + 1) * (DV + 1)],
                              sa[s % 2][:, g * DK:(g + 1) * DK], vt[:, c, g, :], start=True, stop=True)
                last.then_inc(kv_done, 1)

            def front_of(n):
                c, j = n // 4, n % 4
                tok = slice(c * P, (c + 1) * P)
                if n == 0:
                    pe.wait_ge(tok_ev, 2)
                else:
                    pe.wait_ge(s_in, n)
                bc = psum[:, 4, :].rearrange("p (d g t) -> p d g t", d=2, g=2)
                for hh in range(2):
                    mm(bc[:, :, hh, :], sel1[:, 2 * j + hh, :], nm[:, :, tok], start=True, stop=True)
                if c > 0:
                    mm(psum[:, 5, P:3 * P].rearrange("p (d t) -> p d t", d=2), sel2[:, j, :], t1[:, :, tok],
                       start=True, stop=True)
                for hh in range(2):
                    half = slice(hh * DK, (hh + 1) * DK)
                    last = mm(psum[:, 5 + hh, 0:P], mk[half, j, tok], mq[half, j, tok], start=True, stop=True)
                last.then_inc(front, 1)

            def nums_of(n):
                c, j = n // 4, n % 4
                pe.wait_ge(s_in, n + 1)
                if n >= 2:
                    pe.wait_ge(hm_in, n - 1)
                else:
                    pe.wait_ge(st_upd, len(STATES))
                for hh in range(2):
                    half = slice(hh * DK, (hh + 1) * DK)
                    for d in range(2):
                        out = psum[:, 2 * (n % 2) + hh, d * (DV + 1):(d + 1) * (DV + 1)]
                        last = mm(out, sa[n % 2][:, (2 * d + hh) * P:(2 * d + hh + 1) * P], vt[:, c, 2 * j + hh, :],
                                  start=True, stop=(c == 0))
                        if c > 0:
                            last = mm(out, qw[half, n % 2, d, :], cs[half, d, c - 1, j, :], start=False, stop=True)
                last.then_inc(nums, 1)

            def turn_hm(n):
                pe.wait_ge(hm_sc, n + 1)
                if n >= 1:
                    pe.wait_ge(hm_ev, n)
                for hh in range(2):
                    last = tp(psum[:, 7, hh * P:(hh + 1) * P], hmt[:, n % 2, hh, :], ident)
                last.then_inc(hm_t, 1)

            front_of(0)
            for n in range(UNITS):
                if n + 1 < UNITS:
                    front_of(n + 1)
                nums_of(n)
                if n >= 2:
                    turn_hm(n - 2)
            turn_hm(UNITS - 2)
            turn_hm(UNITS - 1)

            def qk_stats(e):
                t = Tile(T_MIX + L_AQ + e)
                dst = aq[:, e, :] if e < KC else ak[:, e - KC, :]
                pe.wait_ge(ev[t.slot], t.pair + 1)
                if e >= 1:
                    pe.wait_ge(qk_rb, e)
                    pe.wait_ge(rope, e)
                for h in range(2):
                    mm(half_out(2, h), ones_h, sq[e % 2][:, h * HALF:(h + 1) * HALF], start=True, stop=True)
                mm(psum[:, 6, :], swap, dst[:, TP:N], start=True, stop=True).then_inc(qk_st, 1)

            for e in range(14):
                gemm(L_AQ + e)
                if 1 <= e <= 12:
                    qk_stats(e - 1)
            pe.wait_ge(rope, 12)
            pe.wait_ge(qk_rb, 12)
            turn(12)
            turn(13)
            pe.wait_ge(ck_in, 48)
            pe.wait_ge(tr_ev, 14)
            for g in range(KVH):
                last = tp(psum[:, 4, g * PAST:(g + 1) * PAST], ck2[:, g, :, :].rearrange("s r d -> s (r d)"), ident)
            last.then_inc(ck_t, 1)
            pe.wait_ge(rope_out, 12)
            for g in range(KVH):
                last = tp(psum[:, 5, g * HD:(g + 1) * HD], ak[0:HD, g, 0:P], ident[0:HD, 0:HD])
            last.then_inc(ck_t, 1)

            def scores(k):
                c, m, s = k // AH, k % AH // 2, k % 2
                half = slice(s * HD, (s + 1) * HD)
                if k >= 2:
                    pe.wait_ge(aexp, k - 1)
                else:
                    pe.wait_ge(ck_ev, 2)
                q = aq[half, m, c * P:(c + 1) * P]
                if c == 0:
                    last = mm(psum[:, 4 * s, 0:P], q, ak[half, m // 2, 0:TP], start=True, stop=True)
                else:
                    mm(psum[:, 4 * s, :], q, ak[half, m // 2, TP:N], start=True, stop=True)
                    last = mm(psum[:, 4 * s + 1, 0:PAST], q, akc[half, m // 2, :], start=True, stop=True)
                last.then_inc(sc, 1)

            def turn_p(k):
                c, s = k // AH, k % 2
                pe.wait_ge(p_nrm, k + 1)
                if k >= 2:
                    pe.wait_ge(ha_ev, k - 1)
                for b in range(1 if c == 0 else NT):
                    last = tp(flat(2 * s + 1)[:, b * P:(b + 1) * P], sa[s][:, b * P:(b + 1) * P], ident)
                last.then_inc(atr, 1)

            def values(k):
                c, m, s = k // AH, k % AH // 2, k % 2
                pe.wait_ge(pta, k + 1)
                if c > 0:
                    pe.wait_ge(ptb, k + 1 - AH)
                tiles = [0] if c == 0 else list(range(1, NT + 1))
                for b, v in enumerate(tiles):
                    last = mm(psum[s * HD:(s + 1) * HD, 4 * s + 3, 2 * P:3 * P],
                              av[:, v, (m // 2) * HD:(m // 2 + 1) * HD], sb[s][:, b * P:(b + 1) * P],
                              start=(b == 0), stop=(b == len(tiles) - 1))
                last.then_inc(pv, 1)

            scores(0)
            for k in range(HEADS):
                if k + 1 < HEADS:
                    scores(k + 1)
                if k >= 1:
                    values(k - 1)
                turn_p(k)
            values(HEADS - 1)

            for l in range(L_MO, L_BM):
                if l == L_MO:
                    pe.wait_ge(ha_ev, HEADS)
                gemm(l)
            for m in range(KC):
                gemm(L_BM + 2 * m)
                gemm(L_BM + 2 * m + 1, m_hi, m_lo, mg_lo if m == 0 else None)
            for m in range(KC):
                gemm(L_BA + 2 * m)
                gemm(L_BA + 2 * m + 1, m_hi, m_lo, hal if m == 0 else None)
            for m in range(KC):
                gemm(L_OUT + m, h_hi, h_lo, yl if m == 0 else None)
            stats_y(1)
            stats(2)
            ffn(1, T_FFN1)
            stats_y(2)
            for c in range(NT):
                if c >= 2:
                    pe.wait_ge(oe, c - 1)
                else:
                    pe.wait_ge(x_upd, 3 * KC)
                for k in range(KC):
                    last = tp(flat(c % 2)[:, k * P:(k + 1) * P], x[:, k, c * P:(c + 1) * P], ident)
                last.then_inc(ot, 1)

        @block.scalar
        def _(act):
            fn, copy = act.activation, act.copy

            def split(t):
                act.wait_ge(raw_in[t.raw], 16 * (t.quad + 1))
                act.wait_ge(tile_done, t.n + 1)
                copy(whi[t.slot][:, :, :], raw[t.raw][:, :, :]).then_inc(w_hi, 1)

            def done(t):
                act.wait_ge(tile_done, t.n + 3)

            def inv_root(n):
                fn(halves(rb[:, :]), both(2), ACT.Ln, bias=epsc[:, 0:1]).then_inc(rb_ln, 1)
                act.wait_ge(rb_ln, n + 1)
                fn(rb[:, :], rb[:, :], ACT.Exp, scale=-0.5).then_inc(rb_ready, 1)

            def stats(n, ready):
                for k in range(KC):
                    ready(k)
                    if k >= 2:
                        act.wait_ge(stat_mm, 8 * n + k - 1)
                    fn(sq[k % 2][:, :], x[:, k, :], ACT.Square).then_inc(sq_in, 1)
                act.wait_ge(stat_mm, 8 * n + KC)
                inv_root(2 * n)

            def square_y(l, m, t):
                act.wait_ge(ev[t.slot], t.pair + 1)
                if m >= 2:
                    act.wait_ge(sq_sum, (KC - 2) * l + max(m - 2, 1))
                else:
                    act.wait_ge(stat_mm, KC * (l + 1))
                fn(sq[m % 2][:, :], y[:, m, :], ACT.Square).then_inc(ysq_in, 1)
                act.wait_ge(ysq_in, KC * l + m + 1)
                for g, cols in GROUPS:
                    last = fn(y[:, m, cols], y[:, m, cols], ACT.Copy, scale=post_s[:, l, m, g:g + 1])
                last.then_inc(y_in, 1)

            def root_y(l):
                act.wait_ge(ystat_mm, l + 1)
                inv_root(2 * l + 1)

            def normed(l):
                for k in range(KC):
                    act.wait_ge(pre_t, 8 * l + k + 1)
                    if k >= 2:
                        act.wait_ge(h_rdy, 8 * l + k - 1)
                    for g, cols in GROUPS:
                        last = fn(sb[k % 2][:, cols], sa[k % 2][:, cols], ACT.Identity,
                                  bias=mod[:, 3 * l * KC + k, g:g + 1], scale=pre_s[:, l, k, g:g + 1])
                    last.then_inc(pre_h, 1)
                    act.wait_ge(pre_h, 8 * l + k + 1)
                    copy(h_hi[:, k, :], sb[k % 2][:, :]).then_inc(pre_hi, 1)

            act.wait_ge(v_ready, 1)
            fn(silc[:, :, :], vT[:, V_CC:V_QG].rearrange("p (g k) -> p g k", g=2), ACT.Silu).then_inc(silc_ready, 1)
            for k in range(0, KC, 2):
                act.wait_ge(x_t, k + 1)
                copy(x[:, k, :], flat(0)[:, 0:N]).then_inc(x_ev[0], 1)
            act.wait_ge(eps_in, 2)
            act.preload_act_table_set(LN_EXP)
            stats(0, lambda k: act.wait_ge(x_ev[k % 2], k // 2 + 1))
            split(Tile(0))
            split(Tile(1))
            act.wait_ge(mod_ready, 1)
            normed(0)

            def ffn(f, base):
                j0 = 0
                for p, nj in enumerate(PHASES):
                    with act.Fori(0, nj // 2) as i:
                        for u in range(4):
                            t = Tile(base + u, i)
                            s = t.c // 2 % 2
                            if u % 2 == 0:
                                done(t)
                                fn(halves(sa[s][:, :]), both(t.slot), ACT.Silu).then_inc(ev[t.slot], 1)
                                split(t.plus(2))
                            else:
                                split(t.plus(2))
                                act.wait_ge(ev[t.slot], t.pair + 1)
                                out = g_hi[:, bass.ds(2 * i + u // 2, 1), :].rearrange("p o n -> p (o n)")
                                copy(out, sb[s][:, :]).then_inc(g_hi_s, 1)
                    base += 2 * nj
                    tail = f == 1 and p == len(PHASES) - 1

                    def outs(t, m):
                        done(t)
                        if p == 0:
                            dst = y[:, bass.ds(m, 1), :].rearrange("p o (h n) -> p (o h) n", h=2)
                            copy(dst, both(t.slot)).then_inc(ev[t.slot], 1)
                    if p == len(PHASES) - 1:
                        act.preload_act_table_set(LN_EXP)
                        act.wait_ge(post_ready, 2 * f + 1)
                        for u in range(KC):
                            if not (tail and u >= KC - 2):
                                split(Tile(base + u + 2))
                            square_y(2 * f, u, Tile(base + u))
                    else:
                        with act.Fori(0, 2) as i:
                            for u in range(4):
                                t = Tile(base + u, i)
                                outs(t, 4 * i + u)
                                split(t.plus(2))
                    base += KC
                    j0 += nj

            ffn(0, 0)
            root_y(0)
            stats(1, lambda k: act.wait_ge(x_upd, k + 1))
            act.wait_ge(mod_ready, 2)
            normed(1)

            for l in range(L_AQ):
                t = Tile(T_MIX + l)
                done(t)
                if l == L_GATE:
                    act.wait_ge(ld_row, 48)
                    for q, dst in enumerate((gi, gf, gi, gf)):
                        last = fn(halves(dst[:, q // 2, :]), psum[32 * q:32 * q + H, 2 * t.slot:2 * t.slot + 2, 0:HALF],
                                  ACT.Identity, bias=gbias[:, q:q + 1])
                elif l < L_MK:
                    last = fn(halves(mq[:, l - L_MQ, :]), both(t.slot), ACT.Copy, scale=DK ** -0.5)
                elif l < L_MV:
                    last = copy(halves(mk[:, l - L_MK, :]), both(t.slot))
                else:
                    jb = 4 + l - L_MV
                    if jb >= 6:
                        act.wait_ge(tr_done, jb - 1)
                    last = copy(halves(sa[jb % 2][:, :]), both(t.slot))
                last.then_inc(ev[t.slot], 1)
                split(t.plus(2))

            act.preload_act_table_set(LN_EXP)
            act.wait_ge(row_d, 1)
            fn(t1[:, :, :], t1[:, :, :], ACT.Exp, scale=-1.0).then_inc(row_a, 1)
            act.wait_ge(row_a, 1)
            fn(t1[:, :, :], t1[:, :, :], ACT.Ln, bias=epsc[0:H, 1:2]).then_inc(row_a, 1)
            act.wait_ge(row_d, ROW_END)
            fn(ar[:, :, :], ar[:, :, :], ACT.Exp).then_inc(row_a, 1)
            fn(t1[:, :, :], t1[:, :, :], ACT.Exp).then_inc(row_a, 1)
            fn(gf[:, :, :], gf[:, :, :], ACT.Exp).then_inc(row_a, 1)
            fn(gm[:, :, :], gm[:, :, :], ACT.Exp, scale=-1.0).then_inc(row_a, 1)

            def squares(n):
                act.wait_ge(hm_in, n + 1)
                for hh in range(2):
                    last = fn(sq[1][:, (2 * (n % 2) + hh) * P:(2 * (n % 2) + hh + 1) * P], hmt[:, n % 2, hh, :], ACT.Square, accum_out=ss[:, n % 2, hh:hh + 1])
                last.then_inc(ss_in, 1)
                act.wait_ge(ss_in, 3 * n + 1)
                fn(ss[:, n % 2, :], ss[:, n % 2, :], ACT.Ln, bias=epsc[:, 0:1], scale=1.0 / DV).then_inc(ss_in, 1)
                act.wait_ge(ss_in, 3 * n + 2)
                fn(ss[:, n % 2, :], ss[:, n % 2, :], ACT.Exp, scale=-0.5).then_inc(ss_in, 1)

            def store_hm(n):
                c, j = n // 4, n % 4
                act.wait_ge(hm_t, n + 1)
                for hh in range(2):
                    g = 2 * j + hh
                    last = fn(hm[:, g, c * P:(c + 1) * P], psum[:, 7, hh * P:(hh + 1) * P], ACT.Copy,
                              scale=vT[:, V_MN + g:V_MN + g + 1])
                last.then_inc(hm_ev, 1)

            for n in range(UNITS):
                act.wait_ge(e_min, n + 1)
                fn(sa[n % 2][:, 0:4 * P], sa[n % 2][:, 0:4 * P], ACT.Exp).then_inc(e_exp, 1)
                if n >= 3:
                    store_hm(n - 3)
                if n >= 1:
                    squares(n - 1)
            squares(UNITS - 1)
            for n in range(UNITS - 3, UNITS):
                store_hm(n)

            def inv_rms(e):
                act.wait_ge(qk_st, e + 1)
                if e >= 1:
                    act.wait_ge(rope_out, e)
                fn(halves(rb[:, :]), both(2), ACT.Ln, bias=epsc[:, 0:1]).then_inc(qk_rb, 1)
                act.wait_ge(qk_rb, e + 1)
                fn(rb[:, :], rb[:, :], ACT.Exp, scale=-0.5).then_inc(qk_rs, 1)

            for e in range(14):
                t = Tile(T_MIX + L_AQ + e)
                done(t)
                if e < 12:
                    dst, gain = (aq[:, e, :], V_QG) if e < KC else (ak[:, e - KC, :], V_KG)
                    fn(halves(dst), both(t.slot), ACT.Copy, scale=vT[:, gain:gain + 1])
                    if e >= 2:
                        act.wait_ge(qk_st, e - 1)
                    last = fn(halves(sq[e % 2][:, :]), both(t.slot), ACT.Square)
                else:
                    last = copy(halves(sa[e % 2][:, :]), both(t.slot))
                last.then_inc(ev[t.slot], 1)
                split(t.plus(2))
                if 1 <= e <= 12:
                    inv_rms(e - 1)

            def take_p(k):
                c, s = k // AH, k % 2
                act.wait_ge(atr, k + 1)
                if k >= 2:
                    act.wait_ge(pv, k - 1)
                w = P if c == 0 else 4 * P
                copy(sb[s][:, 0:w], flat(2 * s + 1)[:, 0:w]).then_inc(pta, 1)

            def store_ha(k):
                c, m, s = k // AH, k % AH // 2, k % 2
                half = slice(s * HD, (s + 1) * HD)
                act.wait_ge(pv, k + 1)
                copy(ha[half, m, c * P:(c + 1) * P], psum[half, 4 * s + 3, 2 * P:3 * P]).then_inc(ha_ev, 1)

            for k in range(HEADS):
                c, s = k // AH, k % 2
                act.wait_ge(nmx, 2 * k + 2)
                if k >= 2:
                    act.wait_ge(atr, k - 1)
                w = P if c == 0 else N
                fn(sa[s][:, 0:w], flat(2 * s)[:, 0:w], ACT.Exp, bias=amax[:, s:s + 1], scale=HD ** -0.5,
                   accum_out=asum[:, s:s + 1]).then_inc(aexp, 1)
                if k >= 1:
                    take_p(k - 1)
                if k >= 2:
                    store_ha(k - 2)
            take_p(HEADS - 1)
            store_ha(HEADS - 2)
            store_ha(HEADS - 1)

            def high(k, dst, src, ready, count, out):
                act.wait_ge(ready, count)
                copy(dst[:, k, :], src).then_inc(out, 1)

            for l in range(L_MO, L_END):
                t = Tile(T_MIX + l)
                done(t)
                if l < L_BM:
                    m = l - L_MO
                    if m >= 2:
                        act.wait_ge(mg, m - 1)
                    fn(halves(sa[m % 2][:, :]), both(t.slot), ACT.Sigmoid).then_inc(ev[t.slot], 1)
                elif l < L_OUT:
                    m, gate = (l - L_BM) % 16 // 2, (l - L_BM) % 2 == 0
                    if gate:
                        if m >= 2:
                            v = t.plus(-3)
                            act.wait_ge(ev[v.slot], v.pair + 1)
                        fn(halves(sa[m % 2][:, :]), both(t.slot), ACT.Sigmoid).then_inc(ev[t.slot], 1)
                else:
                    m = l - L_OUT
                    act.wait_ge(yl, m + 1)
                    copy(halves(y[:, m, :]), both(t.slot)).then_inc(ev[t.slot], 1)
                split(t.plus(2))
                if l >= L_OUT:
                    act.wait_ge(post_ready, 2)
                    square_y(1, m, t)
                if L_MO < l <= L_BM:
                    m = l - 1 - L_MO
                    high(m, m_hi, sb[m % 2][:, :], mg, m + 1, mg_hi)
                if l == L_BA - 1:
                    for k in range(KC):
                        high(k, m_hi, ha[:, k, :], ha_ev, HEADS, hah)
                if l == L_OUT - 2:
                    act.preload_act_table_set(LN_EXP)
                    for k in range(KC - 1):
                        high(k, h_hi, y[:, k, :], y_sum, k + 1, yh)
                if l == L_OUT - 1:
                    high(KC - 1, h_hi, y[:, KC - 1, :], y_sum, KC, yh)

            root_y(1)
            stats(2, lambda k: act.wait_ge(x_upd, KC + k + 1))
            normed(2)
            ffn(1, T_FFN1)
            root_y(2)
            for c in range(NT):
                act.wait_ge(ot, c + 1)
                if c >= 2:
                    act.wait_ge(out_st, 16 * (c - 1))
                copy(otok[c % 2][:, :], flat(c % 2)).then_inc(oe, 1)

        @block.vector
        def _(dve):
            tt, ts, stt, copy = dve.tensor_tensor, dve.tensor_scalar, dve.scalar_tensor_tensor, dve.tensor_copy
            steps = [0]

            def step(ins):
                steps[0] += 1
                ins.then_inc(dv, 1)
                dve.wait_ge(dv, steps[0])

            def split(t):
                dve.wait_ge(w_hi, t.n + 1)
                tt(wlo[t.slot][:, :, :], raw[t.raw][:, :, :], whi[t.slot][:, :, :].bitcast(F32),
                   ALU.subtract).then_inc(raw_free, 1)

            def done(t):
                dve.wait_ge(tile_done, t.n + 3)

            def inverse(n):
                dve.wait_ge(rb_ready, n + 1)

            def normed(l):
                def low(k):
                    dve.wait_ge(pre_hi, 8 * l + k + 1)
                    tt(h_lo[:, k, :], sb[k % 2][:, :], h_hi[:, k, :].bitcast(F32), ALU.subtract).then_inc(h_rdy, 1)
                for k in range(KC):
                    if k >= 2:
                        dve.wait_ge(pre_h, 8 * l + k - 1)
                    tt(sa[k % 2][:, :], x[:, k, :], rb[:, :], ALU.mult).then_inc(pre_t, 1)
                    if k >= 1:
                        low(k - 1)
                low(KC - 1)

            def add_square(l, m):
                dve.wait_ge(ysq_in, KC * l + m + 1)
                if m == 1:
                    tt(rb[:, :], sq[0][:, :], sq[1][:, :], ALU.add).then_inc(sq_sum, 1)
                elif m >= 2:
                    dve.wait_ge(sq_sum, (KC - 2) * l + m - 1)
                    tt(rb[:, :], rb[:, :], sq[m % 2][:, :], ALU.add).then_inc(sq_sum, 1)

            def residual(l):
                def add(k):
                    dve.wait_ge(post_t, 8 * l + k + 1)
                    tt(x[:, k, :], x[:, k, :], sa[k % 2][:, :], ALU.add).then_inc(x_upd, 1)
                for k in range(KC):
                    if k >= 2:
                        dve.wait_ge(x_upd, 8 * l + k - 1)
                    dve.wait_ge(y_in, KC * l + k + 1)
                    tt(sa[k % 2][:, :], y[:, k, :], rb[:, :], ALU.mult).then_inc(post_t, 1)
                    if k >= 1:
                        add(k - 1)
                add(KC - 1)

            def per_group(col):
                return vT[:, col:col + KC].rearrange("p (k o) -> p k o", o=1).broadcast_to([P, KC, 2])

            def scales(l, which):
                if which == "pre":
                    step(stt(pre_s[:, l, :, :], mod[:, (3 * l + 1) * KC:(3 * l + 2) * KC, :], 1.0,
                             per_group(V_PRE + l * KC), ALU.add, ALU.mult))
                else:
                    stt(post_s[:, l, :, :], mod[:, (3 * l + 2) * KC:(3 * l + 3) * KC, :], 0.5 if l != 1 else 1.0,
                        per_group(V_POST + l * KC), ALU.mult, ALU.mult).then_inc(post_ready, 1)

            def over_k(w, ks, done_mul, before):
                for k in ks:
                    for g in range(2):
                        acc, by = macc[:, g, :], silc[:, g, k:k + 1]
                        if k == 0:
                            last = ts(acc, w[:, k, :], by, None, ALU.mult)
                        else:
                            dve.wait_ge(done_mul, before + 2 * k + g - 1)
                            last = stt(acc, w[:, k, :], by, acc, ALU.mult, ALU.add)
                        last.then_inc(done_mul, 1)

            def multiply(n, part):
                dve.wait_ge(mod_in[part], 16 * (n + 1))
                over_k(mw, range(*MOD_K[part]), mod_mul, 2 * KC * n)

            def take_mod(n):
                dve.wait_ge(mod_done, n + 2)
                take_sums(MOD_T * (MOD_FIRST + n), 7)

            def take_sums(lo, bank):
                bias = vT[:, bass.ds(lo, MOD_T)].rearrange("p (t o) -> p t o", o=1).broadcast_to([P, MOD_T, 2])
                stt(mod[:, bass.ds(lo, MOD_T), :], mod_out(0, bank)[:, 0:2 * MOD_T].rearrange("p (t g) -> p t g", g=2),
                    float(D), bias, ALU.mult, ALU.add).then_inc(mod_ev, 1)

            dve.sem_inc(raw_free, RAWS)
            dve.memset(epsc[:, 0:1], EPS).then_inc(eps_in, 1)
            dve.memset(epsc[:, 1:2], 1.0).then_inc(eps_in, 1)
            dve.wait_ge(vec_t, 1)
            copy(vT[:, :], psum[:, 6, 0:V_N]).then_inc(v_ready, 1)
            for k in range(1, KC, 2):
                dve.wait_ge(x_t, k + 1)
                copy(x[:, k, :], flat(1)[:, 0:N]).then_inc(x_ev[1], 1)
            dve.wait_ge(v_ready, 1)
            dve.wait_ge(silc_ready, 1)
            dve.wait_ge(mod0_in[MOD_DVE], 16)
            over_k(mw0[MOD_DVE], range(KC), mod0_mul, 0)
            split(Tile(0))
            split(Tile(1))
            dve.wait_ge(mod_done, 1)
            first = 2 * KC
            tt(mod[:, 0:first, :], mod_out(0)[:, 0:2 * first].rearrange("p (t g) -> p t g", g=2),
               vT[:, 0:first].rearrange("p (t o) -> p t o", o=1).broadcast_to([P, first, 2]), ALU.add).then_inc(mod0_ev, 1)
            dve.wait_ge(mod0_ev, 1)
            take_sums(MOD_DVE * MOD_T, 6)
            dve.wait_ge(mod_ev, 1)
            stt(pre_s[:, 0, :, :], mod[:, KC:2 * KC, :], 1.0, per_group(V_PRE), ALU.add, ALU.mult).then_inc(mod_ready, 1)
            inverse(0)
            dve.wait_ge(x_ev[0], 4)
            dve.wait_ge(x_ev[1], 4)
            normed(0)

            def ffn(f, base):
                it = j0 = 0
                for p, nj in enumerate(PHASES):
                    with dve.Fori(0, nj // 2) as i:
                        for u in range(4):
                            t = Tile(base + u, i)
                            s = t.c // 2 % 2 if u % 2 == 0 else t.plus(-1).c // 2 % 2
                            split(t.plus(2))
                            if u % 2:
                                g = t.plus(-1)
                                done(t)
                                dve.wait_ge(ev[g.slot], g.pair + 1)
                                tt(halves(sb[s][:, :]), halves(sa[s][:, :]), both(t.slot), ALU.mult).then_inc(ev[t.slot], 1)
                            if f == 0 and p < 2 and u < 3:
                                multiply(it + i, u)
                            if u % 2:
                                dve.wait_ge(g_hi_s, NJ * f + j0 + 2 * i + u // 2 + 1)
                                jj = bass.ds(2 * i + u // 2, 1)
                                tt(g_lo[:, jj, :].rearrange("p o n -> p (o n)"), sb[s][:, :],
                                   g_hi[:, jj, :].rearrange("p o n -> p (o n)").bitcast(F32),
                                   ALU.subtract).then_inc(g_lo_s, 1)
                        if f == 0 and p < 2:
                            take_mod(it + i)
                    if p < 2:
                        it += nj // 2
                    base += 2 * nj
                    if p > 0:
                        for q in (base - 2 * nj - 1, base - 2 * nj - 2):
                            dve.wait_ge(ev[q % 2], q // 2 + 1)

                    def outs(t, m):
                        if p > 0:
                            done(t)
                            yv = y[:, bass.ds(m, 1), :].rearrange("p o (h n) -> p (o h) n", h=2)
                            tt(yv, yv, both(t.slot), ALU.add).then_inc(ev[t.slot], 1)
                    if p == len(PHASES) - 1:
                        if f == 0:
                            dve.wait_ge(mod_ev, 3)
                            scales(0, "post")
                        for u in range(KC):
                            if f == 0 or u < KC - 2:
                                split(Tile(base + u + 2))
                            outs(Tile(base + u), u)
                            if u >= 1:
                                add_square(2 * f, u - 1)
                            if f == 0:
                                if u % 4 < 3:
                                    multiply(it + u // 4, u % 4)
                                else:
                                    take_mod(it + u // 4)
                    else:
                        with dve.Fori(0, 2) as i:
                            for u in range(4):
                                t = Tile(base + u, i)
                                split(t.plus(2))
                                outs(t, 4 * i + u)
                                if f == 0 and u < 3:
                                    multiply(it + i, u)
                            if f == 0:
                                take_mod(it + i)
                    it += 2
                    base += KC
                    j0 += nj

            ffn(0, 0)
            dve.wait_ge(mod_ev, MOD_LATER + 1)
            scales(1, "post")
            scales(2, "post")
            scales(1, "pre")
            stt(pre_s[:, 2, :, :], mod[:, 7 * KC:8 * KC, :], 1.0, per_group(V_PRE + 2 * KC),
                ALU.add, ALU.mult).then_inc(mod_ready, 1)
            inverse(1)
            residual(0)
            inverse(2)
            dve.wait_ge(x_upd, KC)
            normed(1)

            def take_turned(jb):
                dve.wait_ge(tr_done, jb + 1)
                if jb < 4:
                    dst = mkt[:, :, jb * P:(jb + 1) * P]
                elif jb < 12:
                    dst = vt[:, :, jb - 4, 0:DV]
                else:
                    dst = av[:, 0:NT, (jb - 12) * P:(jb - 11) * P]
                copy(dst, flat(2 + jb % 2)[:, 0:N].rearrange("p (c t) -> p c t", c=NT)).then_inc(tr_ev, 1)

            dve.wait_ge(x_spill, 16)
            for l in range(L_AQ):
                split(Tile(T_MIX + l + 2))
                if l == 0:
                    dve.wait_ge(tile_done, 2 + T_MIX)
                    dve.memset(vt[:, :, :, DV:DV + 1], 1.0).then_inc(ones_v, 1)
                if l > L_MK:
                    take_turned(l - L_MK - 1)
            take_turned(11)

            rows = [0]

            def row_step(ins, wait=True):
                rows[0] += 1
                ins.then_inc(row_d, 1)
                if wait:
                    dve.wait_ge(row_d, rows[0])

            t = Tile(T_MIX)
            dve.wait_ge(ev[t.slot], t.pair + 1)
            row_step(stt(t1[:, :, :], gf[:, :, :], -1.0, gf[:, :, :], ALU.mult, ALU.max))
            dve.wait_ge(row_a, 2)
            row_step(stt(gf[:, :, :], gf[:, :, :], 0.0, t1[:, :, :], ALU.min, ALU.subtract))
            for c in range(NT):
                for d in range(2):
                    seg = slice(c * P, (c + 1) * P) if d == 0 else slice((c + 1) * P - 1, c * P - 1 if c else None, -1)
                    row_step(dve.tensor_tensor_scan(gb[:, d, seg], one_row, gf[:, d, seg], 0.0, ALU.mult, ALU.add), False)
            for d in range(2):
                for g, cols in GROUPS:
                    if d:
                        cols = slice(cols.stop - 1, cols.start - 1 if cols.start else None, -1)
                    row_step(dve.tensor_tensor_scan(gm[:, d, cols], gf[:, d, cols], gi[:, d, cols],
                                                    m0[:, d:d + 1] if g else 0.0, ALU.add, ALU.max), False)
            dve.wait_ge(row_d, rows[0])
            row_step(dve.memset(m_in[:, :, 0:1], 0.0), False)
            row_step(copy(m_in[:, 0, 1:2], m0[:, 0:1]), False)
            row_step(copy(m_in[:, 1, NT - 1:NT], m0[:, 1:2]), False)
            row_step(copy(m_in[:, 0, 2:NT], gm[:, 0, 2 * P - 1:(NT - 1) * P:P]), False)
            row_step(copy(m_in[:, 1, 1:NT - 1], gm[:, 1, 2 * P:(NT - 1) * P + 1:P]), False)
            row_step(copy(mout[:, 0:1], gm[:, 0, TP - 1:TP]), False)
            row_step(copy(mout[:, 1:2], gm[:, 1, 0:1]), False)
            assert rows[0] == ROW_M
            row_step(tt(gi[:, :, :], gi[:, :, :], gb[:, :, :], ALU.subtract), False)
            row_step(tt(nm[:, :, :], gb[:, :, :], gm[:, :, :], ALU.subtract))
            row_step(copy(nml[:, 0, :], nm[:, 0, P - 1:N:P]), False)
            row_step(copy(nml[:, 1, :], nm[:, 1, 0:N:P]))

            def tiles(v):
                return v[:, :, :].rearrange("h d (c t) -> h (d c) t", t=P)

            def spread(v):
                return v[:, :, :].rearrange("h d (c o) -> h (d c) o", o=1).broadcast_to([H, 2 * NT, P])

            row_step(tt(ar[:, :, :], m_in[:, :, :], nml[:, :, :], ALU.add), False)
            row_step(tt(tiles(t1), tiles(nm), spread(m_in), ALU.add), False)
            row_step(tt(tiles(gf), tiles(gi), spread(nml), ALU.add), False)
            assert rows[0] == ROW_END
            dve.wait_ge(tok_t, 2)
            copy(tk[:, :, :, :, :].rearrange("p q c d h -> p (q c d h)"), psum[:, 4, 0:3 * NT * 2 * H]).then_inc(tok_ev, 1)
            copy(ab[:, :, :].rearrange("p j c -> p (j c)"), psum[:, 5, 0:8 * NT]).then_inc(tok_ev, 1)
            dve.wait_ge(tok_ev, 2)

            dve.wait_ge(st_in, 64)
            for s in range(len(STATES) + 1):
                if s < len(STATES):
                    d, c = STATES[s]
                    if s >= 2:
                        dve.wait_ge(kv_done, s - 1)
                    w = tk[:, 1, c, d, :].rearrange("p (h o) -> p h o", o=1).broadcast_to([P, H, DK])
                    tt(sa[s % 2][:, 0:H * DK].rearrange("p (h k) -> p h k", h=H),
                       mkt[:, c, :].rearrange("p (h k) -> p h k", h=H), w, ALU.mult).then_inc(kw_in, 1)
                if s >= 1:
                    d, c = STATES[s - 1]
                    s1 = (s - 1) % 2
                    dve.wait_ge(kv_done, s)
                    if c == 0:
                        for b in range(2):
                            last = copy(cp[:, d, 2 * b:2 * b + 2, :].rearrange("p j v -> p (j v)"),
                                        psum[:, 2 * s1 + b, 0:2 * (DV + 1)])
                    else:
                        if s >= 3:
                            dve.wait_ge(st_upd, s - 2)
                        for j in range(4):
                            to = c - 1 + (1 if d == 0 else -1)
                            last = stt(cs[:, d, to, j, :], cs[:, d, c - 1, j, :], ab[:, j, d * NT + c:d * NT + c + 1],
                                       psum[:, 2 * s1 + j // 2, (j % 2) * (DV + 1):(j % 2 + 1) * (DV + 1)],
                                       ALU.mult, ALU.add)
                    last.then_inc(st_upd, 1)

            def decays(n):
                c, j = n // 4, n % 4
                dve.wait_ge(front, n + 1)
                if n >= 2:
                    dve.wait_ge(nums, n - 1)
                e = sa[n % 2][:, 0:4 * P].rearrange("p (d g t) -> p d g t", d=2, g=2)
                for d in range(2):
                    for hh in range(2):
                        o = (2 * d + hh) * P
                        last = stt(e[:, d, hh, :], psum[:, 4, o:o + P], tk[:, 0, c, d, 2 * j + hh:2 * j + hh + 1],
                                   mask[d], ALU.add, ALU.min)
                last.then_inc(e_min, 1)
                if c > 0:
                    q = mq[:, j, c * P:(c + 1) * P].rearrange("p (o t) -> p o t", o=1).broadcast_to([P, 2, P])
                    tt(qw[:, n % 2, :, :], q, psum[:, 5, P:3 * P].rearrange("p (d t) -> p d t", d=2), ALU.mult)
                dve.wait_ge(e_exp, n + 1)
                for hh in range(2):
                    s = psum[:, 5 + hh, 0:P].rearrange("p (o t) -> p o t", o=1).broadcast_to([P, 2, P])
                    last = tt(e[:, :, hh, :], e[:, :, hh, :], s, ALU.mult)
                last.then_inc(s_in, 1)

            def outputs(n):
                c, j, s = n // 4, n % 4, n % 2
                dve.wait_ge(nums, n + 1)
                v = psum[:, 2 * s:2 * s + 2, 0:2 * (DV + 1)].rearrange("p g (d v) -> p g d v", d=2)
                dv_, num = v[:, :, :, DV:DV + 1].rearrange("p g d o -> p g (d o)"), v[:, :, :, 0:DV]
                floor = tk[:, 2, c, :, 2 * j:2 * j + 2].rearrange("p d g -> p g d")
                stt(den[:, :, :], dv_, -1.0, floor, ALU.mult, ALU.max).then_inc(den_s, 1)
                dve.wait_ge(den_s, 4 * n + 1)
                tt(den[:, :, :], den[:, :, :], dv_, ALU.max).then_inc(den_s, 1)
                dve.wait_ge(den_s, 4 * n + 2)
                dve.reciprocal(den[:, :, :], den[:, :, :]).then_inc(den_s, 1)
                dve.wait_ge(den_s, 4 * n + 3)
                tmp = sb[0][:, 0:4 * P].rearrange("p (g d v) -> p g d v", g=2, d=2)
                for hh in range(2):
                    r = den[:, hh, :].rearrange("p (d o) -> p d o", o=1).broadcast_to([P, 2, DV])
                    last = tt(tmp[:, hh, :, :], num[:, hh, :, :], r, ALU.mult)
                last.then_inc(den_s, 1)
                dve.wait_ge(den_s, 4 * n + 4)
                if n >= 2:
                    dve.wait_ge(hm_t, n - 1)
                tt(hmt[:, s, :, :], tmp[:, :, 0, :], tmp[:, :, 1, :], ALU.add).then_inc(hm_in, 1)

            def scale_hm(n):
                dve.wait_ge(ss_in, 3 * n + 3)
                r = ss[:, n % 2, :].rearrange("p (g o) -> p g o", o=1).broadcast_to([P, 2, DV])
                tt(hmt[:, n % 2, :, :], hmt[:, n % 2, :, :], r, ALU.mult).then_inc(hm_sc, 1)

            dve.wait_ge(kv_done, len(STATES))
            dve.wait_ge(st_upd, len(STATES))
            for n in range(UNITS):
                decays(n)
                if n >= 1:
                    outputs(n - 1)
                if n >= 2:
                    scale_hm(n - 2)
            outputs(UNITS - 1)
            scale_hm(UNITS - 2)
            scale_hm(UNITS - 1)

            def turn_halves(e):
                dst = aq[:, e, :] if e < KC else ak[:, e - KC, :]
                lat = dst[:, TP:N]
                dve.wait_ge(qk_st, e + 1)
                tt(sb[0][:, 0:TS], psum[:, 6, :], sin, ALU.mult).then_inc(rope, 1)
                tt(lat, lat, cos, ALU.mult).then_inc(rope_c, 1)
                dve.wait_ge(rope_c, 2 * e + 1)
                tt(lat, lat, sb[0][:, 0:TS], ALU.add).then_inc(rope_c, 1)
                dve.wait_ge(rope_c, 2 * e + 2)
                dve.wait_ge(qk_rs, e + 1)
                tt(dst, dst, rb[:, :], ALU.mult).then_inc(rope_out, 1)

            for e in range(14):
                split(Tile(T_MIX + L_AQ + e + 2))
                if 1 <= e <= 12:
                    turn_halves(e - 1)
            take_turned(12)
            take_turned(13)
            dve.wait_ge(ck_t, 1)
            copy(akc[:, :, :].rearrange("p g s -> p (g s)"), psum[:, 4, :]).then_inc(ck_ev, 1)
            dve.wait_ge(ck_t, 2)
            copy(ko[:, :], psum[:, 5, 0:KVH * HD]).then_inc(ck_ev, 1)

            def top(k):
                c, s = k // AH, k % 2
                w = P if c == 0 else N
                dve.wait_ge(sc, k + 1)
                dve.reduce_max(amax[:, s:s + 1], flat(2 * s)[:, 0:w], AX.X).then_inc(nmx, 1)
                dve.wait_ge(nmx, 2 * k + 1)
                ts(amax[:, s:s + 1], amax[:, s:s + 1], -HD ** -0.5, None, ALU.mult).then_inc(nmx, 1)

            def divide(k):
                c, s = k // AH, k % 2
                w = P if c == 0 else N
                dve.wait_ge(aexp, k + 1)
                dve.reciprocal(arec[:, s:s + 1], asum[:, s:s + 1]).then_inc(rcp, 1)
                dve.wait_ge(rcp, k + 1)
                ts(sa[s][:, 0:w], sa[s][:, 0:w], arec[:, s:s + 1], None, ALU.mult).then_inc(p_nrm, 1)

            def take_last(k):
                s = k % 2
                dve.wait_ge(atr, k + 1)
                dve.wait_ge(pv, k - 1)
                copy(sb[s][:, 4 * P:N], flat(2 * s + 1)[:, 4 * P:N]).then_inc(ptb, 1)

            for k in range(HEADS):
                top(k)
                if k - 1 >= AH:
                    take_last(k - 1)
                divide(k)
            take_last(HEADS - 1)

            def low_m(m):
                dve.wait_ge(mg_hi, m + 1)
                tt(m_lo[:, m, :], sb[m % 2][:, :], m_hi[:, m, :].bitcast(F32), ALU.subtract).then_inc(mg_lo, 1)

            for l in range(L_MO, L_END):
                t = Tile(T_MIX + l)
                split(t.plus(2))
                if l < L_BM:
                    m = l - L_MO
                    dve.wait_ge(ev[t.slot], t.pair + 1)
                    if m >= 2:
                        dve.wait_ge(mg_lo, m - 1)
                    tt(sb[m % 2][:, :], hm[:, m, :], sa[m % 2][:, :], ALU.mult).then_inc(mg, 1)
                    if m >= 1:
                        low_m(m - 1)
                elif l < L_OUT:
                    m, gate = (l - L_BM) % 16 // 2, (l - L_BM) % 2 == 0
                    if l == L_BM:
                        low_m(KC - 1)
                    if gate:
                        dve.wait_ge(ev[t.slot], t.pair + 1)
                    elif l < L_BA:
                        done(t)
                        tt(halves(y[:, m, :]), halves(sa[m % 2][:, :]), both(t.slot), ALU.mult).then_inc(ev[t.slot], 1)
                    else:
                        done(t)
                        if m >= 2:
                            dve.wait_ge(y_sum, m - 1)
                        else:
                            dve.wait_ge(mg_lo, KC)
                        tt(halves(sb[m % 2][:, :]), halves(sa[m % 2][:, :]), both(t.slot), ALU.mult).then_inc(ev[t.slot], 1)
                        dve.wait_ge(ev[t.slot], t.pair + 1)
                        tt(y[:, m, :], y[:, m, :], sb[m % 2][:, :], ALU.add).then_inc(y_sum, 1)
                if l == L_BA - 1:
                    for k in range(KC):
                        dve.wait_ge(hah, k + 1)
                        tt(m_lo[:, k, :], ha[:, k, :], m_hi[:, k, :].bitcast(F32), ALU.subtract).then_inc(hal, 1)
                if l in (L_OUT - 2, L_OUT - 1):
                    for k in range(KC - 1) if l == L_OUT - 2 else (KC - 1,):
                        dve.wait_ge(yh, k + 1)
                        tt(h_lo[:, k, :], y[:, k, :], h_hi[:, k, :].bitcast(F32), ALU.subtract).then_inc(yl, 1)
                if l > L_OUT:
                    add_square(1, l - 1 - L_OUT)

            inverse(3)
            dve.wait_ge(x_back, 16)
            residual(1)
            inverse(4)
            dve.wait_ge(x_upd, 2 * KC)
            normed(2)
            ffn(1, T_FFN1)
            inverse(5)
            residual(2)


def constants():
    c = np.zeros((P, C_N), np.float32)
    r = np.arange(P)
    c[:, 0:P] = np.eye(P)
    c[:, P:2 * P] = 1.0 / D
    c[:, 2 * P:3 * P] = (r[:, None] // HD == r[None, :] // HD) / HD
    for p in range(P):
        if p % 32 < 16:
            c[p + 16, 3 * P + p] = -1.0
        else:
            c[p - 16, 3 * P + p] = 1.0
    c[:, 4 * P:5 * P] = np.where(r[:, None] <= r[None, :], 0.0, -1e4)
    c[:, 5 * P:6 * P] = np.where(r[:, None] >= r[None, :], 0.0, -1e4)
    tok = np.arange(TS)
    pos = np.stack([tok // GRID_W, tok % GRID_W]).astype(np.float32)
    freq = np.float32(10000.0) ** (-np.arange(16, dtype=np.float32) / np.float32(16))
    ang = pos[(r % HD) // 32] * freq[r % 16][:, None]
    c[:, 6 * P:6 * P + TS] = np.cos(ang)
    c[:, 6 * P + TS:] = np.sin(ang)
    rc = np.zeros((H, R_N), np.float32)
    for h in range(H):
        rc[h, h * P:(h + 1) * P] = 1.0
        o = H * P + (h // 2) * P + (h % 2) * DK
        rc[h, o:o + DK] = 1.0
    rc[:, H * P + 4 * P:] = 1.0
    return c, rc


def lay_out(i):
    f = lambda n: np.asarray(i[n])

    def tiles(w, order=None):
        k, n = w.shape
        w = w.reshape(k // P, P, n // P, P).transpose(2, 1, 0, 3)
        return w.reshape(n // P, P, k)

    wi = f("ffn_w_in")[0].reshape(2, D, 2, NJ, P).transpose(0, 1, 3, 2, 4).reshape(2, D, 2 * DFF)
    mix = f("w_in_mix")[0]
    sizes = (H * DK, H * DK, H * DV, H * DV, 4 * H, AH * HD, KVH * HD, KVH * HD, 2 * D)
    mq, mk, mv, mo, mg, aq, ak, av, bg = np.split(mix, np.cumsum(sizes)[:-1], axis=1)
    gates = np.tile(mg.reshape(D, 4, 1, H), (1, 1, 4, 1)).reshape(D, P)
    keys = np.tile(ak.reshape(D, KVH, 1, HD), (1, 1, 2, 1)).reshape(D, KVH * P)

    def paired(g, w):
        return np.stack([tiles(g), tiles(w)], 1).reshape(2 * KC, P, D)

    w_mix = np.concatenate([
        tiles(gates), tiles(mq), tiles(mk), tiles(mv), tiles(aq), tiles(keys), tiles(av), tiles(mo),
        paired(bg[:, :D], f("w_branch_m")[0]), paired(bg[:, D:], f("w_branch_a")[0]), tiles(f("w_out")[0])])
    qk = f("qk_norm")[0]
    vecs = np.concatenate([
        f("b_mod")[0].reshape(-1, P), f("norm_pre")[0].reshape(-1, P), f("norm_post")[0].reshape(-1, P),
        f("mlstm_norm")[0].reshape(-1, P), f("c_ctx").reshape(-1, P), f("c")[0].reshape(-1, P),
        np.concatenate([qk, qk], axis=1)])
    cst, rowc = constants()
    return {
        "x_prompt": f("x_prompt"), "x_sample": f("x_sample"),
        "w_mod": f("w_mod")[0].reshape(KC, P, -1, MOD_W).transpose(2, 1, 0, 3).reshape(-1, P, KC * MOD_W),
        "w_ffn_in": np.concatenate([tiles(wi[0]), tiles(wi[1])]),
        "w_ffn_out": np.concatenate([tiles(f("ffn_w_out")[0, n]) for n in range(2)]),
        "w_mix": w_mix, "vec_rows": vecs, "cst": cst, "rowc": rowc,
        "gate_bias": f("mlstm_gate_bias")[0].reshape(4, H).T,
        "m0": f("state_m")[0, 0].T, "state_C": f("state_C"), "state_n": f("state_n"),
        "cache_k": f("cache_k").reshape(PAST, KVH * HD), "cache_v": f("cache_v").reshape(PAST, KVH * HD),
    }


OUTS = (("o_yp", (1, TP, D)), ("o_ys", (1, TS, D)), ("o_k", (PAST, KVH * HD)), ("o_v", (PAST, KVH * HD)),
        ("o_C", (1, 1, 2, H, DK, DV)), ("o_n", (1, 1, 2, H, DK)), ("o_m", (1, 1, 2, H)))


def kernel(**inputs):
    import concourse.bacc as bacc
    from concourse.bass_utils import run_bass_kernel_spmd

    nc = bacc.Bacc("TRN2", target_bir_lowering=False, num_devices=1)
    arrays, a = {}, {}
    for name, v in lay_out(inputs).items():
        v = np.ascontiguousarray(v)
        arrays[f"in_{name}"] = v
        a[name] = nc.dram_tensor(f"in_{name}", v.shape, mybir.dt.from_np(v.dtype), kind="ExternalInput").ap()
    for name, shape in OUTS:
        a[name] = nc.dram_tensor(name, shape, F32, kind="ExternalOutput").ap()
    a["x_keep"] = nc.dram_tensor("x_keep", (P, KC * N), F32, kind="Internal").ap()
    build(nc, a)
    r = run_bass_kernel_spmd(nc, [arrays], core_ids=[0]).results[0]
    out = [np.asarray(r[name]) for name, _ in OUTS]
    out[2] = out[2].reshape(1, 1, TP, KVH, HD)
    out[3] = out[3].reshape(1, 1, TP, KVH, HD)
    return tuple(out)
```

```python
from contextlib import ExitStack

import numpy as np

import concourse.bass as bass
from concourse import mybir

F32 = mybir.dt.float32
F32R = mybir.dt.float32r
ALU = mybir.AluOpType
ACT = mybir.ActivationFunctionType
AX = mybir.AxisListType

P = 128
D = 1024
KC = D // P
TP, TS = 128, 512
N = TP + TS
LAG = 5
BANK_A = 2
LN_EXP = "natural_log_exp_and_others"
NT = N // P
HALF = N // 2
DFF = 2816
NJ = DFF // P
PHASES = (8, 8, 6)
PAST = 128
H, DK, DV = 8, 64, 128
AH, KVH, HD = 16, 4, 64
GRID_W = 64
EPS = 1e-6
NMOD = 9
MOD_T = 4
MOD_W = MOD_T * P
MOD_FIRST = 2 * KC // MOD_T
MOD_LATER = NMOD * KC // MOD_T - MOD_FIRST
MOD_DVE = 2
MOD_K = ((0, 3), (3, 6), (6, 8))
RAWS = 4
GROUPS = ((0, slice(0, TP)), (1, slice(TP, N)))

L_GATE, L_MQ, L_MK, L_MV, L_AV, L_AK, L_AQ, L_MO, L_BM, L_BA, L_OUT, L_END = np.cumsum(
    [0, 1, 4, 4, 8, 2, 2, 8, 8, 16, 16, 8]).tolist()
FFN_TILES = 2 * NJ + KC * len(PHASES)
T_MIX = FFN_TILES
T_FFN1 = T_MIX + L_END
ROW_M, ROW_END = 2 + 2 * NT + 4 + 7, 2 + 2 * NT + 4 + 7 + 4 + 3
QK = L_MO - L_AK
NKC = L_AQ - L_AK
UNITS = NT * 4
HEADS = NT * AH
STATES = ((0, 0), (1, 0), (0, 1), (1, 4), (0, 2), (1, 3), (0, 3), (1, 2))
C_N = 6 * P + 2 * TS
R_N = H * P + 4 * P + P

V_PRE, V_POST, V_MN, V_CC, V_QG, V_KG, V_N = 72, 96, 120, 128, 144, 145, 146


class Tile:

    def __init__(self, c, i=0):
        self.c, self.i = c, i
        self.raw, self.slot = c % RAWS, c % 2
        self.n = 4 * i + c
        self.quad = i + c // 4
        self.pair = 2 * i + c // 2

    def plus(self, k):
        return Tile(self.c + k, self.i)


def build(nc, a):
    ctx = ExitStack()
    with ctx:
        def sem(name):
            return ctx.enter_context(nc.semaphore(name))

        def at(name, shape, dt, offset):
            return nc.alloc_sbuf_tensor_at(name, shape, dt, offset=offset)

        row = N * 4
        cur = [-(-nc.sbuf_base // 64) * 64]

        def place(name, shape, dt=F32):
            t = at(name, shape, dt, cur[0])
            cur[0] += -(-int(np.prod(shape[1:])) * 4 // 32) * 32
            return t

        cst = place("cst", [P, C_N])
        rowc = place("rowc", [H, R_N])
        vT = place("vT", [P, V_N])
        silc = place("silc", [P, 2, KC])
        mod = place("mod", [P, NMOD * KC, 2])
        pre_s = place("pre_s", [P, 3, KC, 2])
        post_s = place("post_s", [P, 3, KC, 2])
        gbias = place("gbias", [H, 4])
        m0 = place("m0", [H, 2])
        epsc = place("epsc", [P, 2])
        x_at = cur[0]
        x = place("x", [P, KC, N])
        h_at = cur[0]
        h_hi = place("h_hi", [P, KC, N], F32R)
        h_lo = place("h_lo", [P, KC, N], F32R)
        raw = [place(f"raw{s}", [P, KC, P]) for s in range(RAWS)]
        whi = [place(f"whi{s}", [P, KC, P], F32R) for s in range(2)]
        wlo = [place(f"wlo{s}", [P, KC, P], F32R) for s in range(2)]
        sa = [place(f"sa{s}", [P, N]) for s in range(2)]
        sb_at = cur[0]
        sb = [place(f"sb{s}", [P, N]) for s in range(2)]
        sq_at = cur[0]
        sq = [place(f"sq{s}", [P, N]) for s in range(2)]
        rb = place("rb", [P, N])
        r1 = cur[0]
        r2 = r1 + KC * row
        r3 = r2 + KC * row
        y = at("y", [P, KC, N], F32, r1)
        g_hi = at("g_hi", [P, PHASES[0], N], F32R, r2)
        g_lo = at("g_lo", [P, PHASES[0], N], F32R, r2 + KC * row)
        mw_at = r2 + 2 * KC * row
        mw = at("mw", [P, KC, MOD_W], F32, mw_at)
        macc = at("macc", [P, 2, MOD_W], F32, mw_at + KC * MOD_W * 4)
        mw0 = [at(f"mw0_{s}", [P, KC, MOD_W], F32, r1 + s * KC * MOD_W * 4) for s in range(MOD_FIRST)]
        xtok = at("xtok", [P, NT, D], F32, h_at)
        vrow = at("vrow", [P, P], F32, r1 + MOD_FIRST * KC * MOD_W * 4)
        vrow2 = at("vrow2", [V_N - P, P], F32, r1 + MOD_FIRST * KC * MOD_W * 4 + 512)
        otok = [at(f"otok{s}", [P, D], F32, r2 + s * D * 4) for s in range(NT)]
        mkt = at("mkt", [P, NT, H * DK], F32, x_at)
        nm = at("nm", [H, 2, N], F32, x_at + 10240)
        t1 = at("t1", [H, 2, N], F32, x_at + 15360)
        gi = at("gi", [H, 2, N], F32, r1)
        gf = at("gf", [H, 2, N], F32, r1 + 5120)
        gb = at("gb", [H, 2, N], F32, r1 + 10240)
        gm = at("gm", [H, 2, N], F32, r1 + 15360)
        hm = at("hm", [P, H, N], F32, r1)
        mq = at("mq", [P, 4, N], F32, r2)
        mk = at("mk", [P, 4, N], F32, r2 + 4 * row)
        cur[0] = r3
        vt = place("vt", [P, NT, H, DV + 1])
        cs = place("cs", [P, 2, NT - 1, 4, DV + 1])
        tk = place("tk", [P, 3, NT, 2, H])
        ab = place("ab", [P, 4, 2 * NT])
        m_in = place("m_in", [H, 2, NT])
        nml = place("nml", [H, 2, NT])
        ar = place("ar", [H, 2, NT])
        mout = place("mout", [H, 2])
        den = place("den", [P, 2, 2])
        ss = place("ss", [P, 2, 2])
        cp = place("cp", [P, 2, 4, DV + 1])
        end_m = cur[0]
        qw = at("qw", [P, 2, 2, P], F32, sq_at)
        hmt = at("hmt", [P, 2, 2, P], F32, sb_at + 2560)
        ha = at("ha", [P, KC, N], F32, r2)
        cur[0] = r3
        aq = place("aq", [P, KC, N])
        ak = place("ak", [P, 2 * NKC, N])
        akc = place("akc", [P, KVH, PAST])
        av = place("av", [P, NT + 1, KVH * HD])
        amax = place("amax", [P, 2])
        asum = place("asum", [P, 2])
        arec = place("arec", [P, 2])
        end_a = cur[0]
        ck2 = at("ck2", [P, KVH, 2, HD], F32, x_at)
        ko = at("ko", [P, KVH * HD], F32, x_at + 2048)
        m_hi = at("m_hi", [P, KC, N], F32R, r3)
        m_lo = at("m_lo", [P, KC, N], F32R, r3 + KC * row)
        assert max(end_m, end_a, r3 + 2 * KC * row, mw_at + (KC + 2) * MOD_W * 4) <= nc.sbuf_usable_end

        ident, ones_d, ones_h, swap = (cst[:, n * P:(n + 1) * P] for n in range(4))
        mask = [cst[:, (4 + d) * P:(5 + d) * P] for d in range(2)]
        cos, sin = cst[:, 6 * P:6 * P + TS], cst[:, 6 * P + TS:6 * P + 2 * TS]
        sel1 = rowc[:, 0:H * P].rearrange("h (g p) -> h g p", g=H)
        sel2 = rowc[:, H * P:H * P + 4 * P].rearrange("h (j p) -> h j p", j=4)
        one_row = rowc[:, H * P + 4 * P:R_N]

        psum = ctx.enter_context(nc.psum_tensor("psum", [P, 8, 512], F32))

        def half_out(slot, h):
            return psum[:, 2 * slot + h, 0:HALF]

        def qk(n):
            return ak[:, n, :] if n < NKC else aq[:, n - NKC, :]

        def both(slot):
            return psum[:, 2 * slot:2 * slot + 2, 0:HALF]

        def flat(slot):
            return psum[:, 2 * slot:2 * slot + 2, :].rearrange("p b n -> p (b n)")

        def halves(t):
            return t.rearrange("p (h n) -> p h n", h=2)

        def mod_out(n, bank=7):
            return psum[:, bank, n:n + P]

        ld_small, ld_row, ld_x = sem("ld_small"), sem("ld_row"), [sem(f"ld_x{c}") for c in range(NT)]
        raw_in = [sem(f"raw_in{s}") for s in range(RAWS)]
        raw_free = sem("raw_free")
        w_hi = sem("w_hi")
        tile_done = sem("tile_done")
        ev = [sem("ev0"), sem("ev1")]
        mod0_in = [sem(f"mod0_in{s}") for s in range(MOD_FIRST)]
        mod0_mul, mod0_ev = sem("mod0_mul"), sem("mod0_ev")
        mod_in = [sem(f"mod_in{s}") for s in range(3)]
        mod_mul, mod_done, mod_ev = sem("mod_mul"), sem("mod_done"), sem("mod_ev")
        mod_ready, post_ready = sem("mod_ready"), sem("post_ready")
        vec_t, v_ready, silc_ready, eps_in = sem("vec_t"), sem("v_ready"), sem("silc_ready"), sem("eps_in")
        x_t, x_ev, dv = sem("x_t"), [sem("x_ev0"), sem("x_ev1")], sem("dv")
        sq_in, stat_mm = sem("sq_in"), sem("stat_mm")
        ysq_in, sq_sum, ystat_mm, y_in = sem("ysq_in"), sem("sq_sum"), sem("ystat_mm"), sem("y_in")
        rb_ln, rb_ready = sem("rb_ln"), sem("rb_ready")
        pre_t, pre_h, h_rdy = sem("pre_t"), sem("pre_h"), sem("h_rdy")
        pre_hi = [sem("pre_hi0"), sem("pre_hi1")]
        post_t, x_upd = sem("post_t"), sem("x_upd")
        g_hi_s, g_lo_s = sem("g_hi_s"), sem("g_lo_s")
        x_spill, x_back = sem("x_spill"), sem("x_back")
        tr_done, tr_ev = sem("tr_done"), sem("tr_ev")
        row_d, row_a, tok_t, tok_ev = sem("row_d"), sem("row_a"), sem("tok_t"), sem("tok_ev")
        st_in, kw_in, kv_done, st_upd = sem("st_in"), sem("kw_in"), sem("kv_done"), sem("st_upd")
        ones_v = sem("ones_v")
        m_spread, front, e_min, e_exp, s_in = (sem(n) for n in ("m_spread", "front", "e_min", "e_exp", "s_in"))
        nums, den_s, hm_in, ss_in, hm_sc, hm_t, hm_ev = (
            sem(n) for n in ("nums", "den_s", "hm_in", "ss_in", "hm_sc", "hm_t", "hm_ev"))
        qk_st, qk_rb, qk_rs = sem("qk_st"), sem("qk_rb"), sem("qk_rs")
        rope, rope_c, rope_out, ak_sw = sem("rope"), sem("rope_c"), sem("rope_out"), sem("ak_sw")
        ck_in, ck_t, ck_ev = sem("ck_in"), sem("ck_t"), sem("ck_ev")
        sc, nmx, aexp, rcp, p_nrm, atr, pta, ptb, pv, ha_ev = (sem(n) for n in (
            "sc", "nmx", "aexp", "rcp", "p_nrm", "atr", "pta", "ptb", "pv", "ha_ev"))
        mg, mg_hi, mg_lo = sem("mg"), sem("mg_hi"), sem("mg_lo")
        hah, hal, yh, yl = sem("hah"), sem("hal"), sem("yh"), sem("yl")
        y_sum = sem("y_sum")
        ot, oe = sem("ot"), [sem("oe0"), sem("oe1")]
        out_st, misc_st = sem("out_st"), sem("misc_st")

        block = ctx.enter_context(nc.Block())

        @block.sync
        def _(sp):
            def load(t, src, nk=KC):
                sp.wait_ge(raw_free, t.n + 1)
                sp.dma_start(raw[t.raw][:, 0:nk, :].rearrange("p k c -> p (k c)"), src).then_inc(raw_in[t.raw], 16)

            def load_mod(n, part):
                lo, hi = MOD_K[part]
                if not (isinstance(n, int) and n == 0):
                    sp.wait_ge(mod_mul, 2 * (KC * (n - 1) + hi))
                src = pick(a["w_mod"][:, :, lo * MOD_W:hi * MOD_W], MOD_FIRST + n)
                sp.dma_start(mw[:, lo:hi, :].rearrange("p k c -> p (k c)"), src).then_inc(mod_in[part], 16)

            def pick(tiles, n):
                if isinstance(n, int):
                    return tiles[n]
                return tiles[bass.ds(n, 1)].rearrange("o p c -> p (o c)")

            sp.dma_start(vrow[:, :], a["vec_rows"][0:P]).then_inc(ld_small, 16)
            sp.dma_start(vrow2[:, :], a["vec_rows"][P:V_N]).then_inc(ld_small, 16)
            sp.dma_start(cst[:, :], a["cst"]).then_inc(ld_small, 16)
            for c in range(NT):
                src = a["x_prompt"][0] if c == 0 else a["x_sample"][0, (c - 1) * P:c * P]
                sp.dma_start(xtok[:, c, :], src).then_inc(ld_x[c], 16)
            for s in range(MOD_FIRST):
                sp.dma_start(mw0[s][:, :, :].rearrange("p k c -> p (k c)"), a["w_mod"][s]).then_inc(mod0_in[s], 16)
            for t in range(RAWS):
                load(Tile(t), a["w_ffn_in"][t])
            for src, dst in ((a["rowc"], rowc[:, :]), (a["gate_bias"], gbias[:, :]), (a["m0"], m0[:, :])):
                sp.dma_start(dst, src).then_inc(ld_row, 16)
            sp.wait_ge(mod_done, 1)

            def ffn(f, base):
                it = 0
                j0 = 0
                for p, nj in enumerate(PHASES):

                    def ahead(n, u):
                        if u == 0 and not (isinstance(n, int) and n in (0, MOD_LATER - 2)):
                            load_mod(n - 1, 2)
                        elif u >= 2:
                            load_mod(n, u - 2)

                    def load_in(i):
                        for u in range(4):
                            if not (isinstance(i, int) and f == 0 and p == 0 and i == 0):
                                load(Tile(base + u, i), pick(a["w_ffn_in"], f * 2 * NJ + 2 * j0 + 4 * i + u))
                            if f == 0 and p < 2:
                                ahead(it + i, u)

                    def load_out(i):
                        for u in range(4):
                            src = a["w_ffn_out"][:, :, j0 * P:(j0 + nj) * P]
                            load(Tile(base + u, i), pick(src, f * KC + 4 * i + u), nj)
                            if f == 0:
                                ahead(it + i, u)

                    if f == 0 and p == 0:
                        load_in(0)
                        with sp.Fori(0, nj // 2 - 1) as i:
                            load_in(i + 1)
                    else:
                        with sp.Fori(0, nj // 2) as i:
                            load_in(i)
                    if p < 2:
                        it += nj // 2
                    base += 2 * nj
                    if f == 0 and p == 2:
                        load_out(0)
                        load_out(1)
                    else:
                        with sp.Fori(0, 2) as i:
                            load_out(i)
                    it += 2
                    base += KC
                    j0 += nj
                    if f == 0 and p > 0:
                        load_mod(it - 1, 2)

            ffn(0, 0)

            def mix(lo, hi):
                for l in range(lo, hi):
                    load(Tile(T_MIX + l), a["w_mix"][l])

            mix(L_GATE, RAWS)
            sp.wait_ge(x_upd, KC)
            sp.dma_start(a["x_keep"], x[:, :, :].rearrange("p k n -> p (k n)")).then_inc(x_spill, 16)
            for d in range(2):
                c = (0, NT - 2)[d]
                sp.dma_start(cs[:, d, c, :, 0:DV],
                             a["state_C"][0, 0, d].rearrange("(j g) k v -> (g k) j v", g=2)).then_inc(st_in, 16)
                sp.dma_start(cs[:, d, c, :, DV:DV + 1],
                             a["state_n"][0, 0, d].rearrange("(j g) (k o) -> (g k) j o", g=2, o=1),
                             allow_slow_non_contiguous=True).then_inc(st_in, 16)
            mix(RAWS, L_AV + 2)
            sp.wait_ge(row_d, ROW_M)
            sp.dma_start(a["o_m"].rearrange("a b d h -> h (a b d)"), mout[:, :],
                         allow_slow_non_contiguous=True).then_inc(misc_st, 16)
            sp.wait_ge(st_upd, 2)
            for d in range(2):
                sp.dma_start(a["o_C"][0, 0, d].rearrange("(j g) k v -> (g k) j v", g=2),
                             cp[:, d, :, 0:DV]).then_inc(misc_st, 16)
                sp.dma_start(a["o_n"][0, 0, d].rearrange("(j g) (k o) -> (g k) j o", g=2, o=1),
                             cp[:, d, :, DV:DV + 1], allow_slow_non_contiguous=True).then_inc(misc_st, 16)
            sp.wait_ge(hm_ev, UNITS)
            sp.wait_ge(misc_st, 16 * 5)
            for r in range(2):
                sp.dma_start(ck2[:, :, r, :], a["cache_k"].rearrange("s (g d) -> s g d", g=KVH)).then_inc(ck_in, 16)
            sp.dma_start(av[:, NT, :], a["cache_v"]).then_inc(ck_in, 16)
            mix(L_AV + 2, L_AQ + 6)
            sp.wait_ge(rope_out, NKC)
            for hh in range(2):
                sp.dma_start(ak[hh * HD:(hh + 1) * HD, NKC:2 * NKC, :],
                             ak[(1 - hh) * HD:(2 - hh) * HD, 0:NKC, :]).then_inc(ak_sw, 16)
            mix(L_AQ + 6, L_MO + 2)
            sp.wait_ge(ck_ev, 2)
            sp.dma_start(a["o_k"], ko[:, :]).then_inc(misc_st, 16)
            sp.wait_ge(tr_ev, 14)
            sp.dma_start(a["o_v"], av[:, 0, :]).then_inc(misc_st, 16)
            sp.wait_ge(misc_st, 16 * 7)
            sp.wait_ge(x_spill, 16)
            sp.dma_start(x[:, :, :].rearrange("p k n -> p (k n)"), a["x_keep"]).then_inc(x_back, 16)
            mix(L_MO + 2, L_END)
            ffn(1, T_FFN1)
            for c in range(NT):
                sp.wait_ge(oe[c % 2], c // 2 + 1)
                dst = a["o_yp"][0] if c == 0 else a["o_ys"][0, (c - 1) * P:c * P]
                sp.dma_start(dst, otok[c][:, :]).then_inc(out_st, 16)
            sp.wait_ge(out_st, 16 * NT)

        @block.tensor
        def _(pe):
            mm, tp = pe.matmul, pe.transpose

            def project(t, nk, hi, lo, ready=None, first=0):
                pe.wait_ge(raw_free, t.n + 1 + RAWS)
                pe.wait_ge(ev[t.slot], t.pair)
                for k in range(nk):
                    if ready is not None:
                        pe.wait_ge(ready, first + k + 1)
                    for h in range(2):
                        cols = slice(h * HALF, (h + 1) * HALF)
                        out = half_out(t.slot, h)
                        mm(out, whi[t.slot][:, k, :], hi[:, k, cols], start=(k == 0), stop=False)
                        mm(out, whi[t.slot][:, k, :], lo[:, k, cols], start=False, stop=False)
                        last = mm(out, wlo[t.slot][:, k, :], hi[:, k, cols], start=False, stop=(k == nk - 1))
                last.then_inc(tile_done, 1)

            def project_two(t0, t1, ready, first):
                for t in (t0, t1):
                    pe.wait_ge(raw_free, t.n + 1 + RAWS)
                    pe.wait_ge(ev[t.slot], t.pair)
                for step in range(KC + LAG):
                    if step < KC:
                        pe.wait_ge(ready, first + step + 1)
                    for t, k in ((t0, step), (t1, step - LAG)):
                        if not 0 <= k < KC:
                            continue
                        for h in range(2):
                            cols = slice(h * HALF, (h + 1) * HALF)
                            out = half_out(t.slot, h)
                            mm(out, whi[t.slot][:, k, :], h_hi[:, k, cols], start=(k == 0), stop=False)
                            mm(out, whi[t.slot][:, k, :], h_lo[:, k, cols], start=False, stop=False)
                            last = mm(out, wlo[t.slot][:, k, :], h_hi[:, k, cols], start=False, stop=(k == KC - 1))
                        if k == KC - 1:
                            last.then_inc(tile_done, 1)

            def modulate(s):
                pe.wait_ge(mod0_in[s], 16)
                for t in range(MOD_T):
                    out = mod_out(2 * (MOD_T * s + t)).rearrange("p (o g) -> p o g", g=2)
                    for k in range(KC):
                        both_c = silc[:, :, k].rearrange("p (o g) -> p o g", o=1).broadcast_to([P, P // 2, 2])
                        last = mm(out, mw0[s][:, k, t * P:(t + 1) * P], both_c, start=(k == 0), stop=(k == KC - 1))
                return last

            def sum_mod(n):
                pe.wait_ge(mod_mul, 2 * KC * (n + 1))
                pe.wait_ge(mod_ev, n + 1)
                sum_products(7).then_inc(mod_done, 1)

            def sum_products(bank):
                for t in range(MOD_T):
                    for g in range(2):
                        last = mm(mod_out(2 * t + g, bank), macc[:, g, t * P:(t + 1) * P], ones_d, start=True, stop=True)
                return last

            def stats_y(n):
                for part, src in enumerate((rb, sq[(KC - 1) % 2])):
                    if part == 0:
                        pe.wait_ge(sq_sum, (KC - 2) * (n + 1))
                    else:
                        pe.wait_ge(ysq_in, KC * (n + 1))
                    for h in range(2):
                        last = mm(half_out(2, h), ones_d, src[:, h * HALF:(h + 1) * HALF],
                                  start=(part == 0), stop=(part == 1))
                last.then_inc(ystat_mm, 1)

            def stats(n):
                for k in range(KC):
                    pe.wait_ge(sq_in, 8 * n + k + 1)
                    for h in range(2):
                        last = mm(half_out(2, h), ones_d, sq[k % 2][:, h * HALF:(h + 1) * HALF],
                                  start=(k == 0), stop=(k == KC - 1))
                    last.then_inc(stat_mm, 1)

            pe.sem_inc(tile_done, 2)
            pe.wait_ge(ld_small, 48)
            tp(psum[:, 6, 0:P], vrow[:, :], ident)
            tp(psum[:, 6, P:V_N], vrow2[:, :], ident[0:V_N - P, 0:V_N - P]).then_inc(vec_t, 1)
            for c in range(NT):
                pe.wait_ge(ld_x[c], 16)
            for k in range(KC):
                if k >= 2:
                    pe.wait_ge(x_ev[k % 2], k // 2)
                for c in range(NT):
                    last = tp(flat(k % 2)[:, c * P:(c + 1) * P], xtok[:, c, k * P:(k + 1) * P], ident)
                last.then_inc(x_t, 1)

            def ffn(f, base):
                it, j0 = 0, 0
                for p, nj in enumerate(PHASES):
                    def tiles_in(i, lo=0):
                        for u in range(lo, 4):
                            project(Tile(base + u, i), KC, h_hi, h_lo)
                        if f == 0 and p < 2:
                            sum_mod(it + i)

                    if p == 0:
                        project_two(Tile(base), Tile(base + 1), h_rdy, 16 * f)
                        tiles_in(0, 2)
                        with pe.Fori(0, nj // 2 - 1) as i:
                            tiles_in(i + 1)
                    else:
                        with pe.Fori(0, nj // 2) as i:
                            tiles_in(i)
                    if p < 2:
                        it += nj // 2
                    base += 2 * nj
                    with pe.Fori(0, 2) as i:
                        for u in range(4):
                            project(Tile(base + u, i), nj, g_hi, g_lo, g_lo_s if u == 0 else None, NJ * f + j0)
                        if f == 0:
                            sum_mod(it + i)
                    it += 2
                    base += KC
                    j0 += nj

            pe.wait_ge(silc_ready, 1)
            for s in range(MOD_FIRST):
                if s == MOD_DVE:
                    stats_y(0)
                else:
                    modulate(s)
            pe.wait_ge(mod0_mul, 2 * KC)
            sum_products(6).then_inc(mod_done, 1)
            ffn(0, 0)
            stats_y(1)
            stats(0)

            def gemm(l, hi=h_hi, lo=h_lo, ready=None, first=0):
                project(Tile(T_MIX + l), KC, hi, lo, ready, first)

            def turn(jb):
                l = L_MK + jb if jb < 12 else L_AV + jb - 12
                t = Tile(T_MIX + l)
                pe.wait_ge(ev[t.slot], t.pair + 1)
                if jb >= 2:
                    pe.wait_ge(tr_ev, jb - 1)
                else:
                    pe.wait_ge(tok_ev, 2)
                src = mk[:, jb, :] if jb < 4 else sa[jb % 2][:, :]
                for c in range(NT):
                    last = tp(flat(2 + jb % 2)[:, c * P:(c + 1) * P], src[:, c * P:(c + 1) * P], ident)
                last.then_inc(tr_done, 1)

            def turn_gates():
                pe.wait_ge(row_a, 6)
                pe.wait_ge(row_d, ROW_END)
                for q, src in enumerate((gi, gf, gm)):
                    for c in range(NT):
                        for d in range(2):
                            o = ((q * NT + c) * 2 + d) * H
                            last = tp(psum[:, 4, o:o + H], src[:, d, c * P:(c + 1) * P], ident[0:H, 0:H])
                last.then_inc(tok_t, 1)
                for j in range(4):
                    last = mm(psum[:, 5, j * 2 * NT:(j + 1) * 2 * NT], sel2[:, j, :],
                              ar[:, :, :].rearrange("h d c -> h (d c)"), start=True, stop=True)
                last.then_inc(tok_t, 1)

            project_two(Tile(T_MIX), Tile(T_MIX + 1), h_rdy, KC)
            for l in range(2, L_AV):
                gemm(l)
                if l == L_MK:
                    turn_gates()
                if l > L_MK:
                    turn(l - L_MK - 1)
            turn(11)

            for s, (d, c) in enumerate(STATES):
                pe.wait_ge(kw_in, s + 1)
                pe.wait_ge(ones_v, 1)
                if s >= 2:
                    pe.wait_ge(st_upd, s - 1)
                else:
                    pe.wait_ge(tr_ev, 12)
                for g in range(H):
                    j, hh = g // 2, g % 2
                    last = mm(psum[hh * DK:(hh + 1) * DK, 2 * (s % 2) + j // 2, (j % 2) * (DV + 1):(j % 2 + 1) * (DV + 1)],
                              sa[s % 2][:, g * DK:(g + 1) * DK], vt[:, c, g, :], start=True, stop=True)
                last.then_inc(kv_done, 1)

            def spread_m(n):
                c, j = n // 4, n % 4
                tok = slice(c * P, (c + 1) * P)
                if n == 0:
                    pe.wait_ge(tok_ev, 2)
                else:
                    pe.wait_ge(e_min, n)
                bc = psum[:, 4, :].rearrange("p (d g t) -> p d g t", d=2, g=2)
                for hh in range(2):
                    last = mm(bc[:, :, hh, :], sel1[:, 2 * j + hh, :], nm[:, :, tok], start=True, stop=True)
                last.then_inc(m_spread, 1)

            def front_of(n):
                c, j = n // 4, n % 4
                tok = slice(c * P, (c + 1) * P)
                if n >= 1:
                    pe.wait_ge(s_in, n)
                if c > 0:
                    mm(psum[:, 5, P:3 * P].rearrange("p (d t) -> p d t", d=2), sel2[:, j, :], t1[:, :, tok],
                       start=True, stop=True)
                for hh in range(2):
                    half = slice(hh * DK, (hh + 1) * DK)
                    last = mm(psum[:, 5 + hh, 0:P], mk[half, j, tok], mq[half, j, tok], start=True, stop=True)
                last.then_inc(front, 1)

            def nums_of(n):
                c, j = n // 4, n % 4
                pe.wait_ge(s_in, n + 1)
                if n >= 2:
                    pe.wait_ge(hm_in, n - 1)
                else:
                    pe.wait_ge(st_upd, len(STATES))
                for hh in range(2):
                    half = slice(hh * DK, (hh + 1) * DK)
                    for d in range(2):
                        out = psum[:, 2 * (n % 2) + hh, d * (DV + 1):(d + 1) * (DV + 1)]
                        last = mm(out, sa[n % 2][:, (2 * d + hh) * P:(2 * d + hh + 1) * P], vt[:, c, 2 * j + hh, :],
                                  start=True, stop=(c == 0))
                        if c > 0:
                            last = mm(out, qw[half, n % 2, d, :], cs[half, d, c - 1, j, :], start=False, stop=True)
                last.then_inc(nums, 1)

            def turn_hm(n):
                pe.wait_ge(hm_sc, n + 1)
                if n >= 1:
                    pe.wait_ge(hm_ev, n)
                for hh in range(2):
                    last = tp(psum[:, 7, hh * P:(hh + 1) * P], hmt[:, n % 2, hh, :], ident)
                last.then_inc(hm_t, 1)

            spread_m(0)
            front_of(0)
            for n in range(UNITS):
                if n + 1 < UNITS:
                    spread_m(n + 1)
                    front_of(n + 1)
                nums_of(n)
                if n >= 2:
                    turn_hm(n - 2)
            pe.wait_ge(hm_in, UNITS)
            gemm(L_AV)
            turn_hm(UNITS - 2)
            turn_hm(UNITS - 1)

            def qk_stats(n):
                t = Tile(T_MIX + L_AK + n)
                pe.wait_ge(ev[t.slot], t.pair + 1)
                if n >= 1:
                    pe.wait_ge(qk_rb, n)
                    pe.wait_ge(rope, n)
                for h in range(2):
                    mm(half_out(2, h), ones_h, sq[n % 2][:, h * HALF:(h + 1) * HALF], start=True, stop=True)
                mm(psum[:, 6, :], swap, qk(n)[:, TP:N], start=True, stop=True).then_inc(qk_st, 1)

            for l in range(L_AV, L_MO):
                if l > L_AV:
                    gemm(l)
                if l in (L_AV + 1, L_AV + 2):
                    turn(12 + l - 1 - L_AV)
                if l == L_AK + 1:
                    pe.wait_ge(ck_in, 48)
                    pe.wait_ge(tr_ev, 14)
                    for g in range(KVH):
                        last = tp(psum[:, 7, g * PAST:(g + 1) * PAST], ck2[:, g, :, :].rearrange("s r d -> s (r d)"), ident)
                    last.then_inc(ck_t, 1)
                if l == L_AQ + 3:
                    pe.wait_ge(rope_out, NKC)
                    pe.wait_ge(ck_ev, 1)
                    for n in range(NKC):
                        last = tp(psum[:, 7, n * P:(n + 1) * P], ak[:, n, 0:P], ident)
                    last.then_inc(ck_t, 1)
                if l > L_AK:
                    qk_stats(l - 1 - L_AK)
            qk_stats(QK - 1)

            def scores(k):
                c, m, s = k // AH, k % AH // 2, k % 2
                half = slice(s * HD, (s + 1) * HD)
                if k >= 2:
                    pe.wait_ge(aexp, k - 1)
                else:
                    pe.wait_ge(ck_ev, 2)
                    pe.wait_ge(ak_sw, 32)
                    pe.wait_ge(rope_out, QK)
                q = aq[half, m, c * P:(c + 1) * P]
                g = m // 2
                key = g // 2 + (0 if g % 2 == s else NKC)
                if c == 0:
                    last = mm(psum[:, 4 * s, 0:P], q, ak[half, key, 0:TP], start=True, stop=True)
                else:
                    mm(psum[:, 4 * s, :], q, ak[half, key, TP:N], start=True, stop=True)
                    last = mm(psum[:, 4 * s + 1, 0:PAST], q, akc[half, m // 2, :], start=True, stop=True)
                last.then_inc(sc, 1)

            def turn_p(k):
                c, s = k // AH, k % 2
                pe.wait_ge(p_nrm, k + 1)
                if k >= 2:
                    pe.wait_ge(ha_ev, k - 1)
                for b in range(1 if c == 0 else NT):
                    bank, o = (4 * s + 2, b) if b < BANK_A else (4 * s + 3, b - BANK_A)
                    last = tp(psum[:, bank, o * P:(o + 1) * P], sa[s][:, b * P:(b + 1) * P], ident)
                last.then_inc(atr, 1)

            def values(k):
                c, m, s = k // AH, k % AH // 2, k % 2
                pe.wait_ge(pta, k + 1)
                if c > 0:
                    pe.wait_ge(ptb, k + 1 - AH)
                tiles = [0] if c == 0 else list(range(1, NT + 1))
                for b, v in enumerate(tiles):
                    last = mm(psum[s * HD:(s + 1) * HD, 4 * s + 3, 3 * P:4 * P],
                              av[:, v, (m // 2) * HD:(m // 2 + 1) * HD], sb[s][:, b * P:(b + 1) * P],
                              start=(b == 0), stop=(b == len(tiles) - 1))
                last.then_inc(pv, 1)

            scores(0)
            scores(1)
            for k in range(HEADS):
                if k + 2 < HEADS:
                    scores(k + 2)
                if k >= 1:
                    values(k - 1)
                turn_p(k)
            pe.wait_ge(ha_ev, HEADS - 1)
            gemm(L_MO)
            values(HEADS - 1)
            for l in range(L_MO + 1, L_BM):
                gemm(l)
            for m in range(KC):
                gemm(L_BM + 2 * m)
                gemm(L_BM + 2 * m + 1, m_hi, m_lo, mg_lo if m == 0 else None)
            for m in range(KC):
                gemm(L_BA + 2 * m)
                gemm(L_BA + 2 * m + 1, m_hi, m_lo, hal if m == 0 else None)
            for m in range(KC):
                gemm(L_OUT + m, h_hi, h_lo, yl if m == 0 else None)
            stats_y(2)
            stats(1)
            ffn(1, T_FFN1)
            stats_y(3)
            for k in range(KC):
                pe.wait_ge(x_upd, 2 * KC + k + 1)
                for c in range(NT - 1):
                    last = tp(flat(c)[:, k * P:(k + 1) * P], x[:, k, c * P:(c + 1) * P], ident)
            last.then_inc(ot, 1)
            pe.wait_ge(oe[0], 1)
            for k in range(KC):
                last = tp(flat(0)[:, k * P:(k + 1) * P], x[:, k, (NT - 1) * P:N], ident)
            last.then_inc(ot, 1)

        @block.scalar
        def _(act):
            fn, copy = act.activation, act.copy

            def split(t):
                act.wait_ge(raw_in[t.raw], 16 * (t.quad + 1))
                act.wait_ge(tile_done, t.n + 1)
                copy(whi[t.slot][:, :, :], raw[t.raw][:, :, :]).then_inc(w_hi, 1)

            def done(t):
                act.wait_ge(tile_done, t.n + 3)

            def inv_root(n):
                fn(halves(rb[:, :]), both(2), ACT.Ln, bias=epsc[:, 0:1]).then_inc(rb_ln, 1)
                act.wait_ge(rb_ln, n + 1)
                fn(rb[:, :], rb[:, :], ACT.Exp, scale=-0.5).then_inc(rb_ready, 1)

            def stats(n, ready):
                for k in range(KC):
                    ready(k)
                    if k >= 2:
                        act.wait_ge(stat_mm, 8 * n + k - 1)
                    fn(sq[k % 2][:, :], x[:, k, :], ACT.Square).then_inc(sq_in, 1)
                act.wait_ge(stat_mm, 8 * n + KC)
                inv_root(2 * (n + 1))

            def reuse(l, m):
                if m >= 2:
                    act.wait_ge(sq_sum, (KC - 2) * l + max(m - 2, 1))

            def square_y(l, m, t):
                act.wait_ge(ev[t.slot], t.pair + 1)
                reuse(l + 1, m)
                if m < 2:
                    act.wait_ge(stat_mm if l else ystat_mm, KC * l if l else 1)
                fn(sq[m % 2][:, :], y[:, m, :], ACT.Square).then_inc(ysq_in, 1)
                act.wait_ge(ysq_in, KC * (l + 1) + m + 1)
                for g, cols in GROUPS:
                    last = fn(y[:, m, cols], y[:, m, cols], ACT.Copy, scale=post_s[:, l, m, g:g + 1])
                last.then_inc(y_in, 1)

            def root_y(l):
                act.wait_ge(ystat_mm, l + 2)
                inv_root(2 * l + 1)

            def normed(l):
                for k in range(KC):
                    act.wait_ge(pre_t, 8 * l + k + 1)
                    if k >= 2:
                        act.wait_ge(h_rdy, 8 * l + k - 1)
                    for g, cols in GROUPS:
                        last = fn(sb[k % 2][:, cols], sa[k % 2][:, cols], ACT.Identity,
                                  bias=mod[:, 3 * l * KC + k, g:g + 1], scale=pre_s[:, l, k, g:g + 1])
                    last.then_inc(pre_h, 1)
                    if k % 2 == 0:
                        act.wait_ge(pre_h, 8 * l + k + 1)
                        copy(h_hi[:, k, :], sb[k % 2][:, :]).then_inc(pre_hi[0], 1)

            act.wait_ge(v_ready, 1)
            fn(silc[:, :, :], vT[:, V_CC:V_QG].rearrange("p (g k) -> p g k", g=2), ACT.Silu).then_inc(silc_ready, 1)
            for k in range(0, KC, 2):
                act.wait_ge(x_t, k + 1)
                copy(x[:, k, :], flat(0)[:, 0:N]).then_inc(x_ev[0], 1)
            act.wait_ge(eps_in, 2)
            act.preload_act_table_set(LN_EXP)
            for k in range(KC):
                act.wait_ge(x_ev[k % 2], k // 2 + 1)
                reuse(0, k)
                fn(sq[k % 2][:, :], x[:, k, :], ACT.Square).then_inc(ysq_in, 1)
            act.wait_ge(ystat_mm, 1)
            inv_root(0)
            split(Tile(0))
            split(Tile(1))
            act.wait_ge(mod_ready, 1)
            normed(0)

            def ffn(f, base):
                j0 = 0
                for p, nj in enumerate(PHASES):
                    with act.Fori(0, nj // 2) as i:
                        for u in range(4):
                            t = Tile(base + u, i)
                            s = t.c // 2 % 2
                            if u % 2 == 0:
                                done(t)
                                fn(halves(sa[s][:, :]), both(t.slot), ACT.Silu).then_inc(ev[t.slot], 1)
                                split(t.plus(2))
                            else:
                                split(t.plus(2))
                                act.wait_ge(ev[t.slot], t.pair + 1)
                                out = g_hi[:, bass.ds(2 * i + u // 2, 1), :].rearrange("p o n -> p (o n)")
                                copy(out, sb[s][:, :]).then_inc(g_hi_s, 1)
                    base += 2 * nj
                    tail = f == 1 and p == len(PHASES) - 1

                    def outs(t, m):
                        done(t)
                        if p == 0:
                            dst = y[:, bass.ds(m, 1), :].rearrange("p o (h n) -> p (o h) n", h=2)
                            copy(dst, both(t.slot)).then_inc(ev[t.slot], 1)
                    if p == len(PHASES) - 1:
                        act.preload_act_table_set(LN_EXP)
                        act.wait_ge(post_ready, 2 * f + 1)
                        for u in range(KC):
                            if u == KC - 1:
                                square_y(2 * f, u, Tile(base + u))
                            if not (tail and u >= KC - 2):
                                split(Tile(base + u + 2))
                            if u < KC - 1:
                                square_y(2 * f, u, Tile(base + u))
                    else:
                        with act.Fori(0, 2) as i:
                            for u in range(4):
                                t = Tile(base + u, i)
                                outs(t, 4 * i + u)
                                split(t.plus(2))
                    base += KC
                    j0 += nj

            ffn(0, 0)
            root_y(0)
            stats(0, lambda k: act.wait_ge(x_upd, k + 1))
            act.wait_ge(mod_ready, 2)
            normed(1)

            for l in range(L_AV):
                t = Tile(T_MIX + l)
                done(t)
                if l == L_GATE:
                    split(t.plus(2))
                    act.wait_ge(ld_row, 48)
                    for q, dst in enumerate((gi, gf, gi, gf)):
                        last = fn(halves(dst[:, q // 2, :]), psum[32 * q:32 * q + H, 2 * t.slot:2 * t.slot + 2, 0:HALF],
                                  ACT.Identity, bias=gbias[:, q:q + 1])
                elif l < L_MK:
                    last = fn(halves(mq[:, l - L_MQ, :]), both(t.slot), ACT.Copy, scale=DK ** -0.5)
                elif l < L_MV:
                    last = copy(halves(mk[:, l - L_MK, :]), both(t.slot))
                else:
                    jb = 4 + l - L_MV
                    if jb >= 6:
                        act.wait_ge(tr_done, jb - 1)
                    last = copy(halves(sa[jb % 2][:, :]), both(t.slot))
                last.then_inc(ev[t.slot], 1)
                if l > L_GATE:
                    split(t.plus(2))
                else:
                    act.wait_ge(row_d, 1)
                    fn(t1[:, :, :], t1[:, :, :], ACT.Exp, scale=-1.0).then_inc(row_a, 1)
                    act.wait_ge(row_a, 1)
                    fn(t1[:, :, :], t1[:, :, :], ACT.Ln, bias=epsc[0:H, 1:2]).then_inc(row_a, 1)
                if l == L_MK - 1:
                    act.wait_ge(row_d, ROW_END)
                    fn(ar[:, :, :], ar[:, :, :], ACT.Exp).then_inc(row_a, 1)
                    fn(t1[:, :, :], t1[:, :, :], ACT.Exp).then_inc(row_a, 1)
                    fn(gf[:, :, :], gf[:, :, :], ACT.Exp).then_inc(row_a, 1)
                    fn(gm[:, :, :], gm[:, :, :], ACT.Exp, scale=-1.0).then_inc(row_a, 1)

            def squares(n):
                act.wait_ge(hm_in, n + 1)
                for hh in range(2):
                    o = (2 * (n % 2) + hh) * P
                    last = fn(sq[1][:, o:o + P], hmt[:, n % 2, hh, :], ACT.Square, accum_out=ss[:, n % 2, hh:hh + 1])
                last.then_inc(ss_in, 1)
                act.wait_ge(ss_in, 3 * n + 1)
                fn(ss[:, n % 2, :], ss[:, n % 2, :], ACT.Ln, bias=epsc[:, 0:1], scale=1.0 / DV).then_inc(ss_in, 1)
                act.wait_ge(ss_in, 3 * n + 2)
                fn(ss[:, n % 2, :], ss[:, n % 2, :], ACT.Exp, scale=-0.5).then_inc(ss_in, 1)

            def store_hm(n):
                c, j = n // 4, n % 4
                act.wait_ge(hm_t, n + 1)
                for hh in range(2):
                    g = 2 * j + hh
                    last = fn(hm[:, g, c * P:(c + 1) * P], psum[:, 7, hh * P:(hh + 1) * P], ACT.Copy,
                              scale=vT[:, V_MN + g:V_MN + g + 1])
                last.then_inc(hm_ev, 1)

            for n in range(UNITS):
                act.wait_ge(e_min, n + 1)
                fn(sa[n % 2][:, 0:4 * P], sa[n % 2][:, 0:4 * P], ACT.Exp).then_inc(e_exp, 1)
                if n >= 3:
                    store_hm(n - 3)
                if n >= 1:
                    squares(n - 1)
            squares(UNITS - 1)
            for n in range(UNITS - 3, UNITS):
                store_hm(n)

            def inv_rms(e):
                act.wait_ge(qk_st, e + 1)
                if e >= 1:
                    act.wait_ge(rope_out, e)
                fn(halves(rb[:, :]), both(2), ACT.Ln, bias=epsc[:, 0:1]).then_inc(qk_rb, 1)
                act.wait_ge(qk_rb, e + 1)
                fn(rb[:, :], rb[:, :], ACT.Exp, scale=-0.5).then_inc(qk_rs, 1)

            for l in range(L_AV, L_MO):
                t = Tile(T_MIX + l)
                done(t)
                if l < L_AK:
                    last = copy(halves(sa[(l - L_AV) % 2][:, :]), both(t.slot))
                else:
                    n = l - L_AK
                    gain = V_KG if n < NKC else V_QG
                    fn(halves(qk(n)), both(t.slot), ACT.Copy, scale=vT[:, gain:gain + 1])
                    if n >= 2:
                        act.wait_ge(qk_st, n - 1)
                    last = fn(halves(sq[n % 2][:, :]), both(t.slot), ACT.Square)
                last.then_inc(ev[t.slot], 1)
                split(t.plus(2))
                if l > L_AK:
                    inv_rms(l - 1 - L_AK)
            inv_rms(QK - 1)

            def take_p(k):
                c, s = k // AH, k % 2
                act.wait_ge(atr, k + 1)
                if k >= 2:
                    act.wait_ge(pv, k - 1)
                w = P if c == 0 else BANK_A * P
                copy(sb[s][:, 0:w], psum[:, 4 * s + 2, 0:w]).then_inc(pta, 1)

            def store_ha(k):
                c, m, s = k // AH, k % AH // 2, k % 2
                half = slice(s * HD, (s + 1) * HD)
                act.wait_ge(pv, k + 1)
                copy(ha[half, m, c * P:(c + 1) * P], psum[half, 4 * s + 3, 3 * P:4 * P]).then_inc(ha_ev, 1)

            def exponentials(k):
                c, s = k // AH, k % 2
                act.wait_ge(nmx, 2 * k + 2)
                if k >= 2:
                    act.wait_ge(atr, k - 1)
                w = P if c == 0 else N
                fn(sa[s][:, 0:w], flat(2 * s)[:, 0:w], ACT.Exp, bias=amax[:, s:s + 1], scale=HD ** -0.5,
                   accum_out=asum[:, s:s + 1]).then_inc(aexp, 1)

            exponentials(0)
            exponentials(1)
            for k in range(HEADS):
                take_p(k)
                if k + 2 < HEADS:
                    exponentials(k + 2)
                if k >= 1:
                    store_ha(k - 1)
            store_ha(HEADS - 1)

            def high(k, dst, src, ready, count, out):
                act.wait_ge(ready, count)
                copy(dst[:, k, :], src).then_inc(out, 1)

            for l in range(L_MO, L_END):
                t = Tile(T_MIX + l)
                done(t)
                if l < L_BM:
                    m = l - L_MO
                    if m >= 2:
                        act.wait_ge(mg, m - 1)
                    fn(halves(sa[m % 2][:, :]), both(t.slot), ACT.Sigmoid).then_inc(ev[t.slot], 1)
                elif l < L_OUT:
                    m, gate = (l - L_BM) % 16 // 2, (l - L_BM) % 2 == 0
                    if gate:
                        if m >= 2:
                            v = t.plus(-3)
                            act.wait_ge(ev[v.slot], v.pair + 1)
                        fn(halves(sa[m % 2][:, :]), both(t.slot), ACT.Sigmoid).then_inc(ev[t.slot], 1)
                else:
                    m = l - L_OUT
                    act.wait_ge(yl, m + 1)
                    copy(halves(y[:, m, :]), both(t.slot)).then_inc(ev[t.slot], 1)
                if l == L_END - 1:
                    square_y(1, m, t)
                split(t.plus(2))
                if L_OUT <= l < L_END - 1:
                    act.wait_ge(post_ready, 2)
                    square_y(1, m, t)
                if L_MO < l <= L_BM:
                    m = l - 1 - L_MO
                    high(m, m_hi, sb[m % 2][:, :], mg, m + 1, mg_hi)
                if l == L_BA - 1:
                    for k in range(KC):
                        high(k, m_hi, ha[:, k, :], ha_ev, HEADS, hah)
                if l == L_OUT - 2:
                    act.preload_act_table_set(LN_EXP)
                    for k in range(KC - 1):
                        high(k, h_hi, y[:, k, :], y_sum, k + 1, yh)
                if l == L_OUT - 1:
                    high(KC - 1, h_hi, y[:, KC - 1, :], y_sum, KC, yh)

            root_y(1)
            stats(1, lambda k: act.wait_ge(x_upd, KC + k + 1))
            normed(2)
            ffn(1, T_FFN1)
            root_y(2)
            for c in range(0, NT, 2):
                act.wait_ge(ot, c // (NT - 1) + 1)
                copy(otok[c][:, :], flat(c % (NT - 1))).then_inc(oe[0], 1)

        @block.vector
        def _(dve):
            tt, ts, stt, copy = dve.tensor_tensor, dve.tensor_scalar, dve.scalar_tensor_tensor, dve.tensor_copy
            steps = [0]

            def step(ins):
                steps[0] += 1
                ins.then_inc(dv, 1)
                dve.wait_ge(dv, steps[0])

            def split(t):
                dve.wait_ge(w_hi, t.n + 1)
                tt(wlo[t.slot][:, :, :], raw[t.raw][:, :, :], whi[t.slot][:, :, :].bitcast(F32),
                   ALU.subtract).then_inc(raw_free, 1)

            def done(t):
                dve.wait_ge(tile_done, t.n + 3)

            def root_ready(n):
                dve.wait_ge(rb_ready, n + 1)

            def normed(l):
                def low(k):
                    if k % 2:
                        dve.wait_ge(pre_h, 8 * l + k + 1)
                        copy(h_hi[:, k, :], sb[k % 2][:, :]).then_inc(pre_hi[1], 1)
                    dve.wait_ge(pre_hi[k % 2], 4 * l + k // 2 + 1)
                    tt(h_lo[:, k, :], sb[k % 2][:, :], h_hi[:, k, :].bitcast(F32), ALU.subtract).then_inc(h_rdy, 1)
                for k in range(KC):
                    if k >= 2:
                        dve.wait_ge(pre_h, 8 * l + k - 1)
                    tt(sa[k % 2][:, :], x[:, k, :], rb[:, :], ALU.mult).then_inc(pre_t, 1)
                    if k >= 1:
                        low(k - 1)
                low(KC - 1)

            def add_square(l, m):
                dve.wait_ge(ysq_in, KC * l + m + 1)
                if m == 1:
                    tt(rb[:, :], sq[0][:, :], sq[1][:, :], ALU.add).then_inc(sq_sum, 1)
                elif m >= 2:
                    dve.wait_ge(sq_sum, (KC - 2) * l + m - 1)
                    tt(rb[:, :], rb[:, :], sq[m % 2][:, :], ALU.add).then_inc(sq_sum, 1)

            def residual(l):
                def add(k):
                    dve.wait_ge(post_t, 8 * l + k + 1)
                    tt(x[:, k, :], x[:, k, :], sa[k % 2][:, :], ALU.add).then_inc(x_upd, 1)
                for k in range(KC):
                    if k >= 2:
                        dve.wait_ge(x_upd, 8 * l + k - 1)
                    dve.wait_ge(y_in, KC * l + k + 1)
                    tt(sa[k % 2][:, :], y[:, k, :], rb[:, :], ALU.mult).then_inc(post_t, 1)
                    if k >= 1:
                        add(k - 1)
                add(KC - 1)

            def per_group(col):
                return vT[:, col:col + KC].rearrange("p (k o) -> p k o", o=1).broadcast_to([P, KC, 2])

            def scales(l, which):
                if which == "pre":
                    step(stt(pre_s[:, l, :, :], mod[:, (3 * l + 1) * KC:(3 * l + 2) * KC, :], 1.0,
                             per_group(V_PRE + l * KC), ALU.add, ALU.mult))
                else:
                    stt(post_s[:, l, :, :], mod[:, (3 * l + 2) * KC:(3 * l + 3) * KC, :], 0.5 if l != 1 else 1.0,
                        per_group(V_POST + l * KC), ALU.mult, ALU.mult).then_inc(post_ready, 1)

            def over_k(w, ks, done_mul, before):
                for k in ks:
                    for g in range(2):
                        acc, by = macc[:, g, :], silc[:, g, k:k + 1]
                        if k == 0:
                            last = ts(acc, w[:, k, :], by, None, ALU.mult)
                        else:
                            dve.wait_ge(done_mul, before + 2 * k + g - 1)
                            last = stt(acc, w[:, k, :], by, acc, ALU.mult, ALU.add)
                        last.then_inc(done_mul, 1)

            def multiply(n, part):
                dve.wait_ge(mod_in[part], 16 * (n + 1))
                over_k(mw, range(*MOD_K[part]), mod_mul, 2 * KC * n)

            def take_mod(n):
                dve.wait_ge(mod_done, n + 2)
                take_sums(MOD_T * (MOD_FIRST + n), 7)

            def take_sums(lo, bank):
                bias = vT[:, bass.ds(lo, MOD_T)].rearrange("p (t o) -> p t o", o=1).broadcast_to([P, MOD_T, 2])
                stt(mod[:, bass.ds(lo, MOD_T), :], mod_out(0, bank)[:, 0:2 * MOD_T].rearrange("p (t g) -> p t g", g=2),
                    float(D), bias, ALU.mult, ALU.add).then_inc(mod_ev, 1)

            dve.sem_inc(raw_free, RAWS)
            dve.memset(epsc[:, 0:1], EPS).then_inc(eps_in, 1)
            dve.memset(epsc[:, 1:2], 1.0).then_inc(eps_in, 1)
            dve.wait_ge(vec_t, 1)
            copy(vT[:, :], psum[:, 6, 0:V_N]).then_inc(v_ready, 1)
            for k in range(1, KC, 2):
                dve.wait_ge(x_t, k + 1)
                copy(x[:, k, :], flat(1)[:, 0:N]).then_inc(x_ev[1], 1)
            dve.wait_ge(v_ready, 1)
            for m in range(KC - 1):
                add_square(0, m)
            dve.wait_ge(silc_ready, 1)
            dve.wait_ge(mod0_in[MOD_DVE], 16)
            over_k(mw0[MOD_DVE], range(KC), mod0_mul, 0)
            split(Tile(0))
            split(Tile(1))
            dve.wait_ge(mod_done, 1)
            first = 2 * KC
            tt(mod[:, 0:first, :], mod_out(0)[:, 0:2 * first].rearrange("p (t g) -> p t g", g=2),
               vT[:, 0:first].rearrange("p (t o) -> p t o", o=1).broadcast_to([P, first, 2]), ALU.add).then_inc(mod0_ev, 1)
            dve.wait_ge(mod0_ev, 1)
            take_sums(MOD_DVE * MOD_T, 6)
            dve.wait_ge(mod_ev, 1)
            stt(pre_s[:, 0, :, :], mod[:, KC:2 * KC, :], 1.0, per_group(V_PRE), ALU.add, ALU.mult).then_inc(mod_ready, 1)
            root_ready(0)
            dve.wait_ge(x_ev[0], 4)
            dve.wait_ge(x_ev[1], 4)
            normed(0)

            def ffn(f, base):
                it = j0 = 0
                for p, nj in enumerate(PHASES):
                    with dve.Fori(0, nj // 2) as i:
                        for u in range(4):
                            t = Tile(base + u, i)
                            s = t.c // 2 % 2 if u % 2 == 0 else t.plus(-1).c // 2 % 2
                            split(t.plus(2))
                            if u % 2:
                                g = t.plus(-1)
                                done(t)
                                dve.wait_ge(ev[g.slot], g.pair + 1)
                                tt(halves(sb[s][:, :]), halves(sa[s][:, :]), both(t.slot), ALU.mult).then_inc(ev[t.slot], 1)
                            if f == 0 and p < 2 and u < 3:
                                multiply(it + i, u)
                            if u % 2:
                                dve.wait_ge(g_hi_s, NJ * f + j0 + 2 * i + u // 2 + 1)
                                jj = bass.ds(2 * i + u // 2, 1)
                                tt(g_lo[:, jj, :].rearrange("p o n -> p (o n)"), sb[s][:, :],
                                   g_hi[:, jj, :].rearrange("p o n -> p (o n)").bitcast(F32),
                                   ALU.subtract).then_inc(g_lo_s, 1)
                        if f == 0 and p < 2:
                            take_mod(it + i)
                    if p < 2:
                        it += nj // 2
                    base += 2 * nj
                    if p > 0:
                        for q in (base - 2 * nj - 1, base - 2 * nj - 2):
                            dve.wait_ge(ev[q % 2], q // 2 + 1)

                    def outs(t, m):
                        if p > 0:
                            done(t)
                            yv = y[:, bass.ds(m, 1), :].rearrange("p o (h n) -> p (o h) n", h=2)
                            tt(yv, yv, both(t.slot), ALU.add).then_inc(ev[t.slot], 1)
                    if p == len(PHASES) - 1:
                        if f == 0:
                            dve.wait_ge(mod_ev, 3)
                            scales(0, "post")
                        for u in range(KC):
                            if (f == 0 or u < KC - 2) and u < KC - 1:
                                split(Tile(base + u + 2))
                            if u == KC - 1:
                                add_square(2 * f + 1, u - 1)
                            outs(Tile(base + u), u)
                            if 1 <= u < KC - 1:
                                add_square(2 * f + 1, u - 1)
                            if f == 0 and u == KC - 1:
                                split(Tile(base + u + 2))
                            if f == 0:
                                if u % 4 < 3:
                                    multiply(it + u // 4, u % 4)
                                else:
                                    take_mod(it + u // 4)
                    else:
                        with dve.Fori(0, 2) as i:
                            for u in range(4):
                                t = Tile(base + u, i)
                                split(t.plus(2))
                                outs(t, 4 * i + u)
                                if f == 0 and u < 3:
                                    multiply(it + i, u)
                            if f == 0:
                                take_mod(it + i)
                    it += 2
                    base += KC
                    j0 += nj

            ffn(0, 0)
            dve.wait_ge(mod_ev, MOD_LATER + 1)
            scales(1, "post")
            scales(2, "post")
            scales(1, "pre")
            stt(pre_s[:, 2, :, :], mod[:, 7 * KC:8 * KC, :], 1.0, per_group(V_PRE + 2 * KC),
                ALU.add, ALU.mult).then_inc(mod_ready, 1)
            root_ready(1)
            residual(0)
            root_ready(2)
            dve.wait_ge(x_upd, KC)
            normed(1)

            def take_turned(jb):
                dve.wait_ge(tr_done, jb + 1)
                if jb < 4:
                    dst = mkt[:, :, jb * P:(jb + 1) * P]
                elif jb < 12:
                    dst = vt[:, :, jb - 4, 0:DV]
                else:
                    dst = av[:, 0:NT, (jb - 12) * P:(jb - 11) * P]
                copy(dst, flat(2 + jb % 2)[:, 0:N].rearrange("p (c t) -> p c t", c=NT)).then_inc(tr_ev, 1)

            rows = [0]

            def row_step(ins, wait=True):
                rows[0] += 1
                ins.then_inc(row_d, 1)
                if wait:
                    dve.wait_ge(row_d, rows[0])

            def forget():
                t = Tile(T_MIX)
                dve.wait_ge(ev[t.slot], t.pair + 1)
                row_step(stt(t1[:, :, :], gf[:, :, :], -1.0, gf[:, :, :], ALU.mult, ALU.max))

            def scans():
                dve.wait_ge(row_a, 2)
                row_step(stt(gf[:, :, :], gf[:, :, :], 0.0, t1[:, :, :], ALU.min, ALU.subtract))
                for c in range(NT):
                    for d in range(2):
                        seg = slice(c * P, (c + 1) * P) if d == 0 else slice((c + 1) * P - 1, c * P - 1 if c else None, -1)
                        row_step(dve.tensor_tensor_scan(gb[:, d, seg], one_row, gf[:, d, seg], 0.0, ALU.mult, ALU.add), False)
                for d in range(2):
                    for g, cols in GROUPS:
                        if d:
                            cols = slice(cols.stop - 1, cols.start - 1 if cols.start else None, -1)
                        row_step(dve.tensor_tensor_scan(gm[:, d, cols], gf[:, d, cols], gi[:, d, cols],
                                                        m0[:, d:d + 1] if g else 0.0, ALU.add, ALU.max), False)
                dve.wait_ge(row_d, rows[0])
                row_step(dve.memset(m_in[:, :, 0:1], 0.0), False)
                row_step(copy(m_in[:, 0, 1:2], m0[:, 0:1]), False)
                row_step(copy(m_in[:, 1, NT - 1:NT], m0[:, 1:2]), False)
                row_step(copy(m_in[:, 0, 2:NT], gm[:, 0, 2 * P - 1:(NT - 1) * P:P]), False)
                row_step(copy(m_in[:, 1, 1:NT - 1], gm[:, 1, 2 * P:(NT - 1) * P + 1:P]), False)
                row_step(copy(mout[:, 0:1], gm[:, 0, TP - 1:TP]), False)
                row_step(copy(mout[:, 1:2], gm[:, 1, 0:1]), False)
                assert rows[0] == ROW_M
                row_step(tt(gi[:, :, :], gi[:, :, :], gb[:, :, :], ALU.subtract), False)
                row_step(tt(nm[:, :, :], gb[:, :, :], gm[:, :, :], ALU.subtract))
                row_step(copy(nml[:, 0, :], nm[:, 0, P - 1:N:P]), False)
                row_step(copy(nml[:, 1, :], nm[:, 1, 0:N:P]))

                def tiles(v):
                    return v[:, :, :].rearrange("h d (c t) -> h (d c) t", t=P)

                def spread(v):
                    return v[:, :, :].rearrange("h d (c o) -> h (d c) o", o=1).broadcast_to([H, 2 * NT, P])

                row_step(tt(ar[:, :, :], m_in[:, :, :], nml[:, :, :], ALU.add), False)
                row_step(tt(tiles(t1), tiles(nm), spread(m_in), ALU.add), False)
                row_step(tt(tiles(gf), tiles(gi), spread(nml), ALU.add), False)
                assert rows[0] == ROW_END

            def take_gates():
                dve.wait_ge(tok_t, 2)
                copy(tk[:, :, :, :, :].rearrange("p q c d h -> p (q c d h)"), psum[:, 4, 0:3 * NT * 2 * H]).then_inc(tok_ev, 1)
                copy(ab[:, :, :].rearrange("p j c -> p (j c)"), psum[:, 5, 0:8 * NT]).then_inc(tok_ev, 1)
                dve.wait_ge(tok_ev, 2)

            dve.wait_ge(x_spill, 16)
            for l in range(L_AV):
                split(Tile(T_MIX + l + 2))
                if l == 0:
                    dve.wait_ge(tile_done, 2 + T_MIX)
                    dve.memset(vt[:, :, :, DV:DV + 1], 1.0).then_inc(ones_v, 1)
                    forget()
                if l == 1:
                    scans()
                if l == L_MK:
                    take_gates()
                if l > L_MK:
                    take_turned(l - L_MK - 1)
            take_turned(11)

            dve.wait_ge(st_in, 64)
            for s in range(len(STATES) + 1):
                if s < len(STATES):
                    d, c = STATES[s]
                    if s >= 2:
                        dve.wait_ge(kv_done, s - 1)
                    w = tk[:, 1, c, d, :].rearrange("p (h o) -> p h o", o=1).broadcast_to([P, H, DK])
                    tt(sa[s % 2][:, 0:H * DK].rearrange("p (h k) -> p h k", h=H),
                       mkt[:, c, :].rearrange("p (h k) -> p h k", h=H), w, ALU.mult).then_inc(kw_in, 1)
                if s >= 1:
                    d, c = STATES[s - 1]
                    s1 = (s - 1) % 2
                    dve.wait_ge(kv_done, s)
                    if c == 0:
                        for b in range(2):
                            last = copy(cp[:, d, 2 * b:2 * b + 2, :].rearrange("p j v -> p (j v)"),
                                        psum[:, 2 * s1 + b, 0:2 * (DV + 1)])
                    else:
                        if s >= 3:
                            dve.wait_ge(st_upd, s - 2)
                        for j in range(4):
                            to = c - 1 + (1 if d == 0 else -1)
                            last = stt(cs[:, d, to, j, :], cs[:, d, c - 1, j, :], ab[:, j, d * NT + c:d * NT + c + 1],
                                       psum[:, 2 * s1 + j // 2, (j % 2) * (DV + 1):(j % 2 + 1) * (DV + 1)],
                                       ALU.mult, ALU.add)
                    last.then_inc(st_upd, 1)

            def decays(n):
                c, j = n // 4, n % 4
                dve.wait_ge(m_spread, n + 1)
                if n >= 2:
                    dve.wait_ge(nums, n - 1)
                e = sa[n % 2][:, 0:4 * P].rearrange("p (d g t) -> p d g t", d=2, g=2)
                for d in range(2):
                    for hh in range(2):
                        o = (2 * d + hh) * P
                        last = stt(e[:, d, hh, :], psum[:, 4, o:o + P], tk[:, 0, c, d, 2 * j + hh:2 * j + hh + 1],
                                   mask[d], ALU.add, ALU.min)
                last.then_inc(e_min, 1)
                dve.wait_ge(front, n + 1)
                if c > 0:
                    q = mq[:, j, c * P:(c + 1) * P].rearrange("p (o t) -> p o t", o=1).broadcast_to([P, 2, P])
                    tt(qw[:, n % 2, :, :], q, psum[:, 5, P:3 * P].rearrange("p (d t) -> p d t", d=2), ALU.mult)
                if n >= 2:
                    scale_hm(n - 2)
                dve.wait_ge(e_exp, n + 1)
                for hh in range(2):
                    s = psum[:, 5 + hh, 0:P].rearrange("p (o t) -> p o t", o=1).broadcast_to([P, 2, P])
                    last = tt(e[:, :, hh, :], e[:, :, hh, :], s, ALU.mult)
                last.then_inc(s_in, 1)

            def outputs(n):
                c, j, s = n // 4, n % 4, n % 2
                dve.wait_ge(nums, n + 1)
                v = psum[:, 2 * s:2 * s + 2, 0:2 * (DV + 1)].rearrange("p g (d v) -> p g d v", d=2)
                dv_, num = v[:, :, :, DV:DV + 1].rearrange("p g d o -> p g (d o)"), v[:, :, :, 0:DV]
                floor = tk[:, 2, c, :, 2 * j:2 * j + 2].rearrange("p d g -> p g d")
                stt(den[:, :, :], dv_, -1.0, floor, ALU.mult, ALU.max).then_inc(den_s, 1)
                dve.wait_ge(den_s, 4 * n + 1)
                tt(den[:, :, :], den[:, :, :], dv_, ALU.max).then_inc(den_s, 1)
                dve.wait_ge(den_s, 4 * n + 2)
                dve.reciprocal(den[:, :, :], den[:, :, :]).then_inc(den_s, 1)
                dve.wait_ge(den_s, 4 * n + 3)
                tmp = sb[0][:, 0:4 * P].rearrange("p (g d v) -> p g d v", g=2, d=2)
                for hh in range(2):
                    r = den[:, hh, :].rearrange("p (d o) -> p d o", o=1).broadcast_to([P, 2, DV])
                    last = tt(tmp[:, hh, :, :], num[:, hh, :, :], r, ALU.mult)
                last.then_inc(den_s, 1)
                dve.wait_ge(den_s, 4 * n + 4)
                if n >= 2:
                    dve.wait_ge(hm_t, n - 1)
                tt(hmt[:, s, :, :], tmp[:, :, 0, :], tmp[:, :, 1, :], ALU.add).then_inc(hm_in, 1)

            def scale_hm(n):
                dve.wait_ge(ss_in, 3 * n + 3)
                r = ss[:, n % 2, :].rearrange("p (g o) -> p g o", o=1).broadcast_to([P, 2, DV])
                tt(hmt[:, n % 2, :, :], hmt[:, n % 2, :, :], r, ALU.mult).then_inc(hm_sc, 1)

            dve.wait_ge(kv_done, len(STATES))
            dve.wait_ge(st_upd, len(STATES))
            for n in range(UNITS):
                decays(n)
                if n >= 1:
                    outputs(n - 1)
            outputs(UNITS - 1)
            scale_hm(UNITS - 2)
            scale_hm(UNITS - 1)

            def turn_halves(e):
                dst = qk(e)
                lat = dst[:, TP:N]
                dve.wait_ge(qk_st, e + 1)
                tt(sb[0][:, 0:TS], psum[:, 6, :], sin, ALU.mult).then_inc(rope, 1)
                tt(lat, lat, cos, ALU.mult).then_inc(rope_c, 1)
                dve.wait_ge(rope_c, 2 * e + 1)
                tt(lat, lat, sb[0][:, 0:TS], ALU.add).then_inc(rope_c, 1)
                dve.wait_ge(rope_c, 2 * e + 2)
                dve.wait_ge(qk_rs, e + 1)
                tt(dst, dst, rb[:, :], ALU.mult).then_inc(rope_out, 1)

            for l in range(L_AV, L_MO):
                split(Tile(T_MIX + l + 2))
                if l in (L_AV + 1, L_AV + 2):
                    take_turned(12 + l - 1 - L_AV)
                if l == L_AK + 1:
                    dve.wait_ge(ck_t, 1)
                    copy(akc[:, :, :].rearrange("p g s -> p (g s)"), psum[:, 7, :]).then_inc(ck_ev, 1)
                if l == L_AQ + 3:
                    dve.wait_ge(ck_t, 2)
                    copy(ko[:, :], psum[:, 7, 0:KVH * HD]).then_inc(ck_ev, 1)
                if l > L_AK:
                    turn_halves(l - 1 - L_AK)
            turn_halves(QK - 1)

            def top(k):
                c, s = k // AH, k % 2
                w = P if c == 0 else N
                dve.wait_ge(sc, k + 1)
                dve.reduce_max(amax[:, s:s + 1], flat(2 * s)[:, 0:w], AX.X).then_inc(nmx, 1)
                dve.wait_ge(nmx, 2 * k + 1)
                ts(amax[:, s:s + 1], amax[:, s:s + 1], -HD ** -0.5, None, ALU.mult).then_inc(nmx, 1)

            def divide(k):
                c, s = k // AH, k % 2
                w = P if c == 0 else N
                dve.wait_ge(aexp, k + 1)
                dve.reciprocal(arec[:, s:s + 1], asum[:, s:s + 1]).then_inc(rcp, 1)
                dve.wait_ge(rcp, k + 1)
                ts(sa[s][:, 0:w], sa[s][:, 0:w], arec[:, s:s + 1], None, ALU.mult).then_inc(p_nrm, 1)

            def take_last(k):
                s = k % 2
                dve.wait_ge(atr, k + 1)
                dve.wait_ge(pv, k - 1)
                copy(sb[s][:, BANK_A * P:N], psum[:, 4 * s + 3, 0:N - BANK_A * P]).then_inc(ptb, 1)

            top(0)
            top(1)
            for k in range(HEADS):
                if k - 1 >= AH:
                    take_last(k - 1)
                divide(k)
                if k + 2 < HEADS:
                    top(k + 2)
            take_last(HEADS - 1)

            def low_m(m):
                dve.wait_ge(mg_hi, m + 1)
                tt(m_lo[:, m, :], sb[m % 2][:, :], m_hi[:, m, :].bitcast(F32), ALU.subtract).then_inc(mg_lo, 1)

            for l in range(L_MO, L_END):
                t = Tile(T_MIX + l)
                if l == L_END - 1:
                    add_square(2, KC - 2)
                split(t.plus(2))
                if l < L_BM:
                    m = l - L_MO
                    dve.wait_ge(ev[t.slot], t.pair + 1)
                    if m >= 2:
                        dve.wait_ge(mg_lo, m - 1)
                    tt(sb[m % 2][:, :], hm[:, m, :], sa[m % 2][:, :], ALU.mult).then_inc(mg, 1)
                    if m >= 1:
                        low_m(m - 1)
                elif l < L_OUT:
                    m, gate = (l - L_BM) % 16 // 2, (l - L_BM) % 2 == 0
                    if l == L_BM:
                        low_m(KC - 1)
                    if gate:
                        dve.wait_ge(ev[t.slot], t.pair + 1)
                    elif l < L_BA:
                        done(t)
                        tt(halves(y[:, m, :]), halves(sa[m % 2][:, :]), both(t.slot), ALU.mult).then_inc(ev[t.slot], 1)
                    else:
                        done(t)
                        if m >= 2:
                            dve.wait_ge(y_sum, m - 1)
                        else:
                            dve.wait_ge(mg_lo, KC)
                        tt(halves(sb[m % 2][:, :]), halves(sa[m % 2][:, :]), both(t.slot), ALU.mult).then_inc(ev[t.slot], 1)
                        dve.wait_ge(ev[t.slot], t.pair + 1)
                        tt(y[:, m, :], y[:, m, :], sb[m % 2][:, :], ALU.add).then_inc(y_sum, 1)
                if l == L_BA - 1:
                    for k in range(KC):
                        dve.wait_ge(hah, k + 1)
                        tt(m_lo[:, k, :], ha[:, k, :], m_hi[:, k, :].bitcast(F32), ALU.subtract).then_inc(hal, 1)
                if l in (L_OUT - 2, L_OUT - 1):
                    for k in range(KC - 1) if l == L_OUT - 2 else (KC - 1,):
                        dve.wait_ge(yh, k + 1)
                        tt(h_lo[:, k, :], y[:, k, :], h_hi[:, k, :].bitcast(F32), ALU.subtract).then_inc(yl, 1)
                if L_OUT < l < L_END - 1:
                    add_square(2, l - 1 - L_OUT)

            root_ready(3)
            dve.wait_ge(x_back, 16)
            residual(1)
            root_ready(4)
            dve.wait_ge(x_upd, 2 * KC)
            normed(2)
            ffn(1, T_FFN1)
            root_ready(5)
            residual(2)
            for c in range(1, NT, 2):
                dve.wait_ge(ot, 1)
                copy(otok[c][:, :], flat(c)).then_inc(oe[1], 1)


def constants():
    c = np.zeros((P, C_N), np.float32)
    r = np.arange(P)
    c[:, 0:P] = np.eye(P)
    c[:, P:2 * P] = 1.0 / D
    c[:, 2 * P:3 * P] = (r[:, None] // HD == r[None, :] // HD) / HD
    for p in range(P):
        if p % 32 < 16:
            c[p + 16, 3 * P + p] = -1.0
        else:
            c[p - 16, 3 * P + p] = 1.0
    c[:, 4 * P:5 * P] = np.where(r[:, None] <= r[None, :], 0.0, -1e4)
    c[:, 5 * P:6 * P] = np.where(r[:, None] >= r[None, :], 0.0, -1e4)
    tok = np.arange(TS)
    pos = np.stack([tok // GRID_W, tok % GRID_W]).astype(np.float32)
    freq = np.float32(10000.0) ** (-np.arange(16, dtype=np.float32) / np.float32(16))
    ang = pos[(r % HD) // 32] * freq[r % 16][:, None]
    c[:, 6 * P:6 * P + TS] = np.cos(ang)
    c[:, 6 * P + TS:] = np.sin(ang)
    rc = np.zeros((H, R_N), np.float32)
    for h in range(H):
        rc[h, h * P:(h + 1) * P] = 1.0
        o = H * P + (h // 2) * P + (h % 2) * DK
        rc[h, o:o + DK] = 1.0
    rc[:, H * P + 4 * P:] = 1.0
    return c, rc


def lay_out(i):
    f = lambda n: np.asarray(i[n])

    def tiles(w, order=None):
        k, n = w.shape
        w = w.reshape(k // P, P, n // P, P).transpose(2, 1, 0, 3)
        return w.reshape(n // P, P, k)

    wi = f("ffn_w_in")[0].reshape(2, D, 2, NJ, P).transpose(0, 1, 3, 2, 4).reshape(2, D, 2 * DFF)
    mix = f("w_in_mix")[0]
    sizes = (H * DK, H * DK, H * DV, H * DV, 4 * H, AH * HD, KVH * HD, KVH * HD, 2 * D)
    mq, mk, mv, mo, mg, aq, ak, av, bg = np.split(mix, np.cumsum(sizes)[:-1], axis=1)
    gates = np.tile(mg.reshape(D, 4, 1, H), (1, 1, 4, 1)).reshape(D, P)

    def paired(g, w):
        return np.stack([tiles(g), tiles(w)], 1).reshape(2 * KC, P, D)

    w_mix = np.concatenate([
        tiles(gates), tiles(mq), tiles(mk), tiles(mv), tiles(av), tiles(ak), tiles(aq), tiles(mo),
        paired(bg[:, :D], f("w_branch_m")[0]), paired(bg[:, D:], f("w_branch_a")[0]), tiles(f("w_out")[0])])
    qk = f("qk_norm")[0]
    vecs = np.concatenate([
        f("b_mod")[0].reshape(-1, P), f("norm_pre")[0].reshape(-1, P), f("norm_post")[0].reshape(-1, P),
        f("mlstm_norm")[0].reshape(-1, P), f("c_ctx").reshape(-1, P), f("c")[0].reshape(-1, P),
        np.concatenate([qk, qk], axis=1)])
    cst, rowc = constants()
    return {
        "x_prompt": f("x_prompt"), "x_sample": f("x_sample"),
        "w_mod": f("w_mod")[0].reshape(KC, P, -1, MOD_W).transpose(2, 1, 0, 3).reshape(-1, P, KC * MOD_W),
        "w_ffn_in": np.concatenate([tiles(wi[0]), tiles(wi[1])]),
        "w_ffn_out": np.concatenate([tiles(f("ffn_w_out")[0, n]) for n in range(2)]),
        "w_mix": w_mix, "vec_rows": vecs, "cst": cst, "rowc": rowc,
        "gate_bias": f("mlstm_gate_bias")[0].reshape(4, H).T,
        "m0": f("state_m")[0, 0].T, "state_C": f("state_C"), "state_n": f("state_n"),
        "cache_k": f("cache_k").reshape(PAST, KVH * HD), "cache_v": f("cache_v").reshape(PAST, KVH * HD),
    }


OUTS = (("o_yp", (1, TP, D)), ("o_ys", (1, TS, D)), ("o_k", (PAST, KVH * HD)), ("o_v", (PAST, KVH * HD)),
        ("o_C", (1, 1, 2, H, DK, DV)), ("o_n", (1, 1, 2, H, DK)), ("o_m", (1, 1, 2, H)))


def kernel(**inputs):
    import concourse.bacc as bacc
    from concourse.bass_utils import run_bass_kernel_spmd

    nc = bacc.Bacc("TRN2", target_bir_lowering=False, num_devices=1)
    arrays, a = {}, {}
    for name, v in lay_out(inputs).items():
        v = np.ascontiguousarray(v)
        arrays[f"in_{name}"] = v
        a[name] = nc.dram_tensor(f"in_{name}", v.shape, mybir.dt.from_np(v.dtype), kind="ExternalInput").ap()
    for name, shape in OUTS:
        a[name] = nc.dram_tensor(name, shape, F32, kind="ExternalOutput").ap()
    a["x_keep"] = nc.dram_tensor("x_keep", (P, KC * N), F32, kind="Internal").ap()
    build(nc, a)
    r = run_bass_kernel_spmd(nc, [arrays], core_ids=[0]).results[0]
    out = [np.asarray(r[name]) for name, _ in OUTS]
    out[2] = out[2].reshape(1, 1, TP, KVH, HD)
    out[3] = out[3].reshape(1, 1, TP, KVH, HD)
    return tuple(out)
```
